# Optimizing a Trainium2 kernel written in Bass

```python
import jax, jax.numpy as jnp
from jax import lax
import numpy as np

D_MODEL = 1024
BATCH = 1
SEQ = 256
DEPTH = 1

MEM_LEN = 256
CHUNK = 128
SG_GROUPS = 8
SG_GROUP_DIM = 64
SG_WIDTH = SG_GROUPS * SG_GROUP_DIM
MLA_HEADS = 8
MLA_NOPE = 64
MLA_ROPE = 32
MLA_V = 64
MLA_QK = MLA_NOPE + MLA_ROPE
MLA_Q_RANK = 384
MLA_KV_RANK = 256
MLA_WIDTH = MLA_HEADS * MLA_V
MEM_HEADS = 4
MEM_HEAD_DIM = 128
MEM_WIDTH = MEM_HEADS * MEM_HEAD_DIM
N_BRANCH = 3
D_FF = 2816
ROPE_BASE = 10000.0
EPS = 1e-6
Q_BLOCK = 128
NEG = -1e30

COL_U = 0
COL_V = COL_U + SG_WIDTH
COL_CQ = COL_V + SG_WIDTH
COL_CKV = COL_CQ + MLA_Q_RANK
COL_KR = COL_CKV + MLA_KV_RANK
COL_QM = COL_KR + MLA_ROPE
COL_GATE = COL_QM + MEM_WIDTH
IN_COLS = COL_GATE + N_BRANCH * D_MODEL


def rmsnorm(x, g):
    xf = x.astype(jnp.float32)
    y = xf * lax.rsqrt(jnp.mean(xf * xf, axis=-1, keepdims=True) + EPS)
    return (y * g.astype(jnp.float32)).astype(x.dtype)

def layernorm(x, g, b):
    xf = x.astype(jnp.float32)
    mu = jnp.mean(xf, axis=-1, keepdims=True)
    xc = xf - mu
    y = xc * lax.rsqrt(jnp.mean(xc * xc, axis=-1, keepdims=True) + EPS)
    return (y * g.astype(jnp.float32) + b.astype(jnp.float32)).astype(x.dtype)

def rope(x, positions):
    half = x.shape[-1] // 2
    inv = ROPE_BASE ** (-jnp.arange(half, dtype=jnp.float32) / half)
    ang = positions.astype(jnp.float32)[:, :, None] * inv
    cos = jnp.cos(ang)[:, :, None, :]
    sin = jnp.sin(ang)[:, :, None, :]
    x1 = x[..., :half].astype(jnp.float32)
    x2 = x[..., half:].astype(jnp.float32)
    return jnp.concatenate([x1 * cos - x2 * sin, x2 * cos + x1 * sin], axis=-1).astype(x.dtype)

def swiglu(x, w_gu, w_down):
    g, u = jnp.split(x @ w_gu, 2, axis=-1)
    return (jax.nn.silu(g) * u) @ w_down

def spatial_gating(u, v, ln_g, ln_b, w_s, b_s):
    B, S, _ = v.shape
    nc = S // CHUNK
    v = layernorm(v, ln_g, ln_b).reshape(B, nc, CHUNK, SG_GROUPS, SG_GROUP_DIM)
    causal = jnp.tril(jnp.ones((CHUNK, CHUNK), dtype=bool))
    w = jnp.where(causal[None], w_s, jnp.zeros_like(w_s))
    mixed = jnp.einsum('gts,bcsgd->bctgd', w, v) + b_s.T[None, None, :, :, None]
    return u * mixed.reshape(B, S, SG_WIDTH)

def causal_block_attention(q, k, v):
    B, S, H, Dqk = q.shape
    Dv = v.shape[-1]
    nb = S // Q_BLOCK
    scale = Dqk ** -0.5
    qb = q.reshape(B, nb, Q_BLOCK, H, Dqk).transpose(1, 0, 2, 3, 4)
    kpos = jnp.arange(S)

    def one_block(args):
        i, qi = args
        s = jnp.einsum('bqhd,bkhd->bhqk', qi, k).astype(jnp.float32) * scale
        qpos = i * Q_BLOCK + jnp.arange(Q_BLOCK)
        mask = kpos[None, :] <= qpos[:, None]
        s = jnp.where(mask[None, None], s, NEG)
        p = jax.nn.softmax(s, axis=-1)
        return jnp.einsum('bhqk,bkhd->bqhd', p.astype(v.dtype), v)

    out = lax.map(one_block, (jnp.arange(nb), qb))
    return out.transpose(1, 0, 2, 3, 4).reshape(B, S, H * Dv)

def mla(c_q, c_kv, k_rope, positions, cq_norm, w_uq, ckv_norm, w_ukv, q_norm, k_norm):
    B, S, _ = c_q.shape
    q = (rmsnorm(c_q, cq_norm) @ w_uq).reshape(B, S, MLA_HEADS, MLA_QK)
    q = rmsnorm(q, q_norm)
    q = jnp.concatenate([q[..., :MLA_NOPE], rope(q[..., MLA_NOPE:], positions)], axis=-1)
    kv = (rmsnorm(c_kv, ckv_norm) @ w_ukv).reshape(B, S, MLA_HEADS, MLA_NOPE + MLA_V)
    k_nope, v = kv[..., :MLA_NOPE], kv[..., MLA_NOPE:]
    k_pe = jnp.broadcast_to(k_rope[:, :, None, :], (B, S, MLA_HEADS, MLA_ROPE))
    k = rmsnorm(jnp.concatenate([k_nope, k_pe], axis=-1), k_norm)
    k = jnp.concatenate([k[..., :MLA_NOPE], rope(k[..., MLA_NOPE:], positions)], axis=-1)
    return causal_block_attention(q, k, v)

def memory_attention(q_m, mem, mem_norm, w_kv, q_norm, k_norm):
    B, S, _ = q_m.shape
    q = rmsnorm(q_m.reshape(B, S, MEM_HEADS, MEM_HEAD_DIM), q_norm)
    kv = rmsnorm(mem, mem_norm) @ w_kv
    M = mem.shape[1]
    k = rmsnorm(kv[..., :MEM_WIDTH].reshape(B, M, MEM_HEADS, MEM_HEAD_DIM), k_norm)
    v = kv[..., MEM_WIDTH:].reshape(B, M, MEM_HEADS, MEM_HEAD_DIM)
    s = jnp.einsum('bshd,bmhd->bhsm', q, k).astype(jnp.float32) * (MEM_HEAD_DIM ** -0.5)
    p = jax.nn.softmax(s, axis=-1)
    return jnp.einsum('bhsm,bmhd->bshd', p.astype(v.dtype), v).reshape(B, S, MEM_WIDTH)

def first_inputs(seed: int = 0) -> dict:
    key = jax.random.key(seed)
    ks = iter(jax.random.split(key, 40))

    def nrm(shape, scale):
        return jax.random.normal(next(ks), shape, jnp.float32) * scale

    def gain(n):
        return 1.0 + nrm((DEPTH, n), 0.05)

    L = DEPTH
    d = D_MODEL
    x = nrm((BATCH, SEQ, d), 1.0)
    mem = nrm((BATCH, MEM_LEN, d), 1.0)
    offset = jax.random.randint(next(ks), (BATCH, 1), 0, 1024, dtype=jnp.int32)
    positions = offset + jnp.arange(SEQ, dtype=jnp.int32)[None, :]
    return {
        "x": x,
        "mem": mem,
        "positions": positions,
        "ffn1_norm": gain(d),
        "ffn1_w_gu": nrm((L, d, 2 * D_FF), d ** -0.5),
        "ffn1_w_down": nrm((L, D_FF, d), D_FF ** -0.5),
        "mix_norm": gain(d),
        "w_in": nrm((L, d, IN_COLS), d ** -0.5),
        "b_gate": nrm((L, N_BRANCH * d), 0.02),
        "sg_ln_g": gain(SG_WIDTH),
        "sg_ln_b": nrm((L, SG_WIDTH), 0.02),
        "sg_w": nrm((L, SG_GROUPS, CHUNK, CHUNK), 0.5 * CHUNK ** -0.5),
        "sg_b": 1.0 + nrm((L, SG_GROUPS, CHUNK), 0.1),
        "mla_cq_norm": gain(MLA_Q_RANK),
        "mla_w_uq": nrm((L, MLA_Q_RANK, MLA_HEADS * MLA_QK), MLA_Q_RANK ** -0.5),
        "mla_ckv_norm": gain(MLA_KV_RANK),
        "mla_w_ukv": nrm((L, MLA_KV_RANK, MLA_HEADS * (MLA_NOPE + MLA_V)), MLA_KV_RANK ** -0.5),
        "mla_q_norm": gain(MLA_QK),
        "mla_k_norm": gain(MLA_QK),
        "mem_norm": gain(d),
        "mem_w_kv": nrm((L, d, 2 * MEM_WIDTH), d ** -0.5),
        "mem_q_norm": gain(MEM_HEAD_DIM),
        "mem_k_norm": gain(MEM_HEAD_DIM),
        "w_branch_a": nrm((L, SG_WIDTH, d), SG_WIDTH ** -0.5),
        "w_branch_b": nrm((L, MLA_WIDTH, d), MLA_WIDTH ** -0.5),
        "w_branch_c": nrm((L, MEM_WIDTH, d), MEM_WIDTH ** -0.5),
        "w_out": nrm((L, d, d), d ** -0.5),
        "ffn2_norm": gain(d),
        "ffn2_w_gu": nrm((L, d, 2 * D_FF), d ** -0.5),
        "ffn2_w_down": nrm((L, D_FF, d), D_FF ** -0.5),
    }

def first_block(x, mem, positions, ffn1_norm, ffn1_w_gu, ffn1_w_down, mix_norm, w_in, b_gate,
              sg_ln_g, sg_ln_b, sg_w, sg_b, mla_cq_norm, mla_w_uq, mla_ckv_norm, mla_w_ukv,
              mla_q_norm, mla_k_norm, mem_norm, mem_w_kv, mem_q_norm, mem_k_norm,
              w_branch_a, w_branch_b, w_branch_c, w_out, ffn2_norm, ffn2_w_gu, ffn2_w_down):
    B, S, _ = x.shape
    for l in range(DEPTH):
        x = x + 0.5 * swiglu(rmsnorm(x, ffn1_norm[l]), ffn1_w_gu[l], ffn1_w_down[l])
        h = rmsnorm(x, mix_norm[l])
        z = h @ w_in[l]
        u = jax.nn.gelu(z[..., COL_U:COL_V], approximate=False)
        v = jax.nn.gelu(z[..., COL_V:COL_CQ], approximate=False)
        y_a = spatial_gating(u, v, sg_ln_g[l], sg_ln_b[l], sg_w[l], sg_b[l])
        y_b = mla(z[..., COL_CQ:COL_CKV], z[..., COL_CKV:COL_KR], z[..., COL_KR:COL_QM], positions,
                  mla_cq_norm[l], mla_w_uq[l], mla_ckv_norm[l], mla_w_ukv[l],
                  mla_q_norm[l], mla_k_norm[l])
        y_c = memory_attention(z[..., COL_QM:COL_GATE], mem, mem_norm[l], mem_w_kv[l],
                               mem_q_norm[l], mem_k_norm[l])
        gates = jax.nn.sigmoid(z[..., COL_GATE:] + b_gate[l]).reshape(B, S, N_BRANCH, D_MODEL)
        merged = (gates[:, :, 0] * (y_a @ w_branch_a[l])
                  + gates[:, :, 1] * (y_b @ w_branch_b[l])
                  + gates[:, :, 2] * (y_c @ w_branch_c[l]))
        x = x + merged @ w_out[l]
        x = x + 0.5 * swiglu(rmsnorm(x, ffn2_norm[l]), ffn2_w_gu[l], ffn2_w_down[l])
    return x


GRID_W = 64
CTX_LEN = 256
N_MIXERS = 2
CONV_WIDTH = 3
GLA_HEADS = 4
GLA_DK_TOT = D_MODEL // 2
GLA_DV_TOT = D_MODEL
GLA_DK = GLA_DK_TOT // GLA_HEADS
GLA_DV = GLA_DV_TOT // GLA_HEADS
GLA_GATE_RANK = 16
GLA_TAU = 16.0
GLA_CHUNK = 64
D_FF_2 = -(-8 * D_MODEL // (3 * 256)) * 256
N_ADA = 6


def rmsnorm_2(x, g):
    xf = x.astype(jnp.float32)
    y = xf * lax.rsqrt(jnp.mean(xf * xf, axis=-1, keepdims=True) + EPS)
    return (y * g.astype(jnp.float32)).astype(x.dtype)

def ada_terms(cond, w, b):
    return jnp.split(jax.nn.silu(cond) @ w + b, N_ADA, axis=-1)

def modulate(h, shift, scale):
    return h * (1.0 + scale) + shift

def conv3_seq(u, w):
    up = jnp.pad(u, ((0, 0), (1, 1), (0, 0)))
    return w[0] * up[:, :-2] + w[1] * up[:, 1:-1] + w[2] * up[:, 2:]

def conv3_grid(u, w):
    B, L, C = u.shape
    rows = L // GRID_W
    return conv3_seq(u.reshape(B * rows, GRID_W, C), w).reshape(B, L, C)

def short_conv_mixer(h, w_in, conv_w, w_out, on_grid):
    gate_b, gate_c, hv = jnp.split(h @ w_in, 3, axis=-1)
    u = gate_c * hv
    conv = conv3_grid(u, conv_w) if on_grid else conv3_seq(u, conv_w)
    return (gate_b * conv) @ w_out

def gla_project(h, w_in, b_r, w_a1, w_a2, b_a):
    B, L, _ = h.shape
    q, k, v, r = jnp.split(h @ w_in, [GLA_DK_TOT, 2 * GLA_DK_TOT, 2 * GLA_DK_TOT + GLA_DV_TOT], axis=-1)

    def heads(t, d):
        return t.reshape(B, L, GLA_HEADS, d).transpose(0, 2, 1, 3).astype(jnp.float32)

    q = heads(q, GLA_DK) * (GLA_DK ** -0.5)
    k = heads(k, GLA_DK)
    v = heads(v, GLA_DV)
    logit = jnp.einsum('zblr,zrk->zblk', jnp.einsum('bld,zdr->zblr', h, w_a1), w_a2) + b_a[:, None, None, :]
    la = jax.nn.log_sigmoid(logit.astype(jnp.float32)) / GLA_TAU
    la = la.reshape(2, B, L, GLA_HEADS, GLA_DK).transpose(0, 1, 3, 2, 4)
    return q, k, v, r + b_r, la

def gla_chunked(q, k, v, la, s0, with_output):
    B, H, T, dk = q.shape
    dv = v.shape[-1]
    n = T // GLA_CHUNK
    q = q.reshape(B, H, n, GLA_CHUNK, dk)
    k = k.reshape(B, H, n, GLA_CHUNK, dk)
    v = v.reshape(B, H, n, GLA_CHUNK, dv)
    b = jnp.cumsum(la.reshape(B, H, n, GLA_CHUNK, dk), axis=3)
    b_last = b[:, :, :, -1]
    k_dec = k * jnp.exp(b_last[:, :, :, None] - b)
    u = jnp.einsum('bhnsd,bhnse->bhnde', k_dec, v)

    def step(state, inp):
        decay, u_n = inp
        return decay[..., None] * state + u_n, state

    s_final, s_prev = lax.scan(step, s0, (jnp.moveaxis(jnp.exp(b_last), 2, 0), jnp.moveaxis(u, 2, 0)))
    if not with_output:
        return None, s_final
    s_prev = jnp.moveaxis(s_prev, 0, 2)
    q_dec = q * jnp.exp(b)
    o_inter = jnp.einsum('bhncd,bhnde->bhnce', q_dec, s_prev)
    scores = jnp.einsum('bhncd,bhnsd->bhncs', q_dec, k * jnp.exp(-b))
    mask = jnp.tril(jnp.ones((GLA_CHUNK, GLA_CHUNK), dtype=bool))
    scores = jnp.where(mask, scores, 0.0)
    o_intra = jnp.einsum('bhncs,bhnse->bhnce', scores, v)
    return (o_inter + o_intra).reshape(B, H, T, dv), s_final

def gla_output(o, r, norm_g, w_out, dtype):
    B, H, T, dv = o.shape
    o = rmsnorm_2(o.transpose(0, 2, 1, 3), norm_g).reshape(B, T, H * dv).astype(dtype)
    return (o * jax.nn.silu(r)) @ w_out

def gla_mixer(hl, hc, w_in, b_r, w_a1, w_a2, b_a, norm_g, w_out, ctx_out):
    ql, kl, vl, rl, la_l = gla_project(hl, w_in, b_r, w_a1, w_a2, b_a)
    qc, kc, vc, rc, la_c = gla_project(hc, w_in, b_r, w_a1, w_a2, b_a)
    flip = lambda t: jnp.flip(t, axis=2)
    s0 = jnp.zeros((hl.shape[0], GLA_HEADS, GLA_DK, GLA_DV), jnp.float32)
    o_cf, s_cf = gla_chunked(qc, kc, vc, la_c[0], s0, ctx_out)
    o_cb, s_cb = gla_chunked(flip(qc), flip(kc), flip(vc), flip(la_c[1]), s0, ctx_out)
    o_lf, _ = gla_chunked(ql, kl, vl, la_l[0], s_cf, True)
    o_lb, _ = gla_chunked(flip(ql), flip(kl), flip(vl), flip(la_l[1]), s_cb, True)
    yl = gla_output(o_lf + flip(o_lb), rl, norm_g, w_out, hl.dtype)
    yc = gla_output(o_cf + flip(o_cb), rc, norm_g, w_out, hc.dtype) if ctx_out else None
    return yl, yc

def swiglu_2(h, w_in, w_out):
    gate, up = jnp.split(h @ w_in, 2, axis=-1)
    return (jax.nn.silu(gate) * up) @ w_out

def second_inputs(seed: int = 0) -> dict:
    key = jax.random.key(seed)
    ks = jax.random.split(key, 24)
    n_conv = (DEPTH + N_MIXERS - 1) // N_MIXERS
    n_gla = DEPTH // N_MIXERS
    nrm = lambda k, shape, s: jax.random.normal(k, shape, jnp.float32) * s
    d = D_MODEL
    return {
        "x": nrm(ks[0], (BATCH, SEQ, d), 1.0),
        "c": nrm(ks[1], (BATCH, d), 1.0),
        "ctx": nrm(ks[2], (BATCH, CTX_LEN, d), 1.0),
        "c_ctx": nrm(ks[3], (d,), 1.0),
        "ada_w": nrm(ks[4], (DEPTH, d, N_ADA * d), 0.5 * d ** -0.5),
        "ada_b": nrm(ks[5], (DEPTH, N_ADA * d), 0.01),
        "norm1_g": 1.0 + nrm(ks[6], (DEPTH, d), 0.02),
        "norm2_g": 1.0 + nrm(ks[7], (DEPTH, d), 0.02),
        "conv_w_in": nrm(ks[8], (n_conv, d, 3 * d), d ** -0.5),
        "conv_w": nrm(ks[9], (n_conv, CONV_WIDTH, d), CONV_WIDTH ** -0.5),
        "conv_w_out": nrm(ks[10], (n_conv, d, d), d ** -0.5),
        "gla_w_in": nrm(ks[11], (n_gla, d, 2 * GLA_DK_TOT + 2 * GLA_DV_TOT), d ** -0.5),
        "gla_b_r": nrm(ks[12], (n_gla, GLA_DV_TOT), 0.01),
        "gla_w_a1": nrm(ks[13], (n_gla, 2, d, GLA_GATE_RANK), d ** -0.5),
        "gla_w_a2": nrm(ks[14], (n_gla, 2, GLA_GATE_RANK, GLA_DK_TOT), GLA_GATE_RANK ** -0.5),
        "gla_b_a": nrm(ks[15], (n_gla, 2, GLA_DK_TOT), 0.01),
        "gla_norm_g": 1.0 + nrm(ks[16], (n_gla, GLA_DV), 0.02),
        "gla_w_out": nrm(ks[17], (n_gla, GLA_DV_TOT, d), GLA_DV_TOT ** -0.5),
        "ffn_w_in": nrm(ks[18], (DEPTH, d, 2 * D_FF_2), d ** -0.5),
        "ffn_w_out": nrm(ks[19], (DEPTH, D_FF_2, d), D_FF_2 ** -0.5),
        "final_g": 1.0 + nrm(ks[20], (d,), 0.02),
    }

def second_block(x, c, ctx, c_ctx, ada_w, ada_b, norm1_g, norm2_g, conv_w_in, conv_w, conv_w_out,
              gla_w_in, gla_b_r, gla_w_a1, gla_w_a2, gla_b_a, gla_norm_g, gla_w_out,
              ffn_w_in, ffn_w_out, final_g):
    cond_lat = c[:, None, :]
    for i in range(DEPTH):
        last = i == DEPTH - 1
        kind = i % N_MIXERS
        j = i // N_MIXERS
        need_ctx_in = (not last) or kind == 1
        sh1, sc1, g1, sh2, sc2, g2 = ada_terms(cond_lat, ada_w[i], ada_b[i])
        hl = modulate(rmsnorm_2(x, norm1_g[i]), sh1, sc1)
        if need_ctx_in:
            csh1, csc1, cg1, csh2, csc2, cg2 = ada_terms(c_ctx, ada_w[i], ada_b[i])
            hc = modulate(rmsnorm_2(ctx, norm1_g[i]), csh1, csc1)
        if kind == 0:
            yl = short_conv_mixer(hl, conv_w_in[j], conv_w[j], conv_w_out[j], True)
            yc = short_conv_mixer(hc, conv_w_in[j], conv_w[j], conv_w_out[j], False) if not last else None
        else:
            yl, yc = gla_mixer(hl, hc, gla_w_in[j], gla_b_r[j], gla_w_a1[j], gla_w_a2[j], gla_b_a[j],
                               gla_norm_g[j], gla_w_out[j], not last)
        x = x + g1 * yl
        x = x + g2 * swiglu_2(modulate(rmsnorm_2(x, norm2_g[i]), sh2, sc2), ffn_w_in[i], ffn_w_out[i])
        if not last:
            ctx = ctx + cg1 * yc
            ctx = ctx + cg2 * swiglu_2(modulate(rmsnorm_2(ctx, norm2_g[i]), csh2, csc2), ffn_w_in[i], ffn_w_out[i])
    return rmsnorm_2(x, final_g)


def setup_inputs(seed=0):
    out = dict(first_inputs(seed))
    for name, value in second_inputs(seed + 1).items():
        if name != "x":
            out[name + "_2"] = value
    return out


def reference(
    x, mem, positions, ffn1_norm, ffn1_w_gu, ffn1_w_down, mix_norm, w_in, b_gate, sg_ln_g,
    sg_ln_b, sg_w, sg_b, mla_cq_norm, mla_w_uq, mla_ckv_norm, mla_w_ukv, mla_q_norm, mla_k_norm,
    mem_norm, mem_w_kv, mem_q_norm, mem_k_norm, w_branch_a, w_branch_b, w_branch_c, w_out,
    ffn2_norm, ffn2_w_gu, ffn2_w_down, c_2, ctx_2, c_ctx_2, ada_w_2, ada_b_2, norm1_g_2,
    norm2_g_2, conv_w_in_2, conv_w_2, conv_w_out_2, gla_w_in_2, gla_b_r_2, gla_w_a1_2,
    gla_w_a2_2, gla_b_a_2, gla_norm_g_2, gla_w_out_2, ffn_w_in_2, ffn_w_out_2, final_g_2,
):
    x = first_block(
        x, mem, positions, ffn1_norm, ffn1_w_gu, ffn1_w_down, mix_norm, w_in, b_gate, sg_ln_g,
        sg_ln_b, sg_w, sg_b, mla_cq_norm, mla_w_uq, mla_ckv_norm, mla_w_ukv, mla_q_norm,
        mla_k_norm, mem_norm, mem_w_kv, mem_q_norm, mem_k_norm, w_branch_a, w_branch_b,
        w_branch_c, w_out, ffn2_norm, ffn2_w_gu, ffn2_w_down,
    )
    return second_block(
        x, c_2, ctx_2, c_ctx_2, ada_w_2, ada_b_2, norm1_g_2, norm2_g_2, conv_w_in_2, conv_w_2,
        conv_w_out_2, gla_w_in_2, gla_b_r_2, gla_w_a1_2, gla_w_a2_2, gla_b_a_2, gla_norm_g_2,
        gla_w_out_2, ffn_w_in_2, ffn_w_out_2, final_g_2,
    )


_drawn_inputs = setup_inputs


def setup_inputs(seed=0):
    import zlib

    import numpy as np

    out = dict(_drawn_inputs(seed))
    spreads = {}
    factors = {'b_gate': 8.0,
     'sg_ln_g': 28.644,
     'sg_ln_b': 64.0,
     'mla_cq_norm': 8.0,
     'mla_ckv_norm': 8.0,
     'mla_q_norm': 8.0,
     'mla_k_norm': 8.0,
     'mem_norm': 8.0,
     'mem_q_norm': 8.0,
     'mem_k_norm': 8.0,
     'ffn2_norm': 3.046,
     'ada_b_2': 3.959,
     'norm1_g_2': 5.463,
     'norm2_g_2': 64.0,
     'final_g_2': 7.825,
     'sg_b': 5.055}
    for name, (base, spread) in spreads.items():
        noise = np.random.default_rng([zlib.crc32(name.encode()), seed]).standard_normal(out[name].shape)
        drawn = base * np.exp(spread * noise) if base else spread * noise
        out[name] = __import__('jax').numpy.asarray(drawn.astype(out[name].dtype))
    for name, factor in factors.items():
        out[name] = (out[name] * factor).astype(out[name].dtype)
    return out
```

```python
from contextlib import ExitStack

import numpy as np

import concourse.bass as bass
from concourse import mybir

F32 = mybir.dt.float32
F32R = mybir.dt.float32r
I32 = mybir.dt.int32
ALU = mybir.AluOpType
ACT = mybir.ActivationFunctionType
AX = mybir.AxisListType

P = 128
D = 1024
KC = 8
FF = 2816
EPS = 1e-6
NEG = -1e30
RAW = 6
SPL = 4
AHEAD = 3
PI = float(np.pi)


def plan():
    out = []

    def add(name, n, w):
        out.extend((name, i, w, False) for i in range(n))

    def ffn(tag, terms):
        units = [(tag + "_up", i, 1024, False) for i in range(44)]
        units += [(tag + "_dn", i, 1024, False) for i in range(22)]
        ada = [("ada", i, 1024, True) for t in terms for i in range(8 * t, 8 * t + 8)]
        for i, u in enumerate(units):
            out.append(u)
            while ada and (24 - len(ada)) * 52 < (i + 1) * 24:
                out.append(ada.pop(0))

    ffn("f1", (0, 1, 2))
    add("mkv", 8, 1024)
    add("cq", 4, 768)
    add("ckv", 4, 576)
    add("qm", 4, 1024)
    add("v", 4, 1024)
    add("u", 4, 1024)
    add("uq", 3, 768)
    add("ukv", 2, 1024)
    for b in "acb":
        add("g" + b, 8, 1024)
        add("br" + b, 4, 1024)
    add("wo", 8, 1024)
    ffn("f2", (3, 4, 5))
    for i in (0, 1):
        add(f"cc{i}", 4, 1024)
        add(f"hv{i}", 4, 1024)
        add(f"gb{i}", 4, 1024)
    add("co", 8, 1024)
    out.extend(("f3_up", i, 1024, False) for i in range(44))
    out.extend(("f3_dn", i, 1024, False) for i in range(22))
    return out


class Queues:

    def __init__(self, sems, me, eng):
        self.sems, self.me, self.eng = sems, me, eng
        self.count = {name: 0 for name in sems}
        self.made = {}

    def wait(self, e, waits):
        if e == self.me:
            for s, v in waits:
                if self.made.get(s, 0) < v:
                    self.made[s] = v
                    self.eng.wait_ge(self.sems[s], v)

    def op(self, e, waits, fn):
        self.wait(e, waits)
        s = "s_" + e
        self.count[s] += 1
        if e == self.me:
            fn(self.eng).then_inc(self.sems[s], 1)
        return (s, self.count[s])

    def silent(self, e, waits, fn):
        self.wait(e, waits)
        if e == self.me:
            fn(self.eng)

    def dma(self, sem, waits, dst, src, e="sp"):
        self.wait(e, waits)
        self.count[sem] += 16
        if e == self.me:
            self.eng.dma_start(dst, src).then_inc(self.sems[sem], 16)
        return (sem, self.count[sem])


def build(nc, A, out):
    ctx = ExitStack()
    with ctx:
        def sb(name, shape, dt=F32, c=None):
            return (c or ctx).enter_context(nc.sbuf_tensor("t_" + name, shape, dt))

        raw = sb("raw", [P, RAW, 1024])
        wh = sb("wh", [P, SPL, 1024], F32R)
        wl = sb("wl", [P, SPL, 1024], F32R)
        X = sb("X", [P, 2, D])
        XH = sb("XH", [P, KC, 256], F32R)
        XL = sb("XL", [P, KC, 256], F32R)
        YH = sb("YH", [P, KC, 256], F32R)
        YL = sb("YL", [P, KC, 256], F32R)
        hn = sb("hn", [P, 2, D])
        tmpT = sb("tmpT", [P, 2, 512])
        gB = sb("gB", [P, 2, D])
        acc2 = sb("acc2", [P, 2, D])
        ident = sb("ident", [P, P])
        ones = sb("ones", [P, P])
        cols = sb("cols", [P, 192])
        sc = sb("sc", [P, 384])
        rp = sb("rp", [P, 2, 12, 16])
        rpi = sb("rpi", [P, 2, 16], I32)
        posi = sb("posi", [P, 2], I32)
        gqk = sb("gqk", [P, 2, 96])
        with ExitStack() as c:
            FG = sb("FG", [P, D], F32, c)
            HH = sb("HH", [P, 22, 256], F32R, c)
            HL = sb("HL", [P, 22, 256], F32R, c)
            sg = sb("sg", [P, 2, 2, 256], F32, c)
            hp = sb("hp", [P, 2, 2, 256], F32, c)
        with ExitStack() as c:
            gates = sb("gates", [P, 2, D], F32, c)
            bgate = sb("bgate", [P, D], F32, c)
            U = sb("U", [P, 2, 512], F32, c)
            V = sb("V", [P, 2, 512], F32, c)
            ZQ = sb("ZQ", [P, 2, 384], F32, c)
            ZK = sb("ZK", [P, 2, 288], F32, c)
            QM = sb("QM", [P, 2, 512], F32, c)
            MK = sb("MK", [P, 2, 512], F32, c)
            MV = sb("MV", [P, 2, 512], F32, c)
            QT = sb("QT", [P, 2, 768], F32, c)
            KT = sb("KT", [P, 2, 768], F32, c)
            VT = sb("VT", [P, 2, 512], F32, c)
            qkT = sb("qkT", [P, 512], F32, c)
            sS = sb("sS", [P, 512], F32, c)
            pS = sb("pS", [P, 512], F32, c)
            pT = sb("pT", [P, 512], F32, c)
            CH = sb("CH", [P, 5, 256], F32R, c)
            CL = sb("CL", [P, 5, 256], F32R, c)
            sgw = sb("sgw", [P, 8, P], F32, c)
            mask = sb("mask", [P, 384], F32, c)
        with ExitStack() as c:
            GC = sb("GC", [P, 2, 512], F32, c)
            UU = sb("UU", [P, 2, 512], F32, c)
            GB = sb("GB", [P, 2, 512], F32, c)
            uT = sb("uT", [P, 2, 512], F32, c)
            cT = sb("cT", [P, 2, 512], F32, c)
        ps = ctx.enter_context(nc.psum_tensor("ps", [P, 8, 512], F32))
        names = ["s_pe", "s_act", "s_dve", "s_pool", "s_x", "s_mem", "s_cols", "s_bc", "s_sg", "s_bg", "s_fin", "s_out"]
        sems = {n: ctx.enter_context(nc.semaphore(n)) for n in names + [f"s_raw{i}" for i in range(RAW)]}

        def schedule(q):
            stream = plan()

            used = [0]

            def col(n=1):
                a = used[0]
                used[0] += n
                assert used[0] <= 384
                return sc[:, a:a + n]

            held = set()

            bank_free = {b: [] for b in range(8)}

            def give(b, waits):
                held.discard(b)
                bank_free[b] = waits

            turn = {"main": 0, "aux": 0}

            def take(kind="main"):
                pool = (0, 1, 2, 3, 4, 5) if kind == "main" else (6, 7)
                for _ in pool:
                    b = pool[turn[kind] % len(pool)]
                    turn[kind] += 1
                    if b not in held:
                        held.add(b)
                        return b
                raise AssertionError("no bank is free")

            raw_free = {}
            raw_in = {}
            split_of = {}
            spl_free = {}
            state = {"dma": 0, "spl": 0, "use": 0, "nspl": 0, "done": 0}
            ada = {"ready": {}, "free": {0: [], 1: []}, "tok": None,
                   "acc": (acc2[:, 0, :], acc2[:, 1, :])}
            tasks = []

            def fetch():
                n = state["dma"]
                if n >= len(stream):
                    return
                name, i, w, _ = stream[n]
                s = n % RAW
                raw_in[n] = q.dma(f"s_raw{s}", raw_free.get(n - RAW, []), raw[:, s, 0:w], A[name][i])
                state["dma"] = n + 1

            def advance():
                n = state["spl"]
                name, i, w, only_raw = stream[n]
                r = raw[:, n % RAW, 0:w]
                if only_raw:
                    term, k = divmod(i, 8)
                    acc = ada["acc"][term % 2]
                    c = ada["c"][:, k:k + 1]
                    if k == 0:
                        ada["tok"] = q.op("dve", [raw_in[n], ada["c_tok"]] + ada["free"][term % 2],
                                          lambda e: e.tensor_scalar(acc, r, c, None, ALU.mult))
                    else:
                        ada["tok"] = q.op("dve", [raw_in[n], ada["tok"]],
                                          lambda e: e.scalar_tensor_tensor(out=acc, in0=r, scalar=c, in1=acc,
                                                                           op0=ALU.mult, op1=ALU.add))
                    raw_free[n] = [ada["tok"]]
                    if k == 7:
                        tasks.append(ada_reduce(term, ada["tok"]))
                else:
                    m = state["nspl"]
                    s = m % SPL
                    free = spl_free.get(m - SPL, [])
                    hi = q.op("act", [raw_in[n]] + free,
                              lambda e: e.activation(wh[:, s, 0:w], r, ACT.Copy))
                    lo = q.op("dve", [hi] + free,
                              lambda e: e.tensor_tensor(wl[:, s, 0:w], r, wh[:, s, 0:w].bitcast(F32), ALU.subtract))
                    raw_free[n] = [lo]
                    split_of[m] = [hi, lo]
                    state["nspl"] = m + 1
                state["spl"] = n + 1
                fetch()

            names = [u[0] for u in stream if not u[3]]

            def step_tasks(n=1):
                for _ in range(n):
                    for t in list(tasks[:2]):
                        if next(t, "end") == "end":
                            tasks.remove(t)

            def begin(t, first=False):
                next(t)
                tasks.insert(0, t) if first else tasks.append(t)

            def finish(t):
                for _ in t:
                    pass
                if t in tasks:
                    tasks.remove(t)

            def unit(name, blocks, lh, ll, ready):
                u = state["use"]
                assert names[u] == name, (names[u], name)
                while state["nspl"] < min(u + 1 + AHEAD, len(names)):
                    advance()
                s = u % SPL
                waits = list(split_of[u])
                tok = None
                for kc, c0, w, banks, start, stop in blocks:
                    for t in (0, 1):
                        o = ps[:, banks[t], 0:w]
                        ww = waits + ready(kc) + (bank_free[banks[t]] if start else [])
                        waits = []
                        xh, xl = lh[:, kc, t * P:t * P + P], ll[:, kc, t * P:t * P + P]
                        h, l = wh[:, s, c0:c0 + w], wl[:, s, c0:c0 + w]
                        q.silent("pe", ww, lambda e, o=o, a=xh, b=h, st=start: e.matmul(o, a, b, start=st, stop=False))
                        q.silent("pe", [], lambda e, o=o, a=xh, b=l: e.matmul(o, a, b, start=False, stop=False))
                        last = lambda e, o=o, a=xl, b=h, sp=stop: e.matmul(o, a, b, start=False, stop=sp)
                        tok = q.op("pe", [], last)
                spl_free[u] = [tok]
                state["use"] = u + 1
                step_tasks()
                return tok

            def group(name, w, lh, ll, ready, step=2):
                banks = (take(), take())
                for i in range(4):
                    tok = unit(name, [(2 * i + j, j * w, w, banks, i + j == 0, i == 3 and j == 1)
                                      for j in (0, 1)], lh, ll, ready)
                return banks, tok

            def wide(name, n, w, lh, ll, ready):
                banks = [(take(), take()), (take(), take())]
                for k in range(n):
                    tok = unit(name, [(k, j * w, w, banks[j], k == 0, k == n - 1) for j in (0, 1)],
                               lh, ll, ready)
                return banks, tok

            def rstd(ss, n, waits):
                k = ss.shape[-1]
                m, r = col(k), col(k)
                t = q.op("dve", waits, lambda e: e.tensor_scalar(m, ss, 1.0 / n, EPS, ALU.mult, ALU.add))
                t = q.op("pool", [t, c_half], lambda e: e.tensor_tensor(r, m, mhalf[:, 0:k], ALU.pow))
                return r, t

            def split_from(src, hi, lo, waits, free, on="act"):
                if on == "act":
                    a = q.op("act", waits + free, lambda e: e.activation(hi, src, ACT.Copy))
                else:
                    a = q.op("dve", waits + free, lambda e: e.tensor_copy(hi, src))
                b = q.op("dve", [a] + waits + free,
                         lambda e: e.tensor_tensor(lo, src, hi.bitcast(F32), ALU.subtract))
                return [a, b]

            tmp_free = {0: [], 1: []}
            nt = [0]

            def transposed(src, waits, n, hi, lo, tok_of, free, a=None, b=None, kind="main", first=0):
                for j in range(n // 2):
                    bank = take(kind)
                    for c in (2 * j, 2 * j + 1):
                        for t in (0, 1):
                            o = ps[:, bank, (c % 2) * 256 + t * P:(c % 2) * 256 + t * P + P]
                            tok = q.op("pe", waits[t] + c_id + (bank_free[bank] if c % 2 == 0 and t == 0 else []),
                                       lambda e, o=o, i=src[t][:, c * P:c * P + P]: e.transpose(o, i, ident[:, :]))
                    h2, l2 = hi[:, first + 2 * j:first + 2 * j + 2, :], lo[:, first + 2 * j:first + 2 * j + 2, :]
                    if a is None:
                        p2 = ps[:, bank, :].rearrange("p (c n) -> p c n", c=2)
                        ab = split_from(p2, h2, l2, [tok], free)
                        give(bank, [ab[1]])
                    else:
                        s = nt[0] % 2
                        nt[0] += 1
                        for c in (0, 1):
                            k = 2 * j + c
                            bias = 0.0 if b is None else b[:, k:k + 1]
                            m = q.op("act", [tok] + tmp_free[s] + ab_ready[0],
                                     lambda e, c=c, k=k, bias=bias: e.activation(
                                         tmpT[:, s, c * 256:c * 256 + 256], ps[:, bank, c * 256:c * 256 + 256],
                                         ACT.Identity, bias=bias, scale=a[:, k:k + 1]))
                        give(bank, [m])
                        ab = split_from(tmpT[:, s, :].rearrange("p (c n) -> p c n", c=2), h2, l2, [m], free, on="dve")
                        tmp_free[s] = ab
                    tok_of[first + 2 * j] = tok_of[first + 2 * j + 1] = ab
                    yield

            ab_ready = [[]]
            x_ready = {0: [], 1: []}
            xt_tok, yt_tok = {}, {}
            xt_free, yt_free = [[]], [[]]
            hn_free = {0: [], 1: []}

            def normed(src, src_tok, a, b, hi, lo, tok_of, free):
                toks = {}
                for t in (0, 1):
                    ss = col()
                    k = q.op("act", src_tok[t] + hn_free[t],
                             lambda e, t=t, ss=ss: e.activation(hn[:, t, :], src[:, t, :], ACT.Square, accum_out=ss))
                    r, k = rstd(ss, D, [k])
                    toks[t] = [q.op("dve", [k], lambda e, t=t, r=r: e.tensor_scalar(
                        hn[:, t, :], src[:, t, :], r, None, ALU.mult))]
                yield
                tok_of.clear()
                yield from transposed([hn[:, 0, :], hn[:, 1, :]], toks, 8, hi, lo, tok_of, free, a, b)
                for t in (0, 1):
                    hn_free[t] = [("s_pe", q.count["s_pe"])]

            def add_residual(banks, tok, how):
                for t in (0, 1):
                    for j in (0, 1):
                        o, xs = ps[:, banks[j][t], :], X[:, t, j * 512:j * 512 + 512]
                        if how == "half":
                            k = q.op("dve", [tok], lambda e, o=o, xs=xs: e.scalar_tensor_tensor(
                                out=xs, in0=o, scalar=0.5, in1=xs, op0=ALU.mult, op1=ALU.add))
                        elif how == "plain":
                            k = q.op("dve", [tok], lambda e, o=o, xs=xs: e.tensor_tensor(xs, o, xs, ALU.add))
                        else:
                            g = gB[:, how, j * 512:j * 512 + 512]
                            m = q.op("dve", [tok] + gb_tok[how] + hn_free[t],
                                     lambda e, o=o, g=g, t=t, j=j: e.tensor_tensor(
                                         hn[:, t, j * 512:j * 512 + 512], o, g, ALU.mult))
                            give(banks[j][t], [m])
                            k = q.op("dve", [m], lambda e, xs=xs, t=t, j=j: e.tensor_tensor(
                                xs, hn[:, t, j * 512:j * 512 + 512], xs, ALU.add))
                            hn_free[t] = [k]
                            continue
                        give(banks[j][t], [k])
                    x_ready[t] = [k]

            for _ in range(2):
                fetch()
            x_in = [q.dma("s_x", [], X[:, t, :], A["x"][t]) for t in (0, 1)][-1]
            x_ready = {0: [x_in], 1: [x_in]}
            m_in = q.dma("s_mem", [], hn[:, 0, :], A["mem"][0])
            m_in = q.dma("s_mem", [], hn[:, 1, :], A["mem"][1])
            c_in = q.dma("s_cols", [], cols[:, 0:A["cols"].shape[1]], A["cols"])
            for _ in range(RAW - 2):
                fetch()
            b_in = [q.dma("s_bc", [], gB[:, 0, :], A["adab_g"][0:1, :].to_broadcast([P, D])),
                    q.dma("s_bc", [], gB[:, 1, :], A["adab_g"][1:2, :].to_broadcast([P, D])),
                    q.dma("s_bc", [], gqk[:, 0, :], A["mla_q_norm"][0:1, :].to_broadcast([P, 96])),
                    q.dma("s_bc", [], gqk[:, 1, :], A["mla_k_norm"][0:1, :].to_broadcast([P, 96])),
                    q.dma("s_bc", [], posi[:, :], A["positions"]),
                    q.dma("s_bc", [], rp[:, 0, 0, :], A["inv"][0:1, :].to_broadcast([P, 16])),
                    q.dma("s_bc", [], rp[:, 1, 0, :], A["inv"][0:1, :].to_broadcast([P, 16]))][-1]
            gb_tok = {0: [], 1: []}

            C = {}
            at = 0
            for nm, k in COLS:
                C[nm] = cols[:, at:at + k]
                at += k

            mhalf = sc[:, 0:8]
            used[0] = 8
            c_half = q.op("pool", [], lambda e: e.memset(mhalf, -0.5))
            z = q.op("pool", [], lambda e: e.memset(ident[:, :], 0.0))
            c_id = [q.op("pool", [z], lambda e: e.affine_select(
                out=ident[:, :], in_=ident[:, :], compare_op=ALU.not_equal, fill=1.0, base=0,
                pattern=[[-1, P]], channel_multiplier=1))]
            c_one = q.op("pool", [], lambda e: e.memset(ones[:, :], 1.0))

            ada["c"] = col(8)
            ada["c_tok"] = q.op("act", [c_in], lambda e: e.activation(ada["c"], C["c"], ACT.Silu))
            mod = {k: col(8) for k in ("b1", "a1", "b2", "a2")}
            mod_tok = {}

            def ada_reduce(term, tok):
                acc = ada["acc"][term % 2]
                yield
                if term in (2, 5):
                    g = 0 if term == 2 else 1
                    bk = take("aux"), take("aux")
                    for j in (0, 1):
                        k = q.op("pe", [tok, c_one] + bank_free[bk[j]], lambda e, j=j: e.matmul(
                            ps[:, bk[j], :], ones[:, :], acc[:, j * 512:j * 512 + 512], start=True, stop=True))
                        d = q.op("dve", [k, b_in], lambda e, j=j: e.tensor_tensor(
                            gB[:, g, j * 512:j * 512 + 512], ps[:, bk[j], :], gB[:, g, j * 512:j * 512 + 512], ALU.add))
                        give(bk[j], [d])
                    gb_tok[g] = [d]
                else:
                    bk = take("aux")
                    for c in range(8):
                        k = q.op("pe", [tok, c_one] + (bank_free[bk] if c == 0 else []), lambda e, c=c: e.matmul(
                            ps[:, bk, 2 * c:2 * c + 1], acc[:, c * P:c * P + P], ones[:, 0:1], start=True, stop=True))
                    pv = ps[:, bk, 0:16].rearrange("p (c x) -> p c x", x=2)[:, :, 0]
                    nm, bias = {0: ("b1", "ab_sh1"), 1: ("a1", "ab_sc1"), 3: ("b2", "ab_sh2"), 4: ("a2", "ab_sc2")}[term]
                    d = q.op("dve", [k, c_in], lambda e: e.tensor_tensor(mod[nm], pv, C[bias], ALU.add))
                    give(bk, [d])
                    if nm[0] == "a":
                        g = C["norm1" if nm == "a1" else "norm2"]
                        d = q.op("dve", [d], lambda e: e.scalar_tensor_tensor(
                            out=mod[nm], in0=mod[nm], scalar=1.0, in1=g, op0=ALU.add, op1=ALU.mult))
                    mod_tok[nm] = d
                ada["free"][term % 2] = [("s_pe", q.count["s_pe"])]

            def ffn(tag, how):
                hid_tok = {}
                n_sg = [0]

                def hidden(g, banks, tok):
                    s = g % 2
                    hs = []
                    for t in (0, 1):
                        a = q.op("act", [tok] + sg_free[s], lambda e, t=t: e.activation(
                            sg[:, s, t, :], ps[:, banks[t], 0:256], ACT.Silu))
                        d = q.op("dve", [a] + hp_free[s], lambda e, t=t: e.tensor_tensor(
                            hp[:, s, t, :], sg[:, s, t, :], ps[:, banks[t], 256:512], ALU.mult))
                        give(banks[t], [d])
                        hs.append([d])
                    sg_free[s] = hs[1]
                    yield
                    yield from transposed([hp[:, s, 0, :], hp[:, s, 1, :]], hs, 2, HH, HL, hid_tok,
                                          ffn_free[0], kind="aux", first=2 * g)
                    hp_free[s] = [("s_pe", q.count["s_pe"])]

                sg_free = {0: ffn_free[0], 1: ffn_free[0]}
                hp_free = {0: ffn_free[0], 1: ffn_free[0]}
                for g in range(11):
                    banks, tok = group(tag + "_up", 512, XH, XL, lambda kc: xt_tok[kc])
                    begin(hidden(g, banks, tok), True)
                xt_free[0] = [tok]

                def ready(kc):
                    while kc not in hid_tok:
                        step_tasks()
                    return hid_tok[kc]

                banks, tok = wide(tag + "_dn", 22, 512, HH, HL, ready)
                while tasks:
                    step_tasks()
                add_residual(banks, tok, how)
                return tok

            ffn_free = [[]]
            hn_free = {0: [m_in], 1: [m_in]}

            def mem_norm():
                toks = {}
                for t in (0, 1):
                    ss = col()
                    k = q.op("act", [m_in], lambda e, t=t, ss=ss: e.activation(
                        tmpT[:, :, :], hn[:, t, 0:D].rearrange("p (a b) -> p a b", a=2), ACT.Square, accum_out=ss)) \
                        if t == 0 else q.op("act", [m_in, tmpw[0]], lambda e, t=t, ss=ss: e.activation(
                            tmpT[:, :, :], hn[:, t, 0:D].rearrange("p (a b) -> p a b", a=2), ACT.Square, accum_out=ss))
                    tmpw[0] = k
                    r, k = rstd(ss, D, [k])
                    toks[t] = [q.op("dve", [k], lambda e, t=t, r=r: e.tensor_scalar(
                        hn[:, t, :], hn[:, t, :], r, None, ALU.mult))]
                for s in (0, 1):
                    tmp_free[s] = [tmpw[0]]
                ab_ready[0] = [c_in]
                yield from transposed([hn[:, 0, :], hn[:, 1, :]], toks, 8, YH, YL, yt_tok, [], C["mem_norm"], None)
                for t in (0, 1):
                    hn_free[t] = [("s_pe", q.count["s_pe"])]

            tmpw = [None]
            finish(mem_norm())
            finish(normed(X, x_ready, C["ffn1"], None, XH, XL, xt_tok, []))

            last = ffn("f1", "half")

            after = [last, ("s_dve", q.count["s_dve"]), ("s_act", q.count["s_act"])]

            s_in = [q.dma("s_sg", after, gates[:, 0, 0:512], A["sg_ln_g"][0:1, :].to_broadcast([P, 512])),
                    q.dma("s_sg", after, gates[:, 0, 512:1024], A["sg_ln_b"][0:1, :].to_broadcast([P, 512])),
                    q.dma("s_sg", after, sgw[:, :, :], A["sg_wT"])][-1]
            sgw_tok = q.op("pool", after + [s_in], lambda e: e.affine_select(
                out=sgw[:, :, :], in_=sgw[:, :, :], compare_op=ALU.is_ge, fill=0.0, base=0,
                pattern=[[0, 8], [1, P]], channel_multiplier=-1))
            mk = q.op("pool", after, lambda e: e.memset(mask[:, :], 0.0))
            for o in (0, 256):
                mk = q.op("pool", [mk], lambda e, o=o: e.affine_select(
                    out=mask[:, o:o + P], in_=mask[:, o:o + P], compare_op=ALU.is_ge, fill=NEG, base=0,
                    pattern=[[-1, P]], channel_multiplier=1))
            mask_tok = mk

            def tables():
                rope_tok = []
                for t in (0, 1):
                    R = lambda i, t=t: rp[:, t, i, :]
                    pf = col()
                    k = q.op("dve", [b_in], lambda e: e.tensor_copy(pf, posi[:, t:t + 1]))
                    k = q.op("dve", [k], lambda e: e.tensor_scalar(R(1), R(0), pf, None, ALU.mult))
                    k = q.op("dve", [k], lambda e: e.tensor_scalar(R(2), R(1), 1.0 / (2 * PI), None, ALU.mult))
                    k = q.op("dve", [k], lambda e: e.tensor_copy(rpi[:, t, :], R(2)))
                    k = q.op("dve", [k], lambda e: e.tensor_copy(R(3), rpi[:, t, :]))
                    c1, c2 = 6.28125, float(np.float32(np.round((2 * np.pi - 6.28125) * 2 ** 20) / 2 ** 20))
                    c3 = float(2 * np.pi - 6.28125 - c2)
                    for n, cc in enumerate((c1, c2, c3)):
                        k = q.op("dve", [k], lambda e, n=n, cc=cc: e.scalar_tensor_tensor(
                            out=R(1), in0=R(3), scalar=-cc, in1=R(1), op0=ALU.mult, op1=ALU.add))
                    k = q.op("dve", [k], lambda e: e.tensor_scalar(R(4), R(1), PI, -PI, ALU.min, ALU.max))
                    k = q.op("dve", [k], lambda e: e.tensor_scalar(R(5), R(4), PI / 2, -2 * PI, ALU.is_gt, ALU.mult))
                    k = q.op("dve", [k], lambda e: e.scalar_tensor_tensor(
                        out=R(6), in0=R(4), scalar=PI / 2, in1=R(5), op0=ALU.add, op1=ALU.add))
                    k = q.op("dve", [k], lambda e: e.tensor_scalar(R(7), R(6), PI, -PI, ALU.min, ALU.max))
                    a = q.op("act", [k], lambda e: e.activation(R(8), R(7), ACT.Sin))
                    rope_tok.append(q.op("act", [k], lambda e: e.activation(R(9), R(4), ACT.Sin)))
                    yield
                tok["rope"] = rope_tok

            tok = {}

            def head_stats(src, n, hd, waits, junk):
                s3 = src.rearrange("p (h d) -> p h d", h=n)
                j3 = junk.rearrange("p (h d) -> p h d", h=n)
                ss = col(n)
                k = q.op("dve", waits, lambda e: e.tensor_tensor(j3, s3, s3, ALU.mult))
                k = q.op("dve", [k], lambda e: e.tensor_reduce(ss, j3, AX.X, ALU.add))
                return rstd(ss, hd, [k])

            def plain_evac(dst, banks, k0, w, key, func=None, accum=None):
                for t in (0, 1):
                    b = banks[t]
                    a = {} if accum is None else {"accum_out": accum[t]}
                    k = q.op("act", [k0] + after, lambda e, t=t, b=b, a=a: e.activation(
                        dst[:, t, 0:w], ps[:, b, 0:w], func or ACT.Copy, **a))
                    give(b, [k])
                    tok[key, t] = k

            def mem_k(banks, k0):
                plain_evac(MK, banks, k0, 512, "mkr")
                yield
                for t in (0, 1):
                    k = tok["mkr", t]
                    r, k2 = head_stats(MK[:, t, :], 4, 128, [k] + sS_free[0], sS[:, :])
                    sS_free[0] = [k2]
                    m3 = MK[:, t, :].rearrange("p (h d) -> p h d", h=4)
                    tok["mk", t] = q.op("pool", [k2], lambda e, m3=m3, r=r: e.tensor_tensor(
                        m3, m3, r.unsqueeze(2).to_broadcast([P, 4, P]), ALU.mult))
                    yield
                tok["mk"] = [tok["mk", 0], tok["mk", 1]]

            sS_free, pS_free, pT_free, qkT_free = [after], [after], [after], [after]
            norm_task = normed(X, x_ready, C["mix"], None, XH, XL, xt_tok, xt_free[0])
            next(norm_task)
            tasks.append(norm_task)
            banks, k = group("mkv", 512, YH, YL, lambda kc: yt_tok[kc])
            begin(mem_k(banks, k))
            tasks.append(tables())
            banks, k = group("mkv", 512, YH, YL, lambda kc: yt_tok[kc])
            yt_free[0] = [k]
            plain_evac(MV, banks, k, 512, "mv")
            finish(norm_task)

            xr = lambda kc: xt_tok[kc]

            def latent(Z, w, n, key, first, gain):
                ks = []
                for t in (0, 1):
                    ss = col()
                    k = q.op("act", [tok[key, t]] + sS_free[0], lambda e, t=t, ss=ss: e.activation(
                        sS[:, 0:w], Z[:, t, 0:w], ACT.Square, accum_out=ss))
                    sS_free[0] = [k]
                    r, k = rstd(ss, w, [k])
                    ks.append([q.op("dve", [k], lambda e, t=t, r=r: e.tensor_scalar(
                        Z[:, t, 0:w], Z[:, t, 0:w], r, None, ALU.mult))])
                yield
                for j in range(0, n, 2):
                    bank = take("aux")
                    m = min(2, n - j)
                    for i in range(m):
                        for t in (0, 1):
                            o = ps[:, bank, i * 256 + t * P:i * 256 + t * P + P]
                            k = q.op("pe", ks[t] + (bank_free[bank] if i == 0 and t == 0 else []),
                                     lambda e, o=o, t=t, i=i: e.transpose(
                                         o, Z[:, t, (j + i) * P:(j + i) * P + P], ident[:, :]))
                    s = nt[0] % 2
                    nt[0] += 1
                    for i in range(m):
                        a = q.op("act", [k] + tmp_free[s], lambda e, i=i: e.activation(
                            tmpT[:, s, i * 256:i * 256 + 256], ps[:, bank, i * 256:i * 256 + 256], ACT.Copy,
                            scale=gain[:, j + i:j + i + 1]))
                    give(bank, [a])
                    f = first + j
                    src = tmpT[:, s, 0:m * 256].rearrange("p (c n) -> p c n", c=m)
                    ab = split_from(src, CH[:, f:f + m, :], CL[:, f:f + m, :], [a], after, on="dve")
                    tmp_free[s] = ab
                    for i in range(m):
                        tok["c", f + i] = ab
                    yield


            banks, k = group("cq", 384, XH, XL, xr)
            plain_evac(ZQ, banks, k, 384, "zq")
            tasks.append(latent(ZQ, 384, 3, "zq", 0, C["cqn"]))
            banks, k = group("ckv", 288, XH, XL, xr)
            plain_evac(ZK, banks, k, 288, "zk")
            tasks.append(latent(ZK, 256, 2, "zk", 3, C["ckvn"]))
            banks, k = group("qm", 512, XH, XL, xr)
            plain_evac(QM, banks, k, 512, "qmr")

            def turned(src, srctok, hi, lo, key):
                where = 0 if key in ("ya", "yb") else 4
                d = {}
                yield from transposed([src[:, 0, :], src[:, 1, :]], srctok, 4, hi, lo, d, yfree[where],
                                      kind="aux", first=where)
                for kc, v in d.items():
                    tok[key, kc - where] = v

            yfree = {0: yt_free[0], 4: yt_free[0]}

            def mem_attention():
                for t in (0, 1):
                    k = tok["qmr", t]
                    r, k2 = head_stats(QM[:, t, :], 4, 128, [k] + pS_free[0], pS[:, :])
                    pS_free[0] = [("s_dve", q.count["s_dve"])]
                    m3 = QM[:, t, :].rearrange("p (h d) -> p h d", h=4)
                    tok["qm", t] = q.op("pool", [k2], lambda e, m3=m3, r=r: e.tensor_tensor(
                        m3, m3, r.unsqueeze(2).to_broadcast([P, 4, P]), ALU.mult))
                    yield
                SC = 128.0 ** -0.5
                for h in range(4):
                    hs = slice(h * P, h * P + P)
                    b1 = take("aux")
                    for i, (src, key) in enumerate(((QM, "qm"), (MK, "mk"))):
                        for t in (0, 1):
                            k = q.op("pe", [tok[key, t]] + (bank_free[b1] if i + t == 0 else []),
                                     lambda e, i=i, t=t, src=src: e.transpose(
                                         ps[:, b1, i * 256 + t * P:i * 256 + t * P + P], src[:, t, hs], ident[:, :]))
                    a = q.op("act", [k] + qkT_free[0], lambda e: e.activation(
                        qkT[:, 0:256], ps[:, b1, 0:256], ACT.Copy, scale=C["mqn"]))
                    a = q.op("act", [k] + qkT_free[0], lambda e: e.activation(
                        qkT[:, 256:512], ps[:, b1, 256:512], ACT.Copy, scale=C["mkn"]))
                    give(b1, [a])
                    yield
                    b2 = take("aux")
                    for t in (0, 1):
                        k = q.op("pe", [a] + (bank_free[b2] if t == 0 else []), lambda e, t=t: e.matmul(
                            ps[:, b2, t * 256:t * 256 + 256], qkT[:, t * P:t * P + P], qkT[:, 256:512],
                            start=True, stop=True))
                    qkT_free[0] = [k]
                    mx, nm, rs, ri = col(2), col(2), col(2), col(2)
                    d = q.op("dve", [k], lambda e: e.tensor_reduce(
                        mx, ps[:, b2, :].rearrange("p (t k) -> p t k", t=2), AX.X, ALU.max))
                    d = q.op("dve", [d], lambda e: e.tensor_scalar(nm, mx, -SC, None, ALU.mult))
                    for t in (0, 1):
                        a = q.op("act", [d] + pS_free[0], lambda e, t=t: e.activation(
                            pS[:, t * 256:t * 256 + 256], ps[:, b2, t * 256:t * 256 + 256], ACT.Exp,
                            bias=nm[:, t:t + 1], scale=SC, accum_out=rs[:, t:t + 1]))
                    give(b2, [a])
                    rk = q.op("dve", [a], lambda e: e.reciprocal(ri, rs))
                    yield
                    b3 = take("aux")
                    for j in range(4):
                        k = q.op("pe", [a] + (bank_free[b3] if j == 0 else []), lambda e, j=j: e.transpose(
                            ps[:, b3, j * P:j * P + P], pS[:, j * P:j * P + P], ident[:, :]))
                    pS_free[0] = [k]
                    a = q.op("act", [k] + pT_free[0], lambda e: e.activation(pT[:, :], ps[:, b3, :], ACT.Copy))
                    give(b3, [a])
                    yield
                    b4 = take("aux")
                    for t in (0, 1):
                        for kt in (0, 1):
                            k = q.op("pe", [a, tok["mv", 0], tok["mv", 1]] + (bank_free[b4] if t + kt == 0 else []),
                                     lambda e, t=t, kt=kt: e.matmul(
                                         ps[:, b4, t * P:t * P + P], pT[:, (2 * t + kt) * P:(2 * t + kt) * P + P],
                                         MV[:, kt, hs], start=kt == 0, stop=kt == 1))
                    pT_free[0] = [k]
                    for t in (0, 1):
                        d = q.op("dve", [k, rk], lambda e, t=t: e.tensor_scalar(
                            QM[:, t, hs], ps[:, b4, t * P:t * P + P], ri[:, t:t + 1], None, ALU.mult))
                        tok["yc", "src", t] = d
                    give(b4, [d])
                    yield
                yield from turned(QM, [[tok["yc", "src", 0]], [tok["yc", "src", 1]]], YH, YL, "yc")

            def spatial_v(banks, k0):
                sms = (col(), col())
                plain_evac(V, banks, k0, 512, "vr", ACT.Gelu, sms)
                yield
                for t in (0, 1):
                    sm, mu, ss = sms[t], col(), col()
                    k = tok["vr", t]
                    k = q.op("dve", [k], lambda e, sm=sm, mu=mu: e.tensor_scalar(mu, sm, 1.0 / 512, None, ALU.mult))
                    k = q.op("dve", [k], lambda e, t=t, mu=mu: e.tensor_scalar(
                        V[:, t, :], V[:, t, :], mu, None, ALU.subtract))
                    a = q.op("act", [k] + sS_free[0], lambda e, t=t, ss=ss: e.activation(
                        sS[:, :], V[:, t, :], ACT.Square, accum_out=ss))
                    sS_free[0] = [a]
                    r, k = rstd(ss, 512, [a])
                    k = q.op("dve", [k, s_in], lambda e, t=t, r=r: e.scalar_tensor_tensor(
                        out=V[:, t, :], in0=V[:, t, :], scalar=r, in1=gates[:, 0, 0:512],
                        op0=ALU.mult, op1=ALU.mult))
                    tok["v", t] = q.op("pool", [k, s_in], lambda e, t=t: e.tensor_tensor(
                        V[:, t, :], V[:, t, :], gates[:, 0, 512:1024], ALU.add))
                    yield

            def spatial_u(banks, k0):
                plain_evac(U, banks, k0, 512, "u", ACT.Gelu)
                yield
                for t in (0, 1):
                    b = take("aux")
                    for g in range(8):
                        k = q.op("pe", [sgw_tok, tok["v", t]] + (bank_free[b] if g == 0 else []),
                                 lambda e, t=t, g=g: e.matmul(ps[:, b, g * 64:g * 64 + 64], sgw[:, g, :],
                                                              V[:, t, g * 64:g * 64 + 64], start=True, stop=True))
                    v3 = V[:, t, :].rearrange("p (g d) -> p g d", g=8)
                    p3 = ps[:, b, :].rearrange("p (g d) -> p g d", g=8)
                    d = q.op("dve", [k], lambda e, v3=v3, p3=p3: e.tensor_tensor(
                        v3, p3, C["sgb"].unsqueeze(2).to_broadcast([P, 8, 64]), ALU.add))
                    give(b, [d])
                    tok["ya", "src", t] = q.op("pool", [d, tok["u", t]], lambda e, t=t: e.tensor_tensor(
                        U[:, t, :], U[:, t, :], V[:, t, :], ALU.mult))
                    yield
                yield from turned(U, [[tok["ya", "src", 0]], [tok["ya", "src", 1]]], YH, YL, "ya")
                tok["u_free"] = [("s_pe", q.count["s_pe"])]

            mem_task = mem_attention()
            while ("mk" not in tok) or ("mv", 1) not in tok:
                step_tasks()
            tasks.append(mem_task)
            banks, k = group("v", 512, XH, XL, xr)
            v_task = spatial_v(banks, k)
            begin(v_task, True)
            banks, k = group("u", 512, XH, XL, xr)
            finish(v_task)
            u_task = spatial_u(banks, k)
            begin(u_task, True)

            def cready(kc):
                while ("c", kc) not in tok:
                    step_tasks()
                return tok["c", kc]

            def rotated(T, t, gain, waits):
                r, k = head_stats(T[:, t, :], 8, 96, waits + hn_free[t], hn[:, t, 0:768])
                t3 = T[:, t, :].rearrange("p (h d) -> p h d", h=8)
                k = q.op("dve", [k], lambda e: e.tensor_tensor(
                    t3, t3, r.unsqueeze(2).to_broadcast([P, 8, 96]), ALU.mult))
                k = q.op("dve", [k, b_in], lambda e: e.tensor_tensor(
                    t3, t3, gqk[:, gain, :].unsqueeze(1).to_broadcast([P, 8, 96]), ALU.mult))
                x1, x2 = t3[:, :, 64:80], t3[:, :, 80:96]
                h4 = hn[:, t, 0:512].rearrange("p (a h d) -> p a h d", a=4, h=8)
                cs = rp[:, t, 8, :].unsqueeze(1).to_broadcast([P, 8, 16])
                sn = rp[:, t, 9, :].unsqueeze(1).to_broadcast([P, 8, 16])
                m = [q.op("pool", [k, *tok["rope"]], lambda e, i=i, a=a, b=b: e.tensor_tensor(
                    h4[:, i], a, b, ALU.mult))
                    for i, (a, b) in enumerate(((x1, cs), (x2, sn), (x2, cs), (x1, sn)))]
                q.op("pool", m, lambda e: e.tensor_tensor(x1, h4[:, 0], h4[:, 1], ALU.subtract))
                k = q.op("pool", m, lambda e: e.tensor_tensor(x2, h4[:, 2], h4[:, 3], ALU.add))
                hn_free[t] = [k]
                return k

            def mla_q(banks, k0):
                for t in (0, 1):
                    for j in (0, 1):
                        b = banks[j][t]
                        k = q.op("act", [k0] + after, lambda e, t=t, j=j, b=b: e.activation(
                            QT[:, t, j * 384:j * 384 + 384], ps[:, b, 0:384], ACT.Copy))
                        give(b, [k])
                    tok["qr", t] = k
                yield
                for t in (0, 1):
                    tok["q", t] = rotated(QT, t, 0, [tok["qr", t]])
                    yield

            def mla_kv(banks, k0):
                for t in (0, 1):
                    k3 = KT[:, t, :].rearrange("p (h d) -> p h d", h=8)
                    for j in (0, 1):
                        b = banks[j][t]
                        p3 = ps[:, b, :].rearrange("p (h d) -> p h d", h=4)
                        v3 = VT[:, t, j * 256:j * 256 + 256].rearrange("p (h d) -> p h d", h=4)
                        k = q.op("act", [k0] + after, lambda e, k3=k3, p3=p3, j=j: e.activation(
                            k3[:, 4 * j:4 * j + 4, 0:64], p3[:, :, 0:64], ACT.Copy))
                        k = q.op("act", [k0], lambda e, v3=v3, p3=p3: e.activation(v3, p3[:, :, 64:128], ACT.Copy))
                        give(b, [k])
                    k2 = q.op("pool", [tok["zk", t]] + after, lambda e, t=t, k3=k3: e.tensor_copy(
                        k3[:, :, 64:96], ZK[:, t, 256:288].unsqueeze(1).to_broadcast([P, 8, 32])))
                    tok["vt", t] = k
                    tok["kr", t] = [k, k2]
                yield
                for t in (0, 1):
                    tok["k", t] = rotated(KT, t, 1, tok["kr", t])
                    yield

            banks, k = wide("uq", 3, 384, CH, CL, cready)
            q_task = mla_q(banks, k)
            begin(q_task)
            banks, k = wide("ukv", 2, 512, CH[:, 3:5, :], CL[:, 3:5, :], lambda kc: cready(kc + 3))
            kv_task = mla_kv(banks, k)
            begin(kv_task)

            def attention():
                SC = 96.0 ** -0.5
                while mem_task in tasks or u_task in tasks:
                    yield
                for h in range(8):
                    hs = slice(h * 96, h * 96 + 96)
                    b1 = take("aux")
                    for i, (src, key) in enumerate(((QT, "q"), (KT, "k"))):
                        for t in (0, 1):
                            k = q.op("pe", [tok[key, t]] + (bank_free[b1] if i + t == 0 else []),
                                     lambda e, i=i, t=t, src=src: e.transpose(
                                         ps[0:96, b1, i * 256 + t * P:i * 256 + t * P + P], src[:, t, hs],
                                         ident[:, :]))
                    a = q.op("act", [k] + qkT_free[0], lambda e: e.activation(
                        qkT[0:96, :], ps[0:96, b1, :], ACT.Copy))
                    give(b1, [a])
                    yield
                    b2 = take("aux")
                    for t in (0, 1):
                        n = P * (t + 1)
                        k = q.op("pe", [a] + (bank_free[b2] if t == 0 else []), lambda e, t=t, n=n: e.matmul(
                            ps[:, b2, t * P:t * P + n], qkT[0:96, t * P:t * P + P], qkT[0:96, 256:256 + n],
                            start=True, stop=True))
                    qkT_free[0] = [k]
                    mx, nm, rs, ri = col(2), col(2), col(2), col(2)
                    s = q.op("dve", [k, mask_tok] + sS_free[0], lambda e: e.scalar_tensor_tensor(
                        out=sS[:, 0:384], in0=ps[:, b2, 0:384], scalar=SC, in1=mask[:, :],
                        op0=ALU.mult, op1=ALU.add))
                    give(b2, [s])
                    q.op("dve", [s], lambda e: e.tensor_reduce(mx[:, 0:1], sS[:, 0:P], AX.X, ALU.max))
                    d = q.op("dve", [s], lambda e: e.tensor_reduce(mx[:, 1:2], sS[:, P:384], AX.X, ALU.max))
                    d = q.op("dve", [d], lambda e: e.tensor_scalar(nm, mx, -1.0, None, ALU.mult))
                    for t in (0, 1):
                        sl = slice(t * P, t * P + P * (t + 1))
                        a = q.op("act", [d] + pS_free[0], lambda e, t=t, sl=sl: e.activation(
                            pS[:, sl], sS[:, sl], ACT.Exp, bias=nm[:, t:t + 1], accum_out=rs[:, t:t + 1]))
                    sS_free[0] = [a]
                    rk = q.op("dve", [a], lambda e: e.reciprocal(ri, rs))
                    yield
                    b3 = take("aux")
                    for j in range(3):
                        k = q.op("pe", [a] + (bank_free[b3] if j == 0 else []), lambda e, j=j: e.transpose(
                            ps[:, b3, j * P:j * P + P], pS[:, j * P:j * P + P], ident[:, :]))
                    pS_free[0] = [k]
                    a = q.op("act", [k] + pT_free[0], lambda e: e.activation(
                        pT[:, 0:384], ps[:, b3, 0:384], ACT.Copy))
                    give(b3, [a])
                    yield
                    b4 = take("aux")
                    vs = slice(h * 64, h * 64 + 64)
                    for n, (t, kt, j) in enumerate(((0, 0, 0), (1, 0, 1), (1, 1, 2))):
                        k = q.op("pe", [a, tok["vt", 0], tok["vt", 1]] + (bank_free[b4] if n == 0 else []),
                                 lambda e, t=t, kt=kt, j=j: e.matmul(
                                     ps[:, b4, t * 64:t * 64 + 64], pT[:, j * P:j * P + P], VT[:, kt, vs],
                                     start=kt == 0, stop=kt == t))
                    pT_free[0] = [k]
                    for t in (0, 1):
                        d = q.op("dve", [k, rk] + tok["u_free"], lambda e, t=t: e.tensor_scalar(
                            U[:, t, vs], ps[:, b4, t * 64:t * 64 + 64], ri[:, t:t + 1], None, ALU.mult))
                        tok["yb", "src", t] = d
                    give(b4, [d])
                    yield
                yield from turned(U, [[tok["yb", "src", 0]], [tok["yb", "src", 1]]], YH, YL, "yb")

            while ("k", 1) not in tok or ("q", 1) not in tok:
                if q_task not in tasks and kv_task not in tasks:
                    break
                if u_task in tasks and tasks.index(u_task) < 2:
                    step_tasks()
                    continue
                finish(q_task)
                finish(kv_task)
            at_task = attention()
            tasks.append(at_task)

            merged_tok = {}
            gates_free = [[tok["v", 0], tok["v", 1]]]
            bg_free = [after]
            for n, br in enumerate("acb"):
                bg = q.dma("s_bg", bg_free[0], bgate[:, :], A["b_gate"]["acb".index(br):"acb".index(br) + 1, :]
                           .to_broadcast([P, D]))
                for j in (0, 1):
                    banks, k = group("g" + br, 512, XH, XL, xr)
                    for t in (0, 1):
                        b = banks[t]
                        g = gates[:, t, j * 512:j * 512 + 512]
                        d = q.op("dve", [k, bg] + gates_free[0], lambda e, b=b, g=g, j=j: e.tensor_tensor(
                            g, ps[:, b, :], bgate[:, j * 512:j * 512 + 512], ALU.add))
                        give(b, [d])
                        tok["gate", t, j] = q.op("act", [d], lambda e, g=g: e.activation(g, g, ACT.Sigmoid))
                bg_free[0] = [d]
                if br == "b":
                    xt_free[0] = [k]
                where = 4 if br == "c" else 0
                key = "y" + br

                def yready(kc, key=key):
                    while (key, kc) not in tok:
                        step_tasks()
                    return tok[key, kc]

                banks, k = wide("br" + br, 4, 512, YH[:, where:where + 4, :], YL[:, where:where + 4, :], yready)
                yfree[where] = [k]
                ends = []
                for j in (0, 1):
                    for t in (0, 1):
                        b = banks[j][t]
                        g = gates[:, t, j * 512:j * 512 + 512]
                        m = hn[:, t, j * 512:j * 512 + 512]
                        if n == 0:
                            d = q.op("dve", [k, tok["gate", t, j]] + hn_free[t], lambda e, b=b, g=g, m=m: e.tensor_tensor(
                                m, ps[:, b, :], g, ALU.mult))
                            give(b, [d])
                            e2 = d
                        else:
                            d = q.op("dve", [k, tok["gate", t, j]], lambda e, b=b, g=g: e.tensor_tensor(
                                g, ps[:, b, :], g, ALU.mult))
                            give(b, [d])
                            e2 = q.op("dve", [d, merged_tok[t, j]], lambda e, g=g, m=m: e.tensor_tensor(
                                m, m, g, ALU.add))
                        merged_tok[t, j] = e2
                        ends.append(e2)
                gates_free[0] = ends
            while tasks:
                step_tasks()
            mt = [[merged_tok[t, 0], merged_tok[t, 1]] for t in (0, 1)]
            finish(transposed([hn[:, 0, :], hn[:, 1, :]], mt, 8, XH, XL, xt_tok, xt_free[0]))
            hn_free = {t: [("s_pe", q.count["s_pe"])] for t in (0, 1)}
            banks, k = wide("wo", 8, 512, XH, XL, xr)
            xt_free[0] = [k]
            add_residual(banks, k, "plain")
            finish(normed(X, x_ready, C["ffn2"], None, XH, XL, xt_tok, xt_free[0]))
            ffn_free[0] = [("s_" + e, q.count["s_" + e]) for e in ("pe", "act", "dve", "pool")]

            ffn("f2", "half")

            ab_ready[0] = [c_in, mod_tok["a1"], mod_tok["b1"]]
            finish(normed(X, x_ready, mod["a1"], mod["b1"], XH, XL, xt_tok, xt_free[0]))
            after = [("s_" + e, q.count["s_" + e]) for e in ("pe", "act", "dve", "pool")]
            xr = lambda kc: xt_tok[kc]
            ct_free = {0: after, 1: after}
            gc_free, uu_free, gb_free = [after], [after], [after]
            tk = {}

            def conv_half(i, ut, gt):
                for j in (0, 1):
                    b1 = take("aux")
                    for c2 in (0, 1):
                        for t in (0, 1):
                            k = q.op("pe", ut[t] + (bank_free[b1] if c2 + t == 0 else []),
                                     lambda e, c2=c2, t=t: e.transpose(
                                         ps[:, b1, c2 * 256 + t * P:c2 * 256 + t * P + P],
                                         UU[:, t, (2 * j + c2) * P:(2 * j + c2) * P + P], ident[:, :]))
                    s = j
                    ta = q.op("act", [k] + ct_free[s], lambda e: e.activation(uT[:, s, :], ps[:, b1, :], ACT.Copy))
                    give(b1, [ta])
                    b2 = take("aux")
                    for c2 in (0, 1):
                        for t in (0, 1):
                            k = q.op("pe", gt[t] + (bank_free[b2] if c2 + t == 0 else []),
                                     lambda e, c2=c2, t=t: e.transpose(
                                         ps[:, b2, c2 * 256 + t * P:c2 * 256 + t * P + P],
                                         GB[:, t, (2 * j + c2) * P:(2 * j + c2) * P + P], ident[:, :]))
                    yield
                    for c2 in (0, 1):
                        ch = 4 * i + 2 * j + c2
                        u3 = uT[:, s, c2 * 256:c2 * 256 + 256].rearrange("p (r n) -> p r n", r=4)
                        c3 = cT[:, s, c2 * 256:c2 * 256 + 256].rearrange("p (r n) -> p r n", r=4)
                        w = [C["cw"][:, n * 8 + ch:n * 8 + ch + 1] for n in range(3)]
                        d = q.op("dve", [ta] + ct_free[s], lambda e, u3=u3, c3=c3, w=w: e.tensor_scalar(
                            c3, u3, w[1], None, ALU.mult))
                        d = q.op("dve", [d], lambda e, u3=u3, c3=c3, w=w: e.scalar_tensor_tensor(
                            out=c3[:, :, 1:64], in0=u3[:, :, 0:63], scalar=w[0], in1=c3[:, :, 1:64],
                            op0=ALU.mult, op1=ALU.add))
                        d = q.op("dve", [d], lambda e, u3=u3, c3=c3, w=w: e.scalar_tensor_tensor(
                            out=c3[:, :, 0:63], in0=u3[:, :, 1:64], scalar=w[2], in1=c3[:, :, 0:63],
                            op0=ALU.mult, op1=ALU.add))
                        tk[c2] = d
                    d = q.op("dve", [tk[0], tk[1], k], lambda e: e.tensor_tensor(
                        cT[:, s, :], ps[:, b2, :], cT[:, s, :], ALU.mult))
                    give(b2, [d])
                    ch = 4 * i + 2 * j
                    ab = split_from(cT[:, s, :].rearrange("p (c n) -> p c n", c=2), YH[:, ch:ch + 2, :],
                                    YL[:, ch:ch + 2, :], [d], yfree[0] + yfree[4])
                    ct_free[s] = ab
                    tk["y", ch] = tk["y", ch + 1] = ab
                    yield
                uu_free[0] = gb_free[0] = [("s_pe", q.count["s_pe"])]

            for i in (0, 1):
                banks, k = group(f"cc{i}", 512, XH, XL, xr)
                gcs = []
                for t in (0, 1):
                    b = banks[t]
                    a = q.op("act", [k] + gc_free[0], lambda e, t=t, b=b: e.activation(
                        GC[:, t, :], ps[:, b, :], ACT.Copy))
                    give(b, [a])
                    gcs.append(a)
                banks, k = group(f"hv{i}", 512, XH, XL, xr)
                while tasks:
                    step_tasks()
                ut, gt = [], []
                for t in (0, 1):
                    b = banks[t]
                    d = q.op("dve", [k, gcs[t]] + uu_free[0], lambda e, t=t, b=b: e.tensor_tensor(
                        UU[:, t, :], GC[:, t, :], ps[:, b, :], ALU.mult))
                    give(b, [d])
                    ut.append([d])
                gc_free[0] = ut[0] + ut[1]
                banks, k = group(f"gb{i}", 512, XH, XL, xr)
                for t in (0, 1):
                    b = banks[t]
                    a = q.op("act", [k] + gb_free[0], lambda e, t=t, b=b: e.activation(
                        GB[:, t, :], ps[:, b, :], ACT.Copy))
                    give(b, [a])
                    gt.append([a])
                tasks.append(conv_half(i, ut, gt))
            xt_free[0] = [k]

            def vready(kc):
                while ("y", kc) not in tk:
                    step_tasks()
                return tk["y", kc]

            banks, k = wide("co", 8, 512, YH, YL, vready)
            add_residual(banks, k, 0)
            for t in (0, 1):
                x_ready[t] = hn_free[t]
            ffn_free[0] = [("s_" + e, q.count["s_" + e]) for e in ("pe", "act", "dve", "pool")]
            ab_ready[0] = [c_in, mod_tok["a2"], mod_tok["b2"]]
            finish(normed(X, x_ready, mod["a2"], mod["b2"], XH, XL, xt_tok, xt_free[0]))

            f_in = q.dma("s_fin", ffn_free[0], FG[:, :], A["final_g"][0:1, :].to_broadcast([P, D]))
            ffn("f3", 1)
            for t in (0, 1):
                ss = col()
                k = q.op("act", hn_free[t], lambda e, t=t, ss=ss: e.activation(
                    hn[:, t, :], X[:, t, :], ACT.Square, accum_out=ss))
                r, k = rstd(ss, D, [k])
                k = q.op("dve", [k, f_in], lambda e, t=t, r=r: e.scalar_tensor_tensor(
                    out=hn[:, t, :], in0=X[:, t, :], scalar=r, in1=FG[:, :], op0=ALU.mult, op1=ALU.mult))
                done = q.dma("s_out", [k], out[t], hn[:, t, :])
            q.wait("sp", [done])

        block = ctx.enter_context(nc.Block())

        @block.sync
        def _(eng):
            schedule(Queues(sems, "sp", eng))

        @block.scalar
        def _(eng):
            schedule(Queues(sems, "act", eng))

        @block.vector
        def _(eng):
            schedule(Queues(sems, "dve", eng))

        @block.gpsimd
        def _(eng):
            schedule(Queues(sems, "pool", eng))

        @block.tensor
        def _(eng):
            schedule(Queues(sems, "pe", eng))


COLS = (("c", 8), ("ffn1", 8), ("mix", 8), ("ffn2", 8), ("mem_norm", 8), ("norm1", 8), ("norm2", 8),
        ("cqn", 3), ("ckvn", 2), ("mqn", 1), ("mkn", 1), ("sgb", 8), ("cw", 24),
        ("ab_sh1", 8), ("ab_sc1", 8), ("ab_sh2", 8), ("ab_sc2", 8))


def layout(i):
    f = lambda a: np.asarray(a)

    def chunks(w):
        return f(w).reshape(-1, P, w.shape[-1])

    def narrow(w, per=2):
        k = chunks(w)
        n = k.shape[0] // per
        return np.ascontiguousarray(k.reshape(n, per, P, -1).transpose(0, 2, 1, 3).reshape(n, P, -1))

    def cc(v):
        return f(v).reshape(-1, P).T

    def up(w):
        g, u = w[:, :FF].reshape(D, 11, 256), w[:, FF:].reshape(D, 11, 256)
        both = np.stack([g, u], 2).reshape(D, 11, 512)
        return np.concatenate([narrow(both[:, j]) for j in range(11)], 0)

    a = {}
    a["x"] = f(i["x"])[0].reshape(2, P, D)
    a["mem"] = f(i["mem"])[0].reshape(2, P, D)
    a["f1_up"], a["f1_dn"] = up(f(i["ffn1_w_gu"])[0]), chunks(f(i["ffn1_w_down"])[0])
    a["f2_up"], a["f2_dn"] = up(f(i["ffn2_w_gu"])[0]), chunks(f(i["ffn2_w_down"])[0])
    a["f3_up"], a["f3_dn"] = up(f(i["ffn_w_in_2"])[0]), chunks(f(i["ffn_w_out_2"])[0])
    kv = f(i["mem_w_kv"])[0]
    a["mkv"] = np.concatenate([narrow(kv[:, :512]), narrow(kv[:, 512:])], 0)
    w = f(i["w_in"])[0]
    for nm, lo, hi in (("u", 0, 512), ("v", 512, 1024), ("cq", 1024, 1408), ("ckv", 1408, 1696), ("qm", 1696, 2208)):
        a[nm] = narrow(w[:, lo:hi])
    for nm, n in (("ga", 0), ("gb_", 1), ("gc", 2)):
        o = 2208 + n * D
        a[nm.rstrip("_")] = np.concatenate([narrow(w[:, o:o + 512]), narrow(w[:, o + 512:o + 1024])], 0)
    a["uq"] = chunks(f(i["mla_w_uq"])[0])
    a["ukv"] = chunks(f(i["mla_w_ukv"])[0])
    for b in "abc":
        a["br" + b] = chunks(f(i["w_branch_" + b])[0])
    a["wo"] = chunks(f(i["w_out"])[0])
    ci = f(i["conv_w_in_2"])[0]
    for n in (0, 1):
        for nm, o in (("gb", 0), ("cc", D), ("hv", 2 * D)):
            a[f"{nm}{n}"] = narrow(ci[:, o + 512 * n:o + 512 * n + 512])
    a["co"] = chunks(f(i["conv_w_out_2"])[0])
    aw = f(i["ada_w_2"])[0]
    a["ada"] = np.ascontiguousarray(aw.reshape(8, P, 6, D).transpose(2, 0, 1, 3).reshape(48, P, D))
    ab = f(i["ada_b_2"])[0].reshape(6, D)
    parts = {
        "c": cc(i["c_2"]), "ffn1": cc(i["ffn1_norm"]), "mix": cc(i["mix_norm"]), "ffn2": cc(i["ffn2_norm"]),
        "mem_norm": cc(i["mem_norm"]), "norm1": cc(i["norm1_g_2"]), "norm2": cc(i["norm2_g_2"]),
        "cqn": cc(i["mla_cq_norm"]), "ckvn": cc(i["mla_ckv_norm"]), "mqn": cc(i["mem_q_norm"]),
        "mkn": cc(i["mem_k_norm"]), "sgb": f(i["sg_b"])[0].T,
        "cw": np.concatenate([cc(f(i["conv_w_2"])[0, n]) for n in range(3)], 1),
        "ab_sh1": cc(ab[0]), "ab_sc1": cc(ab[1]), "ab_sh2": cc(ab[3]), "ab_sc2": cc(ab[4]),
    }
    a["cols"] = np.concatenate([parts[k] for k, _ in COLS], 1)
    a["adab_g"] = ab[[2, 5]]
    a["mla_q_norm"], a["mla_k_norm"] = f(i["mla_q_norm"]), f(i["mla_k_norm"])
    a["positions"] = f(i["positions"])[0].reshape(2, P).T
    a["inv"] = (10000.0 ** (-np.arange(16, dtype=np.float64) / 16)).astype(np.float32)[None]
    a["sg_ln_g"], a["sg_ln_b"] = f(i["sg_ln_g"]), f(i["sg_ln_b"])
    a["sg_wT"] = f(i["sg_w"])[0].transpose(2, 0, 1)
    a["b_gate"] = f(i["b_gate"])[0].reshape(3, D)[[0, 2, 1]]
    a["final_g"] = f(i["final_g_2"])[None]
    return {k: np.ascontiguousarray(v) for k, v in a.items()}


def kernel(**inputs):
    import concourse.bacc as _bacc
    from concourse.bass_utils import run_bass_kernel_spmd as _run

    nc = _bacc.Bacc("TRN2", target_bir_lowering=False, num_devices=1)
    arrays, args = {}, {}
    for name, a in layout(inputs).items():
        arrays[f"in_{name}"] = a
        args[name] = nc.dram_tensor(f"in_{name}", a.shape, mybir.dt.from_np(a.dtype), kind="ExternalInput").ap()
    out = nc.dram_tensor("out_0", (2, P, D), F32, kind="ExternalOutput").ap()
    build(nc, args, out)
    r = _run(nc, [arrays], core_ids=[0])
    return r.results[0]["out_0"].reshape(1, 2 * P, D)
```

```python
from contextlib import ExitStack

import numpy as np

import concourse.bass as bass
from concourse import mybir

F32 = mybir.dt.float32
F32R = mybir.dt.float32r
I32 = mybir.dt.int32
ALU = mybir.AluOpType
ACT = mybir.ActivationFunctionType
AX = mybir.AxisListType

P = 128
D = 1024
KC = 8
FF = 2816
EPS = 1e-6
NEG = -1e30
RAW = 6
SPL = 4
AHEAD = 3
PI = float(np.pi)


def plan():
    out = []

    def add(name, n, w):
        out.extend((name, i, w * min(2, n - 2 * i), False) for i in range((n + 1) // 2))

    def ffn(tag, terms):
        at = len(out)
        for g in range(11):
            add(f"{tag}_up{g}", 8, 512)
        for j in (0, 1):
            add(f"{tag}_dn{j}", 22, 512)
        units, ada = out[at:], [("ada", i, 1024, True) for t in terms for i in range(8 * t, 8 * t + 8)]
        del out[at:]
        for i, u in enumerate(units):
            out.append(u)
            while ada and i >= 4 and (24 - len(ada)) * 50 < (i - 3) * 24:
                out.append(ada.pop(0))

    ffn("f1", (0, 1, 2))
    for j in (0, 1):
        add(f"mkv{j}", 8, 512)
    add("cq", 8, 384)
    add("ckv", 8, 288)
    add("qm", 8, 512)
    for j in (0, 1):
        add(f"uq{j}", 3, 384)
    for j in (0, 1):
        add(f"ukv{j}", 2, 512)
    add("v", 8, 512)
    add("u", 8, 512)
    for b in "acb":
        for j in (0, 1):
            add(f"g{b}{j}", 8, 512)
        for j in (0, 1):
            add(f"br{b}{j}", 4, 512)
    for j in (0, 1):
        add(f"wo{j}", 8, 512)
    ffn("f2", (3, 4, 5))
    for i in (0, 1):
        for n in ("cc", "hv", "gb"):
            add(f"conv_{n}{i}", 8, 512)
    for j in (0, 1):
        add(f"co{j}", 8, 512)
    ffn("f3", ())
    return out


class Queues:

    def __init__(self, sems, me, eng):
        self.sems, self.me, self.eng = sems, me, eng
        self.count = {name: 0 for name in sems}
        self.made = {}

    def wait(self, e, waits):
        if e == self.me:
            for s, v in waits:
                if self.made.get(s, 0) < v:
                    self.made[s] = v
                    self.eng.wait_ge(self.sems[s], v)

    def op(self, e, waits, fn):
        self.wait(e, waits)
        s = "s_" + e
        self.count[s] += 1
        if e == self.me:
            fn(self.eng).then_inc(self.sems[s], 1)
        return (s, self.count[s])

    def silent(self, e, waits, fn):
        self.wait(e, waits)
        if e == self.me:
            fn(self.eng)

    def dma(self, sem, waits, dst, src, e="sp"):
        self.wait(e, waits)
        self.count[sem] += 16
        if e == self.me:
            self.eng.dma_start(dst, src).then_inc(self.sems[sem], 16)
        return (sem, self.count[sem])


def build(nc, A, out):
    ctx = ExitStack()
    with ctx:
        def sb(name, shape, dt=F32, c=None):
            return (c or ctx).enter_context(nc.sbuf_tensor("t_" + name, shape, dt))

        raw = sb("raw", [P, RAW, 1024])
        wh = sb("wh", [P, SPL, 1024], F32R)
        wl = sb("wl", [P, SPL, 1024], F32R)
        X = sb("X", [P, 2, D])
        XH = sb("XH", [P, KC, 256], F32R)
        XL = sb("XL", [P, KC, 256], F32R)
        YH = sb("YH", [P, KC, 256], F32R)
        YL = sb("YL", [P, KC, 256], F32R)
        hn = sb("hn", [P, 2, D])
        tmpT = sb("tmpT", [P, 2, 512])
        gB = sb("gB", [P, 2, D])
        acc2 = sb("acc2", [P, 2, D])
        ident = sb("ident", [P, P])
        ones = sb("ones", [P, P])
        cols = sb("cols", [P, 192])
        sc = sb("sc", [P, 384])
        rp = sb("rp", [P, 2, 12, 16])
        rpi = sb("rpi", [P, 2, 16], I32)
        posi = sb("posi", [P, 2], I32)
        gqk = sb("gqk", [P, 2, 96])
        with ExitStack() as c:
            FG = sb("FG", [P, D], F32, c)
            HH = sb("HH", [P, 22, 256], F32R, c)
            HL = sb("HL", [P, 22, 256], F32R, c)
            sg = sb("sg", [P, 2, 2, 256], F32, c)
            hp = sb("hp", [P, 2, 2, 256], F32, c)
        with ExitStack() as c:
            gates = sb("gates", [P, 2, D], F32, c)
            bgate = sb("bgate", [P, D], F32, c)
            U = sb("U", [P, 2, 512], F32, c)
            V = sb("V", [P, 2, 512], F32, c)
            ZQ = sb("ZQ", [P, 2, 384], F32, c)
            ZK = sb("ZK", [P, 2, 288], F32, c)
            QM = sb("QM", [P, 2, 512], F32, c)
            MK = sb("MK", [P, 2, 512], F32, c)
            MV = sb("MV", [P, 2, 512], F32, c)
            QT = sb("QT", [P, 2, 768], F32, c)
            KT = sb("KT", [P, 2, 768], F32, c)
            VT = sb("VT", [P, 2, 512], F32, c)
            qkT = sb("qkT", [P, 512], F32, c)
            sS = sb("sS", [P, 512], F32, c)
            pS = sb("pS", [P, 512], F32, c)
            pT = sb("pT", [P, 512], F32, c)
            CH = sb("CH", [P, 5, 256], F32R, c)
            CL = sb("CL", [P, 5, 256], F32R, c)
            sgw = sb("sgw", [P, 8, P], F32, c)
            mask = sb("mask", [P, 384], F32, c)
        with ExitStack() as c:
            GC = sb("GC", [P, 2, 512], F32, c)
            UU = sb("UU", [P, 2, 512], F32, c)
            GB = sb("GB", [P, 2, 512], F32, c)
            uT = sb("uT", [P, 2, 512], F32, c)
            cT = sb("cT", [P, 2, 512], F32, c)
        ps = ctx.enter_context(nc.psum_tensor("ps", [P, 8, 512], F32))
        names = ["s_pe", "s_act", "s_dve", "s_pool", "s_x0", "s_x1", "s_mem", "s_cols", "s_bc", "s_sg", "s_bg", "s_fin", "s_out"]
        sems = {n: ctx.enter_context(nc.semaphore(n)) for n in names + [f"s_raw{i}" for i in range(RAW)]}

        def schedule(q):
            stream = plan()

            used = [0]

            def col(n=1):
                a = used[0]
                used[0] += n
                assert used[0] <= 384
                return sc[:, a:a + n]

            held = set()

            bank_free = {b: [] for b in range(8)}

            def give(b, waits):
                held.discard(b)
                bank_free[b] = waits

            turn = {"main": 0, "aux": 0}

            def take(kind="main"):
                pool = (0, 1, 2, 3) if kind == "main" else (4, 5, 6, 7)
                for _ in pool:
                    b = pool[turn[kind] % len(pool)]
                    turn[kind] += 1
                    if b not in held:
                        held.add(b)
                        return b
                raise AssertionError("no bank is free")

            raw_free = {}
            raw_in = {}
            split_of = {}
            spl_free = {}
            state = {"dma": 0, "spl": 0, "use": 0, "nspl": 0, "done": 0}
            ada = {"ready": {}, "free": {0: [], 1: []}, "tok": None,
                   "acc": (acc2[:, 0, :], acc2[:, 1, :])}
            tasks = []

            def fetch():
                n = state["dma"]
                if n >= len(stream):
                    return
                name, i, w, _ = stream[n]
                s = n % RAW
                raw_in[n] = q.dma(f"s_raw{s}", raw_free.get(n - RAW, []), raw[:, s, 0:w], A[name][i][:, 0:w])
                state["dma"] = n + 1

            def advance():
                n = state["spl"]
                name, i, w, only_raw = stream[n]
                r = raw[:, n % RAW, 0:w]
                if only_raw:
                    term, k = divmod(i, 8)
                    acc = ada["acc"][term % 2]
                    c = ada["c"][:, k:k + 1]
                    if k == 0:
                        ada["tok"] = q.op("dve", [raw_in[n], ada["c_tok"]] + ada["free"][term % 2],
                                          lambda e: e.tensor_scalar(acc, r, c, None, ALU.mult))
                    else:
                        ada["tok"] = q.op("dve", [raw_in[n], ada["tok"]],
                                          lambda e: e.scalar_tensor_tensor(out=acc, in0=r, scalar=c, in1=acc,
                                                                           op0=ALU.mult, op1=ALU.add))
                    raw_free[n] = [ada["tok"]]
                    if k == 7:
                        tasks.append(ada_reduce(term, ada["tok"]))
                else:
                    m = state["nspl"]
                    s = m % SPL
                    free = spl_free.get(m - SPL, [])
                    hi = q.op("act", [raw_in[n]] + free,
                              lambda e: e.activation(wh[:, s, 0:w], r, ACT.Copy))
                    lo = q.op("dve", [hi] + free,
                              lambda e: e.tensor_tensor(wl[:, s, 0:w], r, wh[:, s, 0:w].bitcast(F32), ALU.subtract))
                    raw_free[n] = [lo]
                    split_of[m] = [hi, lo]
                    state["nspl"] = m + 1
                state["spl"] = n + 1
                fetch()

            names = [u[0] for u in stream if not u[3]]

            def step_tasks(n=1):
                for _ in range(n):
                    for t in list(tasks[:3]):
                        if next(t, "end") == "end":
                            tasks.remove(t)

            def begin(t, first=False):
                next(t)
                tasks.insert(0, t) if first else tasks.append(t)

            def finish(t):
                for _ in t:
                    pass
                if t in tasks:
                    tasks.remove(t)

            def units(name, blocks, lh, ll, ready):
                u = state["use"]
                n = blocks[-1][0] + 1
                assert names[u] == name and names[u + n - 1] == name, (names[u], name)
                while state["nspl"] < min(u + max(n, 1 + AHEAD), len(names)):
                    advance()
                toks = []
                for t in (0, 1):
                    for m, kc, c0, w, banks, start, stop in blocks:
                        s = (u + m) % SPL
                        o = ps[:, banks[t], 0:w]
                        waits = split_of[u + m] + ready(kc) + (bank_free[banks[t]] if start else [])
                        xh, xl = lh[:, kc, t * P:t * P + P], ll[:, kc, t * P:t * P + P]
                        h, l = wh[:, s, c0:c0 + w], wl[:, s, c0:c0 + w]
                        q.silent("pe", waits, lambda e: e.matmul(o, xh, h, start=start, stop=False))
                        q.silent("pe", [], lambda e: e.matmul(o, xh, l, start=False, stop=False))
                        tok = q.op("pe", [], lambda e: e.matmul(o, xl, h, start=False, stop=stop))
                    toks.append(tok)
                for m in range(n):
                    spl_free[u + m] = [tok]
                state["use"] = u + n
                for m in range(n):
                    step_tasks()
                return toks

            def group(name, n, w, lh, ll, ready, last=1):
                banks = (take(), take())
                nu = (n + 1) // 2
                i = 0
                while i < nu:
                    k = last if i == nu - last else 1
                    toks = units(name, [(m, 2 * (i + m) + j, j * w, w, banks, i + m + j == 0,
                                         2 * (i + m) + j == n - 1)
                                        for m in range(k) for j in (0, 1) if 2 * (i + m) + j < n],
                                 lh, ll, ready)
                    i += k
                return banks, toks

            def rstd(ss, n, waits):
                k = ss.shape[-1]
                m, r = col(k), col(k)
                t = q.op("dve", waits, lambda e: e.tensor_scalar(m, ss, 1.0 / n, EPS, ALU.mult, ALU.add))
                t = q.op("pool", [t, c_half], lambda e: e.tensor_tensor(r, m, mhalf[:, 0:k], ALU.pow))
                return r, t

            def split_from(src, hi, lo, waits, free, on="act"):
                if on == "act":
                    a = q.op("act", waits + free, lambda e: e.activation(hi, src, ACT.Copy))
                else:
                    a = q.op("dve", waits + free, lambda e: e.tensor_copy(hi, src))
                b = q.op("dve", [a] + waits + free,
                         lambda e: e.tensor_tensor(lo, src, hi.bitcast(F32), ALU.subtract))
                return [a, b]

            tmp_free = {0: [], 1: []}
            nt = [0]

            def transposed(src, waits, n, hi, lo, tok_of, free, a=None, b=None, first=0):
                for j in range(n // 2):
                    bank = take("aux")
                    for t in (0, 1):
                        for c in (2 * j, 2 * j + 1):
                            o = ps[:, bank, (c % 2) * 256 + t * P:(c % 2) * 256 + t * P + P]
                            tok = q.op("pe", waits(t, j) + c_id + (bank_free[bank] if c % 2 == 0 and t == 0 else []),
                                       lambda e: e.transpose(o, src[t][:, c * P:c * P + P], ident[:, :]))
                    h2, l2 = hi[:, first + 2 * j:first + 2 * j + 2, :], lo[:, first + 2 * j:first + 2 * j + 2, :]
                    if a is None:
                        p2 = ps[:, bank, :].rearrange("p (c n) -> p c n", c=2)
                        ab = split_from(p2, h2, l2, [tok], free)
                        give(bank, [ab[1]])
                    else:
                        s = nt[0] % 2
                        nt[0] += 1
                        for c in (0, 1):
                            k = 2 * j + c
                            bias = 0.0 if b is None else b[:, k:k + 1]
                            m = q.op("act", [tok] + tmp_free[s] + ab_ready[0],
                                     lambda e: e.activation(
                                         tmpT[:, s, c * 256:c * 256 + 256], ps[:, bank, c * 256:c * 256 + 256],
                                         ACT.Identity, bias=bias, scale=a[:, k:k + 1]))
                        give(bank, [m])
                        ab = split_from(tmpT[:, s, :].rearrange("p (c n) -> p c n", c=2), h2, l2, [m], free,
                                        on="dve")
                        tmp_free[s] = ab
                    tok_of[first + 2 * j] = tok_of[first + 2 * j + 1] = ab
                    yield

            ab_ready = [[]]
            xt_tok, yt_tok = {}, {}
            xt_free, yt_free = [[]], [[]]
            hn_free = {0: [], 1: []}
            x_tok = {}
            R, R_tok, half_ss = {}, {}, {}

            def half_done(j, banks, toks, how):
                for t in (0, 1):
                    h = slice(j * 512, j * 512 + 512)
                    o, xs, tmp = ps[:, banks[t], :], X[:, t, h], hn[:, t, h]
                    if how == "half":
                        k = q.op("dve", [toks[t]], lambda e: e.scalar_tensor_tensor(
                            out=xs, in0=o, scalar=0.5, in1=xs, op0=ALU.mult, op1=ALU.add))
                        give(banks[t], [k])
                    elif how == "plain":
                        k = q.op("dve", [toks[t]], lambda e: e.tensor_tensor(xs, o, xs, ALU.add))
                        give(banks[t], [k])
                    else:
                        m = q.op("dve", [toks[t]] + gb_tok[how] + hn_free[t],
                                 lambda e: e.tensor_tensor(tmp, o, gB[:, how, h], ALU.mult))
                        give(banks[t], [m])
                        k = q.op("dve", [m], lambda e: e.tensor_tensor(xs, tmp, xs, ALU.add))
                    x_tok[t, j] = k
                    ss = col()
                    k = q.op("act", [k] + hn_free[t], lambda e: e.activation(tmp, xs, ACT.Square, accum_out=ss))
                    half_ss[t, j] = k
                    m = col()
                    if j == 0:
                        q0 = q.op("dve", [k], lambda e: e.tensor_scalar(m, ss, 1.0 / D, EPS, ALU.mult, ALU.add))
                        half_ss[t] = (m, q0)
                    else:
                        m0, q0 = half_ss[t]
                        r = col()
                        k = q.op("dve", [k, q0], lambda e: e.tensor_scalar(m, ss, 1.0 / D, m0, ALU.mult, ALU.add))
                        R_tok[t] = q.op("pool", [k, c_half], lambda e: e.tensor_tensor(
                            r, m, mhalf[:, 0:1], ALU.pow))
                        R[t] = r

            def product(name, n, lh, ll, ready, how, after_half):
                for j in (0, 1):
                    banks, toks = group(f"{name}{j}", n, 512, lh, ll, ready, last=2 if j else 1)
                    half_done(j, banks, toks, how)
                    after_half(j)
                return toks[1]

            def gained(a, hi, lo, tok_of, free):
                def waits(t, j):
                    return [x_tok[t, j // 2]]
                for k in range(8):
                    tok_of.pop(k, None)
                g = transposed([X[:, 0, :], X[:, 1, :]], waits, 8, hi, lo, tok_of, free, a)
                for _ in range(2):
                    next(g)
                    yield
                while (1, 1) not in x_tok:
                    yield
                yield from g

            def normed(a, b, hi, lo, tok_of, free, pause=0):
                toks = {}
                for t in (0, 1):
                    toks[t] = [q.op("dve", [R_tok[t], half_ss[t, 0], half_ss[t, 1]], lambda e: e.tensor_scalar(
                        hn[:, t, :], X[:, t, :], R[t], None, ALU.mult))]
                yield
                for _ in range(pause):
                    yield
                tok_of.clear()
                yield from transposed([hn[:, 0, :], hn[:, 1, :]], lambda t, j: toks[t], 8, hi, lo, tok_of, free, a, b)
                for t in (0, 1):
                    hn_free[t] = [("s_pe", q.count["s_pe"])]

            x_in = [q.dma(f"s_x{t}", [], X[:, t, :], A["x"][t]) for t in (0, 1)]
            c_in = q.dma("s_cols", [], cols[:, 0:A["cols"].shape[1]], A["cols"])
            for _ in range(RAW):
                fetch()
            for t in (0, 1):
                for j in (0, 1):
                    x_tok[t, j] = x_in[t]
            m_in = [q.dma("s_mem", [], hn[:, t, :], A["mem"][t]) for t in (0, 1)][-1]
            b_in = [q.dma("s_bc", [], gB[:, 0, :], A["adab_g"][0:1, :].to_broadcast([P, D])),
                    q.dma("s_bc", [], gB[:, 1, :], A["adab_g"][1:2, :].to_broadcast([P, D])),
                    q.dma("s_bc", [], gqk[:, 0, :], A["mla_q_norm"][0:1, :].to_broadcast([P, 96])),
                    q.dma("s_bc", [], gqk[:, 1, :], A["mla_k_norm"][0:1, :].to_broadcast([P, 96])),
                    q.dma("s_bc", [], posi[:, :], A["positions"]),
                    q.dma("s_bc", [], rp[:, 0, 0, :], A["inv"][0:1, :].to_broadcast([P, 16])),
                    q.dma("s_bc", [], rp[:, 1, 0, :], A["inv"][0:1, :].to_broadcast([P, 16]))][-1]
            gb_tok = {0: [], 1: []}

            C = {}
            at = 0
            for nm, k in COLS:
                C[nm] = cols[:, at:at + k]
                at += k

            mhalf = sc[:, 0:8]
            used[0] = 8
            c_half = q.op("pool", [], lambda e: e.memset(mhalf, -0.5))
            z = q.op("pool", [], lambda e: e.memset(ident[:, :], 0.0))
            c_id = [q.op("pool", [z], lambda e: e.affine_select(
                out=ident[:, :], in_=ident[:, :], compare_op=ALU.not_equal, fill=1.0, base=0,
                pattern=[[-1, P]], channel_multiplier=1))]
            c_one = q.op("pool", [], lambda e: e.memset(ones[:, :], 1.0))

            ada["c"] = col(8)
            ada["c_tok"] = q.op("act", [c_in], lambda e: e.activation(ada["c"], C["c"], ACT.Silu))
            mod = {k: col(8) for k in ("b1", "a1", "b2", "a2")}
            mod_tok = {}

            def ada_reduce(term, tok):
                acc = ada["acc"][term % 2]
                yield
                if term in (2, 5):
                    g = 0 if term == 2 else 1
                    bk = take("aux"), take("aux")
                    for j in (0, 1):
                        k = q.op("pe", [tok, c_one] + bank_free[bk[j]], lambda e, j=j: e.matmul(
                            ps[:, bk[j], :], ones[:, :], acc[:, j * 512:j * 512 + 512], start=True, stop=True))
                        d = q.op("dve", [k, b_in], lambda e, j=j: e.tensor_tensor(
                            gB[:, g, j * 512:j * 512 + 512], ps[:, bk[j], :], gB[:, g, j * 512:j * 512 + 512], ALU.add))
                        give(bk[j], [d])
                    gb_tok[g] = [d]
                else:
                    bk = take("aux")
                    for c in range(8):
                        k = q.op("pe", [tok, c_one] + (bank_free[bk] if c == 0 else []), lambda e, c=c: e.matmul(
                            ps[:, bk, 2 * c:2 * c + 1], acc[:, c * P:c * P + P], ones[:, 0:1], start=True, stop=True))
                    pv = ps[:, bk, 0:16].rearrange("p (c x) -> p c x", x=2)[:, :, 0]
                    nm, bias = {0: ("b1", "ab_sh1"), 1: ("a1", "ab_sc1"), 3: ("b2", "ab_sh2"), 4: ("a2", "ab_sc2")}[term]
                    d = q.op("dve", [k, c_in], lambda e: e.tensor_tensor(mod[nm], pv, C[bias], ALU.add))
                    give(bk, [d])
                    if nm[0] == "a":
                        g = C["norm1" if nm == "a1" else "norm2"]
                        d = q.op("dve", [d], lambda e: e.scalar_tensor_tensor(
                            out=mod[nm], in0=mod[nm], scalar=1.0, in1=g, op0=ALU.add, op1=ALU.mult))
                    mod_tok[nm] = d
                ada["free"][term % 2] = [("s_pe", q.count["s_pe"])]

            def ffn(tag, how, xh, xl, x_of, defer, after_half):
                hid_tok = {}

                def hidden(g, banks, toks):
                    s = g % 2
                    hs = []
                    for t in (0, 1):
                        sc1 = R[t] if defer else 1.0
                        w = [R_tok[t]] if defer else []
                        a = q.op("act", [toks[t]] + w + sg_free[s], lambda e: e.activation(
                            sg[:, s, t, :], ps[:, banks[t], 0:256], ACT.Silu, scale=sc1))
                        if defer:
                            d = q.op("dve", [a] + w + hp_free[s], lambda e: e.scalar_tensor_tensor(
                                out=hp[:, s, t, :], in0=ps[:, banks[t], 256:512], scalar=R[t], in1=sg[:, s, t, :],
                                op0=ALU.mult, op1=ALU.mult))
                        else:
                            d = q.op("dve", [a] + hp_free[s], lambda e: e.tensor_tensor(
                                hp[:, s, t, :], sg[:, s, t, :], ps[:, banks[t], 256:512], ALU.mult))
                        give(banks[t], [d])
                        hs.append([d])
                    sg_free[s] = hs[0] + hs[1]
                    yield
                    yield from transposed([hp[:, s, 0, :], hp[:, s, 1, :]], lambda t, j: hs[t], 2, HH, HL, hid_tok,
                                          ffn_free[0], first=2 * g)
                    hp_free[s] = [("s_pe", q.count["s_pe"])]

                sg_free = {0: ffn_free[0] + sg_first[0], 1: ffn_free[0] + sg_first[0]}
                hp_free = {0: ffn_free[0], 1: ffn_free[0]}

                def x_ready(kc):
                    while kc not in x_of:
                        step_tasks()
                    return x_of[kc]

                for g in range(11):
                    banks, toks = group(f"{tag}_up{g}", 8, 512, xh, xl, x_ready)
                    begin(hidden(g, banks, toks), True)
                up_done = [toks[1]]

                def ready(kc):
                    while kc not in hid_tok:
                        step_tasks()
                    return hid_tok[kc]

                last = product(f"{tag}_dn", 22, HH, HL, ready, how, after_half)
                return up_done, last

            ffn_free = [[]]
            sg_first = [[]]
            hn_free = {0: [m_in], 1: [m_in]}
            ab_ready[0] = [c_in]

            def first_stats():
                junk = sg[:, :, :, :].rearrange("p a b n -> p (a b n)")
                k = x_in[0]
                for t in (0, 1):
                    ss = col()
                    k = q.op("act", [k, x_in[t]], lambda e: e.activation(junk, X[:, t, :], ACT.Square, accum_out=ss))
                    R[t], R_tok[t] = rstd(ss, D, [k])
                sg_first[0] = [k]

            def mem_norm():
                for _ in range(12):
                    yield
                toks = {}
                k = m_in
                for t in (0, 1):
                    ss = col()
                    k = q.op("act", [m_in, k] + tmp_free[0] + tmp_free[1], lambda e: e.activation(
                        tmpT[:, :, :], hn[:, t, 0:D].rearrange("p (a b) -> p a b", a=2), ACT.Square, accum_out=ss))
                    for s in (0, 1):
                        tmp_free[s] = [k]
                    r, k2 = rstd(ss, D, [k])
                    toks[t] = [q.op("dve", [k2], lambda e: e.tensor_scalar(
                        hn[:, t, :], hn[:, t, :], r, None, ALU.mult))]
                    yield
                yield
                yield from transposed([hn[:, 0, :], hn[:, 1, :]], lambda t, j: toks[t], 8, YH, YL, yt_tok, [],
                                      C["mem_norm"])
                for t in (0, 1):
                    hn_free[t] = [("s_pe", q.count["s_pe"])]

            def drain():
                while tasks:
                    step_tasks()

            x_task = gained(C["ffn1"], XH, XL, xt_tok, [])
            begin(x_task)
            first_stats()
            tasks.append(mem_norm())

            def nothing(j):
                if j == 0:
                    drain()

            up_done, last = ffn("f1", "half", XH, XL, xt_tok, True, nothing)
            xt_free[0] = up_done
            sg_first[0] = []

            after = [last, ("s_dve", q.count["s_dve"]), ("s_act", q.count["s_act"])]

            s_in = [q.dma("s_sg", after, gates[:, 0, 0:512], A["sg_ln_g"][0:1, :].to_broadcast([P, 512])),
                    q.dma("s_sg", after, gates[:, 0, 512:1024], A["sg_ln_b"][0:1, :].to_broadcast([P, 512])),
                    q.dma("s_sg", after, sgw[:, :, :], A["sg_wT"])][-1]
            sgw_tok = q.op("pool", after + [s_in], lambda e: e.affine_select(
                out=sgw[:, :, :], in_=sgw[:, :, :], compare_op=ALU.is_ge, fill=0.0, base=0,
                pattern=[[0, 8], [1, P]], channel_multiplier=-1))
            mk = q.op("pool", after, lambda e: e.memset(mask[:, :], 0.0))
            for o in (0, 256):
                mk = q.op("pool", [mk], lambda e, o=o: e.affine_select(
                    out=mask[:, o:o + P], in_=mask[:, o:o + P], compare_op=ALU.is_ge, fill=NEG, base=0,
                    pattern=[[-1, P]], channel_multiplier=1))
            mask_tok = mk

            def tables():
                rope_tok = []
                for t in (0, 1):
                    R = lambda i, t=t: rp[:, t, i, :]
                    pf = col()
                    k = q.op("dve", [b_in], lambda e: e.tensor_copy(pf, posi[:, t:t + 1]))
                    k = q.op("dve", [k], lambda e: e.tensor_scalar(R(1), R(0), pf, None, ALU.mult))
                    k = q.op("dve", [k], lambda e: e.tensor_scalar(R(2), R(1), 1.0 / (2 * PI), None, ALU.mult))
                    k = q.op("dve", [k], lambda e: e.tensor_copy(rpi[:, t, :], R(2)))
                    k = q.op("dve", [k], lambda e: e.tensor_copy(R(3), rpi[:, t, :]))
                    c1, c2 = 6.28125, float(np.float32(np.round((2 * np.pi - 6.28125) * 2 ** 20) / 2 ** 20))
                    c3 = float(2 * np.pi - 6.28125 - c2)
                    for n, cc in enumerate((c1, c2, c3)):
                        k = q.op("dve", [k], lambda e, n=n, cc=cc: e.scalar_tensor_tensor(
                            out=R(1), in0=R(3), scalar=-cc, in1=R(1), op0=ALU.mult, op1=ALU.add))
                    k = q.op("dve", [k], lambda e: e.tensor_scalar(R(4), R(1), PI, -PI, ALU.min, ALU.max))
                    k = q.op("dve", [k], lambda e: e.tensor_scalar(R(5), R(4), PI / 2, -2 * PI, ALU.is_gt, ALU.mult))
                    k = q.op("dve", [k], lambda e: e.scalar_tensor_tensor(
                        out=R(6), in0=R(4), scalar=PI / 2, in1=R(5), op0=ALU.add, op1=ALU.add))
                    k = q.op("dve", [k], lambda e: e.tensor_scalar(R(7), R(6), PI, -PI, ALU.min, ALU.max))
                    a = q.op("act", [k], lambda e: e.activation(R(8), R(7), ACT.Sin))
                    rope_tok.append(q.op("act", [k], lambda e: e.activation(R(9), R(4), ACT.Sin)))
                    yield
                tok["rope"] = rope_tok

            tok = {}

            def head_stats(src, n, hd, waits, junk):
                s3 = src.rearrange("p (h d) -> p h d", h=n)
                j3 = junk.rearrange("p (h d) -> p h d", h=n)
                ss = col(n)
                k = q.op("dve", waits, lambda e: e.tensor_tensor(j3, s3, s3, ALU.mult))
                k = q.op("dve", [k], lambda e: e.tensor_reduce(ss, j3, AX.X, ALU.add))
                return rstd(ss, hd, [k])

            def plain_evac(dst, banks, k0, w, key, func=None, accum=None):
                for t in (0, 1):
                    b = banks[t]
                    a = {} if accum is None else {"accum_out": accum[t]}
                    k = q.op("act", [k0[t]] + after, lambda e, t=t, b=b, a=a: e.activation(
                        dst[:, t, 0:w], ps[:, b, 0:w], func or ACT.Copy, **a))
                    give(b, [k])
                    tok[key, t] = k

            def mem_k(banks, k0):
                plain_evac(MK, banks, k0, 512, "mkr")
                yield
                for t in (0, 1):
                    k = tok["mkr", t]
                    r, k2 = head_stats(MK[:, t, :], 4, 128, [k] + sS_free[0], sS[:, :])
                    sS_free[0] = [k2]
                    m3 = MK[:, t, :].rearrange("p (h d) -> p h d", h=4)
                    tok["mk", t] = q.op("pool", [k2], lambda e, m3=m3, r=r: e.tensor_tensor(
                        m3, m3, r.unsqueeze(2).to_broadcast([P, 4, P]), ALU.mult))
                    yield
                tok["mk"] = [tok["mk", 0], tok["mk", 1]]

            sS_free, pS_free, pT_free, qkT_free = [after], [after], [after], [after]
            norm_task = normed(C["mix"], None, XH, XL, xt_tok, xt_free[0], 3)
            next(norm_task)
            tasks.append(norm_task)
            banks, k = group("mkv0", 8, 512, YH, YL, lambda kc: yt_tok[kc])
            begin(mem_k(banks, k))
            tasks.append(tables())
            banks, k = group("mkv1", 8, 512, YH, YL, lambda kc: yt_tok[kc])
            yt_free[0] = [k[1]]
            plain_evac(MV, banks, k, 512, "mv")
            finish(norm_task)

            xr = lambda kc: xt_tok[kc]

            def latent(Z, w, n, key, first, gain):
                ks = []
                for t in (0, 1):
                    ss = col()
                    k = q.op("act", [tok[key, t]] + sS_free[0], lambda e, t=t, ss=ss: e.activation(
                        sS[:, 0:w], Z[:, t, 0:w], ACT.Square, accum_out=ss))
                    sS_free[0] = [k]
                    r, k = rstd(ss, w, [k])
                    ks.append([q.op("dve", [k], lambda e, t=t, r=r: e.tensor_scalar(
                        Z[:, t, 0:w], Z[:, t, 0:w], r, None, ALU.mult))])
                yield
                for j in range(0, n, 2):
                    bank = take("aux")
                    m = min(2, n - j)
                    for i in range(m):
                        for t in (0, 1):
                            o = ps[:, bank, i * 256 + t * P:i * 256 + t * P + P]
                            k = q.op("pe", ks[t] + (bank_free[bank] if i == 0 and t == 0 else []),
                                     lambda e, o=o, t=t, i=i: e.transpose(
                                         o, Z[:, t, (j + i) * P:(j + i) * P + P], ident[:, :]))
                    s = nt[0] % 2
                    nt[0] += 1
                    for i in range(m):
                        a = q.op("act", [k] + tmp_free[s], lambda e, i=i: e.activation(
                            tmpT[:, s, i * 256:i * 256 + 256], ps[:, bank, i * 256:i * 256 + 256], ACT.Copy,
                            scale=gain[:, j + i:j + i + 1]))
                    give(bank, [a])
                    f = first + j
                    src = tmpT[:, s, 0:m * 256].rearrange("p (c n) -> p c n", c=m)
                    ab = split_from(src, CH[:, f:f + m, :], CL[:, f:f + m, :], [a], after, on="dve")
                    tmp_free[s] = ab
                    for i in range(m):
                        tok["c", f + i] = ab
                    yield


            banks, k = group("cq", 8, 384, XH, XL, xr)
            plain_evac(ZQ, banks, k, 384, "zq")
            tasks.append(latent(ZQ, 384, 3, "zq", 0, C["cqn"]))
            banks, k = group("ckv", 8, 288, XH, XL, xr)
            plain_evac(ZK, banks, k, 288, "zk")
            tasks.append(latent(ZK, 256, 2, "zk", 3, C["ckvn"]))
            banks, k = group("qm", 8, 512, XH, XL, xr)
            plain_evac(QM, banks, k, 512, "qmr")

            def turned(src, srctok, hi, lo, key):
                where = 0 if key in ("ya", "yb") else 4
                d = {}
                yield from transposed([src[:, 0, :], src[:, 1, :]], lambda t, j: srctok[t], 4, hi, lo, d, yfree[where],
                                      first=where)
                for kc, v in d.items():
                    tok[key, kc - where] = v

            yfree = {0: yt_free[0], 4: yt_free[0]}

            def mem_attention():
                mqk, mp, mpT = hn[:, 0, 0:512], hn[:, 0, 512:1024], hn[:, 1, 0:512]
                qk_free, p_free, pt_free = [[hn_free[0] + hn_free[1]] for _ in range(3)]
                for t in (0, 1):
                    k = tok["qmr", t]
                    r, k2 = head_stats(QM[:, t, :], 4, 128, [k] + p_free[0], mp)
                    p_free[0] = [("s_dve", q.count["s_dve"])]
                    m3 = QM[:, t, :].rearrange("p (h d) -> p h d", h=4)
                    tok["qm", t] = q.op("pool", [k2], lambda e, m3=m3, r=r: e.tensor_tensor(
                        m3, m3, r.unsqueeze(2).to_broadcast([P, 4, P]), ALU.mult))
                    yield
                SC = 128.0 ** -0.5
                for h in range(4):
                    hs = slice(h * P, h * P + P)
                    b1 = take("aux")
                    for i, (src, key) in enumerate(((QM, "qm"), (MK, "mk"))):
                        for t in (0, 1):
                            k = q.op("pe", [tok[key, t]] + (bank_free[b1] if i + t == 0 else []),
                                     lambda e, i=i, t=t, src=src: e.transpose(
                                         ps[:, b1, i * 256 + t * P:i * 256 + t * P + P], src[:, t, hs], ident[:, :]))
                    a = q.op("act", [k] + qk_free[0], lambda e: e.activation(
                        mqk[:, 0:256], ps[:, b1, 0:256], ACT.Copy, scale=C["mqn"]))
                    a = q.op("act", [k] + qk_free[0], lambda e: e.activation(
                        mqk[:, 256:512], ps[:, b1, 256:512], ACT.Copy, scale=C["mkn"]))
                    give(b1, [a])
                    yield
                    b2 = take("aux")
                    for t in (0, 1):
                        k = q.op("pe", [a] + (bank_free[b2] if t == 0 else []), lambda e, t=t: e.matmul(
                            ps[:, b2, t * 256:t * 256 + 256], mqk[:, t * P:t * P + P], mqk[:, 256:512],
                            start=True, stop=True))
                    qk_free[0] = [k]
                    mx, nm, rs, ri = col(2), col(2), col(2), col(2)
                    d = q.op("dve", [k], lambda e: e.tensor_reduce(
                        mx, ps[:, b2, :].rearrange("p (t k) -> p t k", t=2), AX.X, ALU.max))
                    d = q.op("dve", [d], lambda e: e.tensor_scalar(nm, mx, -SC, None, ALU.mult))
                    for t in (0, 1):
                        a = q.op("act", [d] + p_free[0], lambda e, t=t: e.activation(
                            mp[:, t * 256:t * 256 + 256], ps[:, b2, t * 256:t * 256 + 256], ACT.Exp,
                            bias=nm[:, t:t + 1], scale=SC, accum_out=rs[:, t:t + 1]))
                    give(b2, [a])
                    rk = q.op("dve", [a], lambda e: e.reciprocal(ri, rs))
                    yield
                    b3 = take("aux")
                    for j in range(4):
                        k = q.op("pe", [a] + (bank_free[b3] if j == 0 else []), lambda e, j=j: e.transpose(
                            ps[:, b3, j * P:j * P + P], mp[:, j * P:j * P + P], ident[:, :]))
                    p_free[0] = [k]
                    a = q.op("act", [k] + pt_free[0], lambda e: e.activation(mpT, ps[:, b3, :], ACT.Copy))
                    give(b3, [a])
                    yield
                    b4 = take("aux")
                    for t in (0, 1):
                        for kt in (0, 1):
                            k = q.op("pe", [a, tok["mv", 0], tok["mv", 1]] + (bank_free[b4] if t + kt == 0 else []),
                                     lambda e, t=t, kt=kt: e.matmul(
                                         ps[:, b4, t * P:t * P + P], mpT[:, (2 * t + kt) * P:(2 * t + kt) * P + P],
                                         MV[:, kt, hs], start=kt == 0, stop=kt == 1))
                    pt_free[0] = [k]
                    for t in (0, 1):
                        d = q.op("dve", [k, rk], lambda e, t=t: e.tensor_scalar(
                            QM[:, t, hs], ps[:, b4, t * P:t * P + P], ri[:, t:t + 1], None, ALU.mult))
                        tok["yc", "src", t] = d
                    give(b4, [d])
                    yield
                hn_free[0] = hn_free[1] = [("s_pe", q.count["s_pe"])]
                yield from turned(QM, [[tok["yc", "src", 0]], [tok["yc", "src", 1]]], YH, YL, "yc")

            def spatial_v(banks, k0):
                sms = (col(), col())
                plain_evac(V, banks, k0, 512, "vr", ACT.Gelu, sms)
                yield
                for t in (0, 1):
                    sm, mu, ss = sms[t], col(), col()
                    k = tok["vr", t]
                    k = q.op("dve", [k], lambda e, sm=sm, mu=mu: e.tensor_scalar(mu, sm, 1.0 / 512, None, ALU.mult))
                    k = q.op("dve", [k], lambda e, t=t, mu=mu: e.tensor_scalar(
                        V[:, t, :], V[:, t, :], mu, None, ALU.subtract))
                    a = q.op("act", [k] + sS_free[0], lambda e, t=t, ss=ss: e.activation(
                        sS[:, :], V[:, t, :], ACT.Square, accum_out=ss))
                    sS_free[0] = [a]
                    r, k = rstd(ss, 512, [a])
                    k = q.op("dve", [k, s_in], lambda e, t=t, r=r: e.scalar_tensor_tensor(
                        out=V[:, t, :], in0=V[:, t, :], scalar=r, in1=gates[:, 0, 0:512],
                        op0=ALU.mult, op1=ALU.mult))
                    tok["v", t] = q.op("pool", [k, s_in], lambda e, t=t: e.tensor_tensor(
                        V[:, t, :], V[:, t, :], gates[:, 0, 512:1024], ALU.add))
                    yield

            def spatial_u(banks, k0):
                plain_evac(U, banks, k0, 512, "u", ACT.Gelu)
                yield
                for t in (0, 1):
                    b = take("aux")
                    for g in range(8):
                        k = q.op("pe", [sgw_tok, tok["v", t]] + (bank_free[b] if g == 0 else []),
                                 lambda e, t=t, g=g: e.matmul(ps[:, b, g * 64:g * 64 + 64], sgw[:, g, :],
                                                              V[:, t, g * 64:g * 64 + 64], start=True, stop=True))
                    v3 = V[:, t, :].rearrange("p (g d) -> p g d", g=8)
                    p3 = ps[:, b, :].rearrange("p (g d) -> p g d", g=8)
                    d = q.op("dve", [k], lambda e, v3=v3, p3=p3: e.tensor_tensor(
                        v3, p3, C["sgb"].unsqueeze(2).to_broadcast([P, 8, 64]), ALU.add))
                    give(b, [d])
                    tok["ya", "src", t] = q.op("pool", [d, tok["u", t]], lambda e, t=t: e.tensor_tensor(
                        U[:, t, :], U[:, t, :], V[:, t, :], ALU.mult))
                    yield
                yield from turned(U, [[tok["ya", "src", 0]], [tok["ya", "src", 1]]], YH, YL, "ya")
                tok["u_free"] = [("s_pe", q.count["s_pe"])]

            while "mk" not in tok:
                step_tasks()
            mem_task = mem_attention()
            tasks.append(mem_task)

            def cready(kc):
                while ("c", kc) not in tok:
                    step_tasks()
                return tok["c", kc]

            def rotated(T, t, gain, waits, key):
                junk = acc2[:, t, 0:768]
                r, k = head_stats(T[:, t, :], 8, 96, waits + ada["free"][t], junk)
                yield
                t3 = T[:, t, :].rearrange("p (h d) -> p h d", h=8)
                k = q.op("dve", [k], lambda e: e.tensor_tensor(
                    t3, t3, r.unsqueeze(2).to_broadcast([P, 8, 96]), ALU.mult))
                k = q.op("pool", [k, b_in], lambda e: e.tensor_tensor(
                    t3, t3, gqk[:, gain, :].unsqueeze(1).to_broadcast([P, 8, 96]), ALU.mult))
                yield
                x1, x2 = t3[:, :, 64:80], t3[:, :, 80:96]
                h4 = acc2[:, t, 0:512].rearrange("p (a h d) -> p a h d", a=4, h=8)
                cs = rp[:, t, 8, :].unsqueeze(1).to_broadcast([P, 8, 16])
                sn = rp[:, t, 9, :].unsqueeze(1).to_broadcast([P, 8, 16])
                m = [q.op("pool", [k, *tok["rope"]], lambda e: e.tensor_tensor(h4[:, i], a, b, ALU.mult))
                     for i, (a, b) in enumerate(((x1, cs), (x2, sn), (x2, cs), (x1, sn)))]
                q.op("pool", m, lambda e: e.tensor_tensor(x1, h4[:, 0], h4[:, 1], ALU.subtract))
                k = q.op("pool", m, lambda e: e.tensor_tensor(x2, h4[:, 2], h4[:, 3], ALU.add))
                ada["free"][t] = [k]
                tok[key, t] = k
                yield

            def read_q(j, banks, toks):
                for t in (0, 1):
                    k = q.op("act", [toks[t]] + after, lambda e: e.activation(
                        QT[:, t, j * 384:j * 384 + 384], ps[:, banks[t], 0:384], ACT.Copy))
                    give(banks[t], [k])
                    tok["qr", t] = [k]

            def read_kv(j, banks, toks):
                for t in (0, 1):
                    k3 = KT[:, t, :].rearrange("p (h d) -> p h d", h=8)
                    p3 = ps[:, banks[t], :].rearrange("p (h d) -> p h d", h=4)
                    v3 = VT[:, t, j * 256:j * 256 + 256].rearrange("p (h d) -> p h d", h=4)
                    q.op("act", [toks[t]] + after, lambda e: e.activation(
                        k3[:, 4 * j:4 * j + 4, 0:64], p3[:, :, 0:64], ACT.Copy))
                    k = q.op("act", [toks[t]], lambda e: e.activation(v3, p3[:, :, 64:128], ACT.Copy))
                    give(banks[t], [k])
                    tok["vt", t] = k
                    if j == 1:
                        k2 = q.op("pool", [tok["zk", t]] + after, lambda e: e.tensor_copy(
                            k3[:, :, 64:96], ZK[:, t, 256:288].unsqueeze(1).to_broadcast([P, 8, 32])))
                        tok["kr", t] = [k, k2]

            def mla_rows():
                for t in (0, 1):
                    yield from rotated(QT, t, 0, tok["qr", t], "q")
                for t in (0, 1):
                    yield from rotated(KT, t, 1, tok["kr", t], "k")

            for j in (0, 1):
                banks, k = group(f"uq{j}", 3, 384, CH, CL, cready)
                read_q(j, banks, k)
            for j in (0, 1):
                banks, k = group(f"ukv{j}", 2, 512, CH[:, 3:5, :], CL[:, 3:5, :], lambda kc: cready(kc + 3))
                read_kv(j, banks, k)
            rows_task = mla_rows()
            tasks.append(rows_task)
            banks, k = group("v", 8, 512, XH, XL, xr)
            v_task = spatial_v(banks, k)
            begin(v_task, True)
            banks, k = group("u", 8, 512, XH, XL, xr)
            finish(v_task)
            u_task = spatial_u(banks, k)
            begin(u_task, True)

            def attention():
                SC = 96.0 ** -0.5
                while rows_task in tasks or u_task in tasks:
                    yield
                yield
                for h in range(8):
                    hs = slice(h * 96, h * 96 + 96)
                    b1 = take("aux")
                    for i, (src, key) in enumerate(((QT, "q"), (KT, "k"))):
                        for t in (0, 1):
                            k = q.op("pe", [tok[key, t]] + (bank_free[b1] if i + t == 0 else []),
                                     lambda e, i=i, t=t, src=src: e.transpose(
                                         ps[0:96, b1, i * 256 + t * P:i * 256 + t * P + P], src[:, t, hs],
                                         ident[:, :]))
                    a = q.op("act", [k] + qkT_free[0], lambda e: e.activation(
                        qkT[0:96, :], ps[0:96, b1, :], ACT.Copy))
                    give(b1, [a])
                    yield
                    b2 = take("aux")
                    for t in (0, 1):
                        n = P * (t + 1)
                        k = q.op("pe", [a] + (bank_free[b2] if t == 0 else []), lambda e, t=t, n=n: e.matmul(
                            ps[:, b2, t * P:t * P + n], qkT[0:96, t * P:t * P + P], qkT[0:96, 256:256 + n],
                            start=True, stop=True))
                    qkT_free[0] = [k]
                    mx, nm, rs, ri = col(2), col(2), col(2), col(2)
                    s = q.op("dve", [k, mask_tok] + sS_free[0], lambda e: e.scalar_tensor_tensor(
                        out=sS[:, 0:384], in0=ps[:, b2, 0:384], scalar=SC, in1=mask[:, :],
                        op0=ALU.mult, op1=ALU.add))
                    give(b2, [s])
                    q.op("dve", [s], lambda e: e.tensor_reduce(mx[:, 0:1], sS[:, 0:P], AX.X, ALU.max))
                    d = q.op("dve", [s], lambda e: e.tensor_reduce(mx[:, 1:2], sS[:, P:384], AX.X, ALU.max))
                    d = q.op("dve", [d], lambda e: e.tensor_scalar(nm, mx, -1.0, None, ALU.mult))
                    for t in (0, 1):
                        sl = slice(t * P, t * P + P * (t + 1))
                        a = q.op("act", [d] + pS_free[0], lambda e, t=t, sl=sl: e.activation(
                            pS[:, sl], sS[:, sl], ACT.Exp, bias=nm[:, t:t + 1], accum_out=rs[:, t:t + 1]))
                    sS_free[0] = [a]
                    rk = q.op("dve", [a], lambda e: e.reciprocal(ri, rs))
                    yield
                    b3 = take("aux")
                    for j in range(3):
                        k = q.op("pe", [a] + (bank_free[b3] if j == 0 else []), lambda e, j=j: e.transpose(
                            ps[:, b3, j * P:j * P + P], pS[:, j * P:j * P + P], ident[:, :]))
                    pS_free[0] = [k]
                    a = q.op("act", [k] + pT_free[0], lambda e: e.activation(
                        pT[:, 0:384], ps[:, b3, 0:384], ACT.Copy))
                    give(b3, [a])
                    yield
                    b4 = take("aux")
                    vs = slice(h * 64, h * 64 + 64)
                    for n, (t, kt, j) in enumerate(((0, 0, 0), (1, 0, 1), (1, 1, 2))):
                        k = q.op("pe", [a, tok["vt", 0], tok["vt", 1]] + (bank_free[b4] if n == 0 else []),
                                 lambda e, t=t, kt=kt, j=j: e.matmul(
                                     ps[:, b4, t * 64:t * 64 + 64], pT[:, j * P:j * P + P], VT[:, kt, vs],
                                     start=kt == 0, stop=kt == t))
                    pT_free[0] = [k]
                    for t in (0, 1):
                        d = q.op("dve", [k, rk] + tok["u_free"], lambda e, t=t: e.tensor_scalar(
                            U[:, t, vs], ps[:, b4, t * 64:t * 64 + 64], ri[:, t:t + 1], None, ALU.mult))
                        tok["yb", "src", t] = d
                    give(b4, [d])
                    yield
                yield from turned(U, [[tok["yb", "src", 0]], [tok["yb", "src", 1]]], YH, YL, "yb")

            at_task = attention()
            tasks.append(at_task)

            merged_tok = {}
            gates_free = [[tok["v", 0], tok["v", 1]]]
            bg_free = [after]
            merged_t = {}

            def merge(n, j, banks, k):
                h = slice(j * 512, j * 512 + 512)
                for t in (0, 1):
                    b, g, m = banks[t], gates[:, t, h], hn[:, t, h]
                    if n == 0:
                        d = q.op("dve", [k[t], tok["gate", t, j]] + hn_free[0] + hn_free[1],
                                 lambda e: e.tensor_tensor(m, ps[:, b, :], g, ALU.mult))
                        give(b, [d])
                        merged_tok[t, j] = d
                    else:
                        d = q.op("dve", [k[t], tok["gate", t, j]], lambda e: e.tensor_tensor(
                            g, ps[:, b, :], g, ALU.mult))
                        give(b, [d])
                        merged_tok[t, j] = q.op("dve", [d, merged_tok[t, j]], lambda e: e.tensor_tensor(
                            m, m, g, ALU.add))
                    gates_free[0] = gates_free[0] + [merged_tok[t, j]]

            def turn_merged():
                g = transposed([hn[:, 0, :], hn[:, 1, :]], lambda t, j: [merged_tok[t, j // 2]], 8, XH, XL, merged_t,
                               xt_free[0])
                for _ in range(2):
                    yield
                    next(g)
                while "merged" not in tok:
                    yield
                yield from g
                hn_free[0] = hn_free[1] = [("s_pe", q.count["s_pe"])]

            for n, br in enumerate("acb"):
                bg = q.dma("s_bg", bg_free[0], bgate[:, :], A["b_gate"]["acb".index(br):"acb".index(br) + 1, :]
                           .to_broadcast([P, D]))
                free, gates_free[0] = gates_free[0], []
                for j in (0, 1):
                    banks, k = group(f"g{br}{j}", 8, 512, XH, XL, xr)
                    for t in (0, 1):
                        b = banks[t]
                        g = gates[:, t, j * 512:j * 512 + 512]
                        d = q.op("dve", [k[t], bg] + free, lambda e: e.tensor_tensor(
                            g, ps[:, b, :], bgate[:, j * 512:j * 512 + 512], ALU.add))
                        give(b, [d])
                        tok["gate", t, j] = q.op("act", [d], lambda e: e.activation(g, g, ACT.Sigmoid))
                bg_free[0] = [d]
                if br == "b":
                    xt_free[0] = [k[1]]
                where = 4 if br == "c" else 0

                def yready(kc):
                    while ("y" + br, kc) not in tok:
                        step_tasks()
                    return tok["y" + br, kc]

                if n == 0:
                    while mem_task in tasks:
                        step_tasks()
                for j in (0, 1):
                    banks, k = group(f"br{br}{j}", 4, 512, YH[:, where:where + 4, :], YL[:, where:where + 4, :],
                                     yready, last=2 if j and n == 2 else 1)
                    merge(n, j, banks, k)
                    if n == 2 and j == 0:
                        drain()
                        tasks.append(turn_merged())
                yfree[where] = [k[1]]
            tok["merged"] = True

            def mready(kc):
                while kc not in merged_t:
                    step_tasks()
                return merged_t[kc]

            def start_f2(j):
                if j == 0:
                    drain()
                    for key in ((0, 1), (1, 1)):
                        x_tok.pop(key)
                    tasks.append(gained(C["ffn2"], YH, YL, yt_tok, yfree[0] + yfree[4]))

            yt_tok.clear()
            product("wo", 8, XH, XL, mready, "plain", start_f2)
            xt_free[0] = [("s_pe", q.count["s_pe"])]
            ffn_free[0] = [("s_" + e, q.count["s_" + e]) for e in ("pe", "act", "dve", "pool")]

            up_done, last = ffn("f2", "half", YH, YL, yt_tok, True, nothing)
            yfree[0] = yfree[4] = up_done

            ab_ready[0] = [c_in, mod_tok["a1"], mod_tok["b1"]]
            finish(normed(mod["a1"], mod["b1"], XH, XL, xt_tok, xt_free[0]))
            after = [("s_" + e, q.count["s_" + e]) for e in ("pe", "act", "dve", "pool")]
            xr = lambda kc: xt_tok[kc]
            ct_free = {0: after, 1: after}
            gc_free, uu_free, gb_free = [after], [after], [after]
            tk = {}

            def conv_half(i, ut, gt):
                for j in (0, 1):
                    b1 = take("aux")
                    for c2 in (0, 1):
                        for t in (0, 1):
                            k = q.op("pe", ut[t] + (bank_free[b1] if c2 + t == 0 else []),
                                     lambda e, c2=c2, t=t: e.transpose(
                                         ps[:, b1, c2 * 256 + t * P:c2 * 256 + t * P + P],
                                         UU[:, t, (2 * j + c2) * P:(2 * j + c2) * P + P], ident[:, :]))
                    s = j
                    ta = q.op("act", [k] + ct_free[s], lambda e: e.activation(uT[:, s, :], ps[:, b1, :], ACT.Copy))
                    give(b1, [ta])
                    b2 = take("aux")
                    for c2 in (0, 1):
                        for t in (0, 1):
                            k = q.op("pe", gt[t] + (bank_free[b2] if c2 + t == 0 else []),
                                     lambda e, c2=c2, t=t: e.transpose(
                                         ps[:, b2, c2 * 256 + t * P:c2 * 256 + t * P + P],
                                         GB[:, t, (2 * j + c2) * P:(2 * j + c2) * P + P], ident[:, :]))
                    yield
                    for c2 in (0, 1):
                        ch = 4 * i + 2 * j + c2
                        u3 = uT[:, s, c2 * 256:c2 * 256 + 256].rearrange("p (r n) -> p r n", r=4)
                        c3 = cT[:, s, c2 * 256:c2 * 256 + 256].rearrange("p (r n) -> p r n", r=4)
                        w = [C["cw"][:, n * 8 + ch:n * 8 + ch + 1] for n in range(3)]
                        d = q.op("dve", [ta] + ct_free[s], lambda e, u3=u3, c3=c3, w=w: e.tensor_scalar(
                            c3, u3, w[1], None, ALU.mult))
                        d = q.op("dve", [d], lambda e, u3=u3, c3=c3, w=w: e.scalar_tensor_tensor(
                            out=c3[:, :, 1:64], in0=u3[:, :, 0:63], scalar=w[0], in1=c3[:, :, 1:64],
                            op0=ALU.mult, op1=ALU.add))
                        d = q.op("dve", [d], lambda e, u3=u3, c3=c3, w=w: e.scalar_tensor_tensor(
                            out=c3[:, :, 0:63], in0=u3[:, :, 1:64], scalar=w[2], in1=c3[:, :, 0:63],
                            op0=ALU.mult, op1=ALU.add))
                        tk[c2] = d
                    d = q.op("dve", [tk[0], tk[1], k], lambda e: e.tensor_tensor(
                        cT[:, s, :], ps[:, b2, :], cT[:, s, :], ALU.mult))
                    give(b2, [d])
                    ch = 4 * i + 2 * j
                    ab = split_from(cT[:, s, :].rearrange("p (c n) -> p c n", c=2), YH[:, ch:ch + 2, :],
                                    YL[:, ch:ch + 2, :], [d], yfree[0] + yfree[4])
                    ct_free[s] = ab
                    tk["y", ch] = tk["y", ch + 1] = ab
                    yield
                uu_free[0] = gb_free[0] = [("s_pe", q.count["s_pe"])]

            for i in (0, 1):
                banks, k = group(f"conv_cc{i}", 8, 512, XH, XL, xr)
                gcs = []
                for t in (0, 1):
                    b = banks[t]
                    a = q.op("act", [k[t]] + gc_free[0], lambda e, t=t, b=b: e.activation(
                        GC[:, t, :], ps[:, b, :], ACT.Copy))
                    give(b, [a])
                    gcs.append(a)
                banks, k = group(f"conv_hv{i}", 8, 512, XH, XL, xr)
                while tasks:
                    step_tasks()
                ut, gt = [], []
                for t in (0, 1):
                    b = banks[t]
                    d = q.op("dve", [k[t], gcs[t]] + uu_free[0], lambda e, t=t, b=b: e.tensor_tensor(
                        UU[:, t, :], GC[:, t, :], ps[:, b, :], ALU.mult))
                    give(b, [d])
                    ut.append([d])
                gc_free[0] = ut[0] + ut[1]
                banks, k = group(f"conv_gb{i}", 8, 512, XH, XL, xr)
                for t in (0, 1):
                    b = banks[t]
                    a = q.op("act", [k[t]] + gb_free[0], lambda e, t=t, b=b: e.activation(
                        GB[:, t, :], ps[:, b, :], ACT.Copy))
                    give(b, [a])
                    gt.append([a])
                tasks.append(conv_half(i, ut, gt))
            xt_free[0] = [k[1]]

            def vready(kc):
                while ("y", kc) not in tk:
                    step_tasks()
                return tk["y", kc]

            product("co", 8, YH, YL, vready, 0, nothing)
            ffn_free[0] = [("s_" + e, q.count["s_" + e]) for e in ("pe", "act", "dve", "pool")]
            ab_ready[0] = [c_in, mod_tok["a2"], mod_tok["b2"]]
            finish(normed(mod["a2"], mod["b2"], XH, XL, xt_tok, xt_free[0]))

            f_in = q.dma("s_fin", ffn_free[0], FG[:, :], A["final_g"][0:1, :].to_broadcast([P, D]))
            ffn("f3", 1, XH, XL, xt_tok, False, nothing)
            for t in (0, 1):
                for j in (0, 1):
                    h = slice(j * 512, j * 512 + 512)
                    k = q.op("dve", [R_tok[t], half_ss[t, j], f_in], lambda e: e.scalar_tensor_tensor(
                        out=hn[:, t, h], in0=X[:, t, h], scalar=R[t], in1=FG[:, h], op0=ALU.mult, op1=ALU.mult))
                    done = q.dma("s_out", [k], out[t][:, h], hn[:, t, h])
            q.wait("sp", [done])

        block = ctx.enter_context(nc.Block())

        @block.sync
        def _(eng):
            schedule(Queues(sems, "sp", eng))

        @block.scalar
        def _(eng):
            schedule(Queues(sems, "act", eng))

        @block.vector
        def _(eng):
            schedule(Queues(sems, "dve", eng))

        @block.gpsimd
        def _(eng):
            schedule(Queues(sems, "pool", eng))

        @block.tensor
        def _(eng):
            schedule(Queues(sems, "pe", eng))


COLS = (("c", 8), ("ffn1", 8), ("mix", 8), ("ffn2", 8), ("mem_norm", 8), ("norm1", 8), ("norm2", 8),
        ("cqn", 3), ("ckvn", 2), ("mqn", 1), ("mkn", 1), ("sgb", 8), ("cw", 24),
        ("ab_sh1", 8), ("ab_sc1", 8), ("ab_sh2", 8), ("ab_sc2", 8))


def layout(i):
    f = lambda a: np.asarray(a)

    a = {}

    def add(name, w):
        k = f(w).reshape(-1, P, w.shape[-1])
        n, c = k.shape[0], w.shape[-1]
        if n % 2:
            k = np.concatenate([k, np.zeros((1, P, c), k.dtype)], 0)
        a[name] = k.reshape(-1, 2, P, c).transpose(0, 2, 1, 3).reshape(-1, P, 2 * c)

    def halves(name, w):
        c = w.shape[1] // 2
        for j in (0, 1):
            add(f"{name}{j}", w[:, c * j:c * j + c])

    def cc(v):
        return f(v).reshape(-1, P).T

    def ffn(tag, w, down):
        g, u = w[:, :FF].reshape(D, 11, 256), w[:, FF:].reshape(D, 11, 256)
        for j in range(11):
            add(f"{tag}_up{j}", np.concatenate([g[:, j], u[:, j]], 1))
        halves(f"{tag}_dn", down)

    a["x"] = f(i["x"])[0].reshape(2, P, D)
    a["mem"] = f(i["mem"])[0].reshape(2, P, D)
    ffn("f1", f(i["ffn1_w_gu"])[0], f(i["ffn1_w_down"])[0])
    ffn("f2", f(i["ffn2_w_gu"])[0], f(i["ffn2_w_down"])[0])
    ffn("f3", f(i["ffn_w_in_2"])[0], f(i["ffn_w_out_2"])[0])
    halves("mkv", f(i["mem_w_kv"])[0])
    w = f(i["w_in"])[0]
    for nm, lo, hi in (("u", 0, 512), ("v", 512, 1024), ("cq", 1024, 1408), ("ckv", 1408, 1696), ("qm", 1696, 2208)):
        add(nm, w[:, lo:hi])
    for n, nm in enumerate("abc"):
        o = 2208 + n * D
        halves("g" + nm, w[:, o:o + D])
        halves("br" + nm, f(i["w_branch_" + nm])[0])
    halves("uq", f(i["mla_w_uq"])[0])
    halves("ukv", f(i["mla_w_ukv"])[0])
    halves("wo", f(i["w_out"])[0])
    ci = f(i["conv_w_in_2"])[0]
    for nm, o in (("gb", 0), ("cc", D), ("hv", 2 * D)):
        halves("conv_" + nm, ci[:, o:o + D])
    halves("co", f(i["conv_w_out_2"])[0])
    aw = f(i["ada_w_2"])[0]
    a["ada"] = np.ascontiguousarray(aw.reshape(8, P, 6, D).transpose(2, 0, 1, 3).reshape(48, P, D))
    ab = f(i["ada_b_2"])[0].reshape(6, D)
    parts = {
        "c": cc(i["c_2"]), "ffn1": cc(i["ffn1_norm"]), "mix": cc(i["mix_norm"]), "ffn2": cc(i["ffn2_norm"]),
        "mem_norm": cc(i["mem_norm"]), "norm1": cc(i["norm1_g_2"]), "norm2": cc(i["norm2_g_2"]),
        "cqn": cc(i["mla_cq_norm"]), "ckvn": cc(i["mla_ckv_norm"]), "mqn": cc(i["mem_q_norm"]),
        "mkn": cc(i["mem_k_norm"]), "sgb": f(i["sg_b"])[0].T,
        "cw": np.concatenate([cc(f(i["conv_w_2"])[0, n]) for n in range(3)], 1),
        "ab_sh1": cc(ab[0]), "ab_sc1": cc(ab[1]), "ab_sh2": cc(ab[3]), "ab_sc2": cc(ab[4]),
    }
    a["cols"] = np.concatenate([parts[k] for k, _ in COLS], 1)
    a["adab_g"] = ab[[2, 5]]
    a["mla_q_norm"], a["mla_k_norm"] = f(i["mla_q_norm"]), f(i["mla_k_norm"])
    a["positions"] = f(i["positions"])[0].reshape(2, P).T
    a["inv"] = (10000.0 ** (-np.arange(16, dtype=np.float64) / 16)).astype(np.float32)[None]
    a["sg_ln_g"], a["sg_ln_b"] = f(i["sg_ln_g"]), f(i["sg_ln_b"])
    a["sg_wT"] = f(i["sg_w"])[0].transpose(2, 0, 1)
    a["b_gate"] = f(i["b_gate"])[0].reshape(3, D)[[0, 2, 1]]
    a["final_g"] = f(i["final_g_2"])[None]
    return {k: np.ascontiguousarray(v) for k, v in a.items()}


def kernel(**inputs):
    import concourse.bacc as _bacc
    from concourse.bass_utils import run_bass_kernel_spmd as _run

    nc = _bacc.Bacc("TRN2", target_bir_lowering=False, num_devices=1)
    arrays, args = {}, {}
    for name, a in layout(inputs).items():
        arrays[f"in_{name}"] = a
        args[name] = nc.dram_tensor(f"in_{name}", a.shape, mybir.dt.from_np(a.dtype), kind="ExternalInput").ap()
    out = nc.dram_tensor("out_0", (2, P, D), F32, kind="ExternalOutput").ap()
    build(nc, args, out)
    r = _run(nc, [arrays], core_ids=[0])
    return r.results[0]["out_0"].reshape(1, 2 * P, D)
```

```python
from contextlib import ExitStack

import numpy as np

import concourse.bass as bass
from concourse import mybir

F32 = mybir.dt.float32
F32R = mybir.dt.float32r
I32 = mybir.dt.int32
ALU = mybir.AluOpType
ACT = mybir.ActivationFunctionType
AX = mybir.AxisListType

P = 128
D = 1024
KC = 8
FF = 2816
EPS = 1e-6
NEG = -1e30
RAW = 6
SPL = 4
AHEAD = 3
LATE = ((0, 0, 1), (0, 1, 1), (1, 0, 1), (0, 2, 1), (0, 3, 1), (1, 1, 3))
PI = float(np.pi)


def plan():
    out = []

    def add(name, n, w):
        out.extend((name, i, w * min(2, n - 2 * i), False) for i in range((n + 1) // 2))

    def ffn(tag, terms):
        at = len(out)
        for g in range(11):
            add(f"{tag}_up{g}", 8, 512)
        for j in (0, 1):
            add(f"{tag}_dn{j}", 22, 512)
        units, ada = out[at:], [("ada", i, 1024, True) for t in terms for i in range(8 * t, 8 * t + 8)]
        del out[at:]
        for i, u in enumerate(units):
            out.append(u)
            while ada and i >= 4 and (24 - len(ada)) * 50 < (i - 3) * 24:
                out.append(ada.pop(0))

    ffn("f1", (0, 1, 2))
    for j in (0, 1):
        add(f"mkv{j}", 8, 512)
    add("cq", 8, 384)
    add("ckv", 8, 288)
    add("qm", 8, 512)
    for j in (0, 1):
        add(f"uq{j}", 3, 384)
    for j in (0, 1):
        add(f"ukv{j}", 2, 512)
    add("v", 8, 512)
    add("u", 8, 512)
    for b in "acb":
        for j in (0, 1):
            add(f"g{b}{j}", 8, 512)
        for j in (0, 1):
            add(f"br{b}{j}", 4, 512)
    def late(name):
        out.extend((f"{name}{j}", i, 1024, False) for j, k, n in LATE for i in range(k, k + n))

    late("wo")
    ffn("f2", (3, 4, 5))
    for i in (0, 1):
        for n in ("cc", "hv", "gb"):
            add(f"conv_{n}{i}", 8, 512)
    late("co")
    ffn("f3", ())
    return out


class Queues:

    def __init__(self, sems, me, eng):
        self.sems, self.me, self.eng = sems, me, eng
        self.count = {name: 0 for name in sems}
        self.made = {}

    def wait(self, e, waits):
        if e == self.me:
            for s, v in waits:
                if self.made.get(s, 0) < v:
                    self.made[s] = v
                    self.eng.wait_ge(self.sems[s], v)

    def op(self, e, waits, fn):
        self.wait(e, waits)
        s = "s_" + e
        self.count[s] += 1
        if e == self.me:
            fn(self.eng).then_inc(self.sems[s], 1)
        return (s, self.count[s])

    def silent(self, e, waits, fn):
        self.wait(e, waits)
        if e == self.me:
            fn(self.eng)

    def dma(self, sem, waits, dst, src, e="sp"):
        self.wait(e, waits)
        self.count[sem] += 16
        if e == self.me:
            self.eng.dma_start(dst, src).then_inc(self.sems[sem], 16)
        return (sem, self.count[sem])


def build(nc, A, out):
    ctx = ExitStack()
    with ctx:
        def sb(name, shape, dt=F32, c=None):
            return (c or ctx).enter_context(nc.sbuf_tensor("t_" + name, shape, dt))

        raw = sb("raw", [P, RAW, 1024])
        wh = sb("wh", [P, SPL, 1024], F32R)
        wl = sb("wl", [P, SPL, 1024], F32R)
        X = sb("X", [P, 2, D])
        XH = sb("XH", [P, KC, 256], F32R)
        XL = sb("XL", [P, KC, 256], F32R)
        YH = sb("YH", [P, KC, 256], F32R)
        YL = sb("YL", [P, KC, 256], F32R)
        hn = sb("hn", [P, 2, D])
        tmpT = sb("tmpT", [P, 2, 512])
        gB = sb("gB", [P, 2, D])
        acc2 = sb("acc2", [P, 2, D])
        ident = sb("ident", [P, P])
        ones = sb("ones", [P, P])
        cols = sb("cols", [P, 192])
        sc = sb("sc", [P, 384])
        rp = sb("rp", [P, 2, 12, 16])
        rpi = sb("rpi", [P, 2, 16], I32)
        posi = sb("posi", [P, 2], I32)
        gqk = sb("gqk", [P, 2, 96])
        with ExitStack() as c:
            FG = sb("FG", [P, D], F32, c)
            HH = sb("HH", [P, 22, 256], F32R, c)
            HL = sb("HL", [P, 22, 256], F32R, c)
            sg = sb("sg", [P, 2, 2, 256], F32, c)
            hp = sb("hp", [P, 2, 2, 256], F32, c)
        with ExitStack() as c:
            gates = sb("gates", [P, 2, D], F32, c)
            bgate = sb("bgate", [P, D], F32, c)
            U = sb("U", [P, 2, 512], F32, c)
            V = sb("V", [P, 2, 512], F32, c)
            ZQ = sb("ZQ", [P, 2, 384], F32, c)
            ZK = sb("ZK", [P, 2, 288], F32, c)
            QM = sb("QM", [P, 2, 512], F32, c)
            MK = sb("MK", [P, 2, 512], F32, c)
            MV = sb("MV", [P, 2, 512], F32, c)
            QT = sb("QT", [P, 2, 768], F32, c)
            KT = sb("KT", [P, 2, 768], F32, c)
            VT = sb("VT", [P, 2, 512], F32, c)
            qkT = sb("qkT", [P, 512], F32, c)
            sS = sb("sS", [P, 512], F32, c)
            pS = sb("pS", [P, 2, 384], F32, c)
            pT = sb("pT", [P, 384], F32, c)
            CH = sb("CH", [P, 5, 256], F32R, c)
            CL = sb("CL", [P, 5, 256], F32R, c)
            sgw = sb("sgw", [P, 8, P], F32, c)
            mask = sb("mask", [P, 384], F32, c)
        with ExitStack() as c:
            GC = sb("GC", [P, 2, 512], F32, c)
            UU = sb("UU", [P, 2, 512], F32, c)
            GB = sb("GB", [P, 2, 512], F32, c)
            uT = sb("uT", [P, 2, 512], F32, c)
            cT = sb("cT", [P, 2, 512], F32, c)
        ps = ctx.enter_context(nc.psum_tensor("ps", [P, 8, 512], F32))
        names = ["s_pe", "s_act", "s_dve", "s_pool", "s_x00", "s_x10", "s_x01", "s_x11", "s_mem", "s_cols", "s_bc", "s_sg", "s_bg", "s_fin", "s_out"]
        sems = {n: ctx.enter_context(nc.semaphore(n)) for n in names + [f"s_raw{i}" for i in range(RAW)]}

        def schedule(q):
            stream = plan()

            used = [0]

            def col(n=1):
                a = used[0]
                used[0] += n
                assert used[0] <= 384
                return sc[:, a:a + n]

            held = set()

            bank_free = {b: [] for b in range(8)}

            def give(b, waits):
                held.discard(b)
                bank_free[b] = waits

            turn = {"main": 0, "aux": 0}

            def take(kind="main"):
                for k in (kind, "aux"):
                    pool = (0, 1, 2, 3) if k == "main" else (4, 5, 6, 7)
                    for _ in pool:
                        b = pool[turn[k] % len(pool)]
                        turn[k] += 1
                        if b not in held:
                            held.add(b)
                            return b
                raise AssertionError("no bank is free")

            raw_free = {}
            raw_in = {}
            split_of = {}
            spl_free = {}
            state = {"dma": 0, "spl": 0, "use": 0, "nspl": 0, "done": 0}
            ada = {"ready": {}, "free": {0: [], 1: []}, "tok": None,
                   "acc": (acc2[:, 0, :], acc2[:, 1, :])}
            tasks = []

            def fetch():
                n = state["dma"]
                if n >= len(stream):
                    return
                name, i, w, _ = stream[n]
                s = n % RAW
                raw_in[n] = q.dma(f"s_raw{s}", raw_free.get(n - RAW, []), raw[:, s, 0:w], A[name][i][:, 0:w])
                state["dma"] = n + 1

            def advance():
                n = state["spl"]
                name, i, w, only_raw = stream[n]
                r = raw[:, n % RAW, 0:w]
                if only_raw:
                    term, k = divmod(i, 8)
                    acc = ada["acc"][term % 2]
                    c = ada["c"][:, k:k + 1]
                    if k == 0:
                        ada["tok"] = q.op("dve", [raw_in[n], ada["c_tok"]] + ada["free"][term % 2],
                                          lambda e: e.tensor_scalar(acc, r, c, None, ALU.mult))
                    else:
                        ada["tok"] = q.op("dve", [raw_in[n], ada["tok"]],
                                          lambda e: e.scalar_tensor_tensor(out=acc, in0=r, scalar=c, in1=acc,
                                                                           op0=ALU.mult, op1=ALU.add))
                    raw_free[n] = [ada["tok"]]
                    if k == 7:
                        tasks.append(ada_reduce(term, ada["tok"]))
                else:
                    m = state["nspl"]
                    s = m % SPL
                    free = spl_free.get(m - SPL, [])
                    hi = q.op("act", [raw_in[n]] + free,
                              lambda e: e.activation(wh[:, s, 0:w], r, ACT.Copy))
                    lo = q.op("dve", [hi] + free,
                              lambda e: e.tensor_tensor(wl[:, s, 0:w], r, wh[:, s, 0:w].bitcast(F32), ALU.subtract))
                    raw_free[n] = [lo]
                    split_of[m] = [hi, lo]
                    state["nspl"] = m + 1
                state["spl"] = n + 1
                fetch()

            names = [u[0] for u in stream if not u[3]]

            def step_tasks(n=1):
                for _ in range(n):
                    for t in list(tasks[:5]):
                        if next(t, "end") == "end":
                            tasks.remove(t)

            def begin(t, first=False):
                next(t)
                tasks.insert(0, t) if first else tasks.append(t)

            def finish(t):
                for _ in t:
                    pass
                if t in tasks:
                    tasks.remove(t)

            def ahead():
                while state["spl"] < len(stream):
                    raw_only = stream[state["spl"]][3]
                    if not raw_only and state["nspl"] - SPL not in spl_free:
                        return
                    advance()
                    if not raw_only:
                        return

            def units(name, blocks, lh, ll, ready, hook=None):
                u = state["use"]
                n = blocks[-1][0] + 1
                assert names[u] == name and names[u + n - 1] == name, (names[u], name)
                while state["nspl"] < min(u + max(n, 1 + AHEAD), len(names)):
                    advance()
                toks = []
                for t in (0, 1):
                    at = -t
                    for m, kc, c0, w, banks, start, stop in blocks:
                        if m != at:
                            if t and m:
                                spl_free[u + m - 1] = [tok]
                            held_back = hook(t, m, toks) if hook else False
                            if t and m and not held_back:
                                ahead()
                            at = m
                        s = (u + m) % SPL
                        o = ps[:, banks[t], 0:w]
                        r = ready(kc)
                        while isinstance(r, dict) and t not in r:
                            assert tasks
                            step_tasks()
                        waits = split_of[u + m] + (r[t] if isinstance(r, dict) else r)
                        waits += bank_free[banks[t]] if start else []
                        xh, xl = lh[:, kc, t * P:t * P + P], ll[:, kc, t * P:t * P + P]
                        h, l = wh[:, s, c0:c0 + w], wl[:, s, c0:c0 + w]
                        q.silent("pe", waits, lambda e: e.matmul(o, xh, h, start=start, stop=False))
                        q.silent("pe", [], lambda e: e.matmul(o, xh, l, start=False, stop=False))
                        tok = q.op("pe", [], lambda e: e.matmul(o, xl, h, start=False, stop=stop))
                    toks.append(tok)
                spl_free[u + n - 1] = [tok]
                state["use"] = u + n
                for m in range(n):
                    step_tasks()
                return toks

            def group(name, n, w, lh, ll, ready, head=1, last=1, head_hook=None, last_hook=None):
                banks = (take(), take())
                if last_hook:
                    last_hook = last_hook(banks)
                nu = (n + 1) // 2
                i = 0
                while i < nu:
                    k = head if i == 0 else last if i == nu - last else 1
                    toks = units(name, [(m, 2 * (i + m) + j, j * w, w, banks, i + m + j == 0,
                                         2 * (i + m) + j == n - 1)
                                        for m in range(k) for j in (0, 1) if 2 * (i + m) + j < n],
                                 lh, ll, ready, last_hook if last_hook and i + k == nu else head_hook if i == 0 else None)
                    i += k
                return banks, toks

            def rstd(ss, n, waits):
                k = ss.shape[-1]
                m, r = col(k), col(k)
                t = q.op("dve", waits, lambda e: e.tensor_scalar(m, ss, 1.0 / n, EPS, ALU.mult, ALU.add))
                t = q.op("pool", [t, c_half], lambda e: e.tensor_tensor(r, m, mhalf[:, 0:k], ALU.pow))
                return r, t

            def split_from(src, hi, lo, waits, free, on="act"):
                if on == "act":
                    a = q.op("act", waits + free, lambda e: e.activation(hi, src, ACT.Copy))
                else:
                    a = q.op("dve", waits + free, lambda e: e.tensor_copy(hi, src))
                b = q.op("dve", [a] + waits + free,
                         lambda e: e.tensor_tensor(lo, src, hi.bitcast(F32), ALU.subtract))
                return [a, b]

            tmp_free = {0: [], 1: []}
            nt = [0]

            def transposed(src, waits, n, hi, lo, tok_of, free, a=None, b=None, first=0, burst=1):
                nj = n // 2
                turned_tok = {}
                banks = {}
                for j in range(nj):
                    if j not in banks:
                        some = range(j, min(j + burst, nj))
                        for i in some:
                            banks[i] = take("aux")
                        for t in (0, 1):
                            for i in some:
                                for c in (2 * i, 2 * i + 1):
                                    o = ps[:, banks[i], (c % 2) * 256 + t * P:(c % 2) * 256 + t * P + P]
                                    tok_pe = q.op(
                                        "pe", waits(t, i) + c_id + (bank_free[banks[i]] if c % 2 + t == 0 else []),
                                        lambda e: e.transpose(o, src[t][:, c * P:c * P + P], ident[:, :]))
                                turned_tok[i] = tok_pe
                    bank, tok = banks[j], turned_tok[j]
                    h2, l2 = hi[:, first + 2 * j:first + 2 * j + 2, :], lo[:, first + 2 * j:first + 2 * j + 2, :]
                    if a is None:
                        p2 = ps[:, bank, :].rearrange("p (c n) -> p c n", c=2)
                        ab = split_from(p2, h2, l2, [tok], free)
                        give(bank, [ab[1]])
                    else:
                        s = nt[0] % 2
                        nt[0] += 1
                        for c in (0, 1):
                            k = 2 * j + c
                            bias = 0.0 if b is None else b[:, k:k + 1]
                            m = q.op("act", [tok] + tmp_free[s] + ab_ready[0],
                                     lambda e: e.activation(
                                         tmpT[:, s, c * 256:c * 256 + 256], ps[:, bank, c * 256:c * 256 + 256],
                                         ACT.Identity, bias=bias, scale=a[:, k:k + 1]))
                        give(bank, [m])
                        ab = split_from(tmpT[:, s, :].rearrange("p (c n) -> p c n", c=2), h2, l2, [m], free,
                                        on="dve")
                        tmp_free[s] = ab
                    tok_of[first + 2 * j] = tok_of[first + 2 * j + 1] = ab
                    yield

            ab_ready = [[]]
            xt_tok, yt_tok = {}, {}
            xt_free, yt_free = [[]], [[]]
            hn_free = {0: [], 1: []}
            x_tok = {}
            R, R_tok, half_ss = {}, {}, {}

            def half_done(j, banks, toks, how, tiles=(0, 1)):
                for t in tiles:
                    h = slice(j * 512, j * 512 + 512)
                    o, xs, tmp = ps[:, banks[t], :], X[:, t, h], hn[:, t, h]
                    if how == "half":
                        k = q.op("dve", [toks[t]], lambda e: e.scalar_tensor_tensor(
                            out=xs, in0=o, scalar=0.5, in1=xs, op0=ALU.mult, op1=ALU.add))
                        give(banks[t], [k])
                    elif how == "plain":
                        k = q.op("dve", [toks[t]], lambda e: e.tensor_tensor(xs, o, xs, ALU.add))
                        give(banks[t], [k])
                    else:
                        m = q.op("dve", [toks[t]] + gb_tok[how] + hn_free[t],
                                 lambda e: e.tensor_tensor(tmp, o, gB[:, how, h], ALU.mult))
                        give(banks[t], [m])
                        k = q.op("dve", [m], lambda e: e.tensor_tensor(xs, tmp, xs, ALU.add))
                    x_tok[t, j] = k
                    ss = col()
                    k = q.op("act", [k] + hn_free[t], lambda e: e.activation(tmp, xs, ACT.Square, accum_out=ss))
                    half_ss[t, j] = k
                    if j == 0:
                        half_ss[t] = ss
                    else:
                        half_ss[t, "last"] = ss

            def row_rms(t):
                m0, m, r = col(), col(), col()
                k = q.op("dve", [half_ss[t, 0]], lambda e: e.tensor_scalar(
                    m0, half_ss[t], 1.0 / D, EPS, ALU.mult, ALU.add))
                k = q.op("dve", [half_ss[t, 1], k], lambda e: e.tensor_scalar(
                    m, half_ss[t, "last"], 1.0 / D, m0, ALU.mult, ALU.add))
                R_tok[t] = q.op("pool", [k, c_half], lambda e: e.tensor_tensor(r, m, mhalf[:, 0:1], ALU.pow))
                R[t] = r

            def tail_of(how, tail):
                def for_banks(banks):
                    def hook(t, m, toks):
                        if (t, m) == (1, 0):
                            half_done(1, banks, toks, how, (0,))
                            row_rms(0)
                        return tail(t, m)
                    return hook
                return for_banks

            def product(name, n, lh, ll, ready, how, after_half, tail):
                banks, toks = group(f"{name}0", n, 512, lh, ll, ready)
                half_done(0, banks, toks, how)
                after_half()
                banks, toks = group(f"{name}1", n, 512, lh, ll, ready, last=3, last_hook=tail_of(how, tail))
                half_done(1, banks, toks, how, (1,))
                tail(1, 3)
                row_rms(1)
                tail(1, 4)
                return toks[1]

            def late_product(name, lh, ll, ready, how, after_half, tail):
                banks = {j: (take(), take()) for j in (0, 1)}
                then = tail_of(how, tail)(banks[1])

                def hook(t, m, toks):
                    if (t, m) == (0, 1):
                        half_done(0, banks[0], first, how)
                        after_half()
                    return then(t, m, toks)

                for j, k, n in LATE:
                    end = k + n == 4
                    toks = units(f"{name}{j}", [(m, 2 * (k + m) + c, c * 512, 512, banks[j], k + m + c == 0,
                                                 k + m == 3 and c == 1) for m in range(n) for c in (0, 1)],
                                 lh, ll, ready, hook if j and end else None)
                    if j == 0:
                        first = toks
                half_done(1, banks[1], toks, how, (1,))
                tail(1, 3)
                row_rms(1)
                tail(1, 4)

            def gained(a, hi, lo, tok_of, free):
                for k in range(8):
                    tok_of.pop(k, None)
                yield from transposed([X[:, 0, :], X[:, 1, :]], lambda t, j: [x_tok[t, 0]], 4, hi, lo, tok_of, free, a)

            def normed(a, b, hi, lo, tok_of, free, pause=0):
                n = Norm(a, b, hi, lo, tok_of, free)
                n.scaled(0)
                n.scaled(1)
                yield
                for _ in range(pause):
                    yield
                tok_of.clear()
                tok_of.update({k: {} for k in range(8)})
                for t in (0, 1):
                    for j in (0, 1):
                        finish(n.turned(t, j))
                        yield

            class Norm:

                def __init__(self, *args, ready=None):
                    self.args, self.ready, self.toks = args, ready, {}

                def scaled(self, t):
                    for j in (0, 1):
                        h = slice(j * 512, j * 512 + 512)
                        self.toks[t, j] = [q.op("dve", [R_tok[t], half_ss[t, j]], lambda e: e.tensor_scalar(
                            hn[:, t, h], X[:, t, h], R[t], None, ALU.mult))]

                def turned(self, t, j):
                    a, b, hi, lo, tok_of, free = self.args
                    rest = tile_turning(hn[:, t, :], t, j, self.toks[t, j], hi, lo, tok_of, free, a, b)
                    next(rest)
                    if j == 1:
                        hn_free[t] = [("s_pe", q.count["s_pe"])]
                    return rest

                def tail(self, t, m):
                    if (t, m) == (1, 0):
                        self.args[4].clear()
                        self.args[4].update({k: {} for k in range(8)})
                        ab_ready[0] = [c_in] + [mod_tok[k] for k in self.ready]
                        self.scaled(0)
                    elif (t, m) == (1, 2):
                        self.rest = self.turned(0, 0)
                        return True
                    elif (t, m) == (1, 3):
                        finish(self.rest)
                    elif (t, m) == (1, 4):
                        self.scaled(1)
                        ahead()
                        finish(self.turned(0, 1))

                def head(self, t, m, toks):
                    if t == 0 and m in (2, 3):
                        finish(self.turned(1, m - 2))

            def tile_turned(*args):
                finish(tile_turning(*args))

            def tile_turning(src, t, j, waits, hi, lo, tok_of, free, a, b):
                bank = take("aux")
                for c in range(4):
                    tok = q.op("pe", waits + c_id + (bank_free[bank] if c == 0 else []), lambda e: e.transpose(
                        ps[:, bank, c * P:c * P + P], src[:, (4 * j + c) * P:(4 * j + c) * P + P], ident[:, :]))
                h4, l4 = (d[:, 4 * j:4 * j + 4, t * P:t * P + P] for d in (hi, lo))
                if a is None:
                    yield
                    ab = split_from(ps[:, bank, :].rearrange("p (c n) -> p c n", c=4), h4, l4, [tok], free)
                    give(bank, [ab[1]])
                else:
                    s = nt[0] % 2
                    nt[0] += 1
                    for c in range(4):
                        k = 4 * j + c
                        bias = 0.0 if b is None else b[:, k:k + 1]
                        m = q.op("act", [tok] + tmp_free[s] + ab_ready[0], lambda e: e.activation(
                            tmpT[:, s, c * P:c * P + P], ps[:, bank, c * P:c * P + P], ACT.Identity, bias=bias,
                            scale=a[:, k:k + 1]))
                    give(bank, [m])
                    yield
                    ab = split_from(tmpT[:, s, :].rearrange("p (c n) -> p c n", c=4), h4, l4, [m], free, on="dve")
                    tmp_free[s] = ab
                for c in range(4):
                    tok_of.setdefault(4 * j + c, {})[t] = ab

            c_in = q.dma("s_cols", [], cols[:, 0:A["cols"].shape[1]], A["cols"])
            x_in = {}
            for j in (0, 1):
                h = slice(j * 512, j * 512 + 512)
                for t in (0, 1):
                    x_in[t, j] = q.dma(f"s_x{t}{j}", [], X[:, t, h], A["x"][t][:, h])
                if j == 0:
                    fetch()
            for _ in range(RAW - 1):
                fetch()
            for t in (0, 1):
                for j in (0, 1):
                    x_tok[t, j] = x_in[t, j]
            late = {}

            def late_loads():
                for _ in range(3):
                    yield
                late["mem"] = [q.dma("s_mem", [], hn[:, t, :], A["mem"][t]) for t in (0, 1)][-1]
                for _ in range(5):
                    yield
                late["bc"] = [
                    q.dma("s_bc", [], gB[:, 0, :], A["adab_g"][0:1, :].to_broadcast([P, D])),
                    q.dma("s_bc", [], gB[:, 1, :], A["adab_g"][1:2, :].to_broadcast([P, D])),
                    q.dma("s_bc", [], gqk[:, 0, :], A["mla_q_norm"][0:1, :].to_broadcast([P, 96])),
                    q.dma("s_bc", [], gqk[:, 1, :], A["mla_k_norm"][0:1, :].to_broadcast([P, 96])),
                    q.dma("s_bc", [], posi[:, :], A["positions"]),
                    q.dma("s_bc", [], rp[:, 0, 0, :], A["inv"][0:1, :].to_broadcast([P, 16])),
                    q.dma("s_bc", [], rp[:, 1, 0, :], A["inv"][0:1, :].to_broadcast([P, 16]))][-1]

            gb_tok = {0: [], 1: []}

            C = {}
            at = 0
            for nm, k in COLS:
                C[nm] = cols[:, at:at + k]
                at += k

            mhalf = sc[:, 0:8]
            used[0] = 8
            c_half = q.op("pool", [], lambda e: e.memset(mhalf, -0.5))
            z = q.op("pool", [], lambda e: e.memset(ident[:, :], 0.0))
            c_id = [q.op("pool", [z], lambda e: e.affine_select(
                out=ident[:, :], in_=ident[:, :], compare_op=ALU.not_equal, fill=1.0, base=0,
                pattern=[[-1, P]], channel_multiplier=1))]
            c_one = q.op("pool", [], lambda e: e.memset(ones[:, :], 1.0))

            ada["c"] = col(8)
            ada["c_tok"] = q.op("act", [c_in], lambda e: e.activation(ada["c"], C["c"], ACT.Silu))
            mod = {k: col(8) for k in ("b1", "a1", "b2", "a2")}
            mod_tok = {}

            def ada_reduce(term, tok):
                acc = ada["acc"][term % 2]
                yield
                if term in (2, 5):
                    g = 0 if term == 2 else 1
                    bk = take("aux"), take("aux")
                    for j in (0, 1):
                        k = q.op("pe", [tok, c_one] + bank_free[bk[j]], lambda e, j=j: e.matmul(
                            ps[:, bk[j], :], ones[:, :], acc[:, j * 512:j * 512 + 512], start=True, stop=True))
                        d = q.op("dve", [k, late["bc"]], lambda e, j=j: e.tensor_tensor(
                            gB[:, g, j * 512:j * 512 + 512], ps[:, bk[j], :], gB[:, g, j * 512:j * 512 + 512], ALU.add))
                        give(bk[j], [d])
                    gb_tok[g] = [d]
                else:
                    bk = take("aux")
                    for c in range(8):
                        k = q.op("pe", [tok, c_one] + (bank_free[bk] if c == 0 else []), lambda e, c=c: e.matmul(
                            ps[:, bk, 2 * c:2 * c + 1], acc[:, c * P:c * P + P], ones[:, 0:1], start=True, stop=True))
                    pv = ps[:, bk, 0:16].rearrange("p (c x) -> p c x", x=2)[:, :, 0]
                    nm, bias = {0: ("b1", "ab_sh1"), 1: ("a1", "ab_sc1"), 3: ("b2", "ab_sh2"), 4: ("a2", "ab_sc2")}[term]
                    d = q.op("dve", [k, c_in], lambda e: e.tensor_tensor(mod[nm], pv, C[bias], ALU.add))
                    give(bk, [d])
                    if nm[0] == "a":
                        g = C["norm1" if nm == "a1" else "norm2"]
                        d = q.op("dve", [d], lambda e: e.scalar_tensor_tensor(
                            out=mod[nm], in0=mod[nm], scalar=1.0, in1=g, op0=ALU.add, op1=ALU.mult))
                    mod_tok[nm] = d
                ada["free"][term % 2] = [("s_pe", q.count["s_pe"])]

            def ffn(tag, how, xh, xl, x_of, defer, tail, head_hook=None):
                hid_tok = {}

                def hidden(g, banks, toks):
                    s = g % 2
                    hs = []
                    for t in (0, 1):
                        sc1 = R[t] if defer else 1.0
                        w = [R_tok[t]] if defer else []
                        a = q.op("act", [toks[t]] + w + sg_free[s], lambda e: e.activation(
                            sg[:, s, t, :], ps[:, banks[t], 0:256], ACT.Silu, scale=sc1))
                        if defer:
                            d = q.op("dve", [a] + w + hp_free[s], lambda e: e.scalar_tensor_tensor(
                                out=hp[:, s, t, :], in0=ps[:, banks[t], 256:512], scalar=R[t], in1=sg[:, s, t, :],
                                op0=ALU.mult, op1=ALU.mult))
                        else:
                            d = q.op("dve", [a] + hp_free[s], lambda e: e.tensor_tensor(
                                hp[:, s, t, :], sg[:, s, t, :], ps[:, banks[t], 256:512], ALU.mult))
                        give(banks[t], [d])
                        hs.append([d])
                    sg_free[s] = hs[0] + hs[1]
                    yield
                    yield from transposed([hp[:, s, 0, :], hp[:, s, 1, :]], lambda t, j: hs[t], 2, HH, HL, hid_tok,
                                          ffn_free[0], first=2 * g)
                    hp_free[s] = [("s_pe", q.count["s_pe"])]

                sg_free = {0: ffn_free[0], 1: ffn_free[0]}
                hp_free = {0: ffn_free[0], 1: ffn_free[0]}

                def x_ready(kc):
                    while kc not in x_of:
                        assert tasks
                        step_tasks()
                    return x_of[kc]

                for g in range(11):
                    banks, toks = group(f"{tag}_up{g}", 8, 512, xh, xl, x_ready,
                                        head=4 if g == 0 and head_hook else 1,
                                        head_hook=None if g else head_hook)
                    begin(hidden(g, banks, toks), True)
                up_done = [toks[1]]

                def ready(kc):
                    while kc not in hid_tok:
                        step_tasks()
                    return hid_tok[kc]

                last = product(f"{tag}_dn", 22, HH, HL, ready, how, drain, tail)
                return up_done, last

            ffn_free = [[]]
            ab_ready[0] = [c_in]

            def first_stats():
                for t in (0, 1):
                    ss = col()
                    k = q.op("act", [x_in[t, 0], x_in[t, 1]], lambda e: e.activation(acc2[:, t, :], X[:, t, :], ACT.Square, accum_out=ss))
                    R[t], R_tok[t] = rstd(ss, D, [k])
                    ada["free"][t] = [k]
                yield

            def mem_norm():
                for _ in range(12):
                    yield
                toks = {}
                k = m_in = late["mem"]
                for t in (0, 1):
                    ss = col()
                    k = q.op("act", [m_in, k] + tmp_free[0] + tmp_free[1], lambda e: e.activation(
                        tmpT[:, :, :], hn[:, t, 0:D].rearrange("p (a b) -> p a b", a=2), ACT.Square, accum_out=ss))
                    for s in (0, 1):
                        tmp_free[s] = [k]
                    r, k2 = rstd(ss, D, [k])
                    toks[t] = [q.op("dve", [k2], lambda e: e.tensor_scalar(
                        hn[:, t, :], hn[:, t, :], r, None, ALU.mult))]
                    yield
                yield
                yield from transposed([hn[:, 0, :], hn[:, 1, :]], lambda t, j: toks[t], 8, YH, YL, yt_tok, [],
                                      C["mem_norm"])
                for t in (0, 1):
                    hn_free[t] = [("s_pe", q.count["s_pe"])]

            def drain():
                while tasks:
                    step_tasks()

            tok = {}

            def tables():
                rope_tok = []
                for _ in range(26):
                    yield
                for t in (0, 1):
                    V_ = lambda i: rp[:, t, i, :]
                    pf = col()
                    k = q.op("dve", [late["bc"]], lambda e: e.tensor_copy(pf, posi[:, t:t + 1]))
                    k = q.op("dve", [k], lambda e: e.tensor_scalar(V_(1), V_(0), pf, None, ALU.mult))
                    k = q.op("dve", [k], lambda e: e.tensor_scalar(V_(2), V_(1), 1.0 / (2 * PI), None, ALU.mult))
                    k = q.op("dve", [k], lambda e: e.tensor_copy(rpi[:, t, :], V_(2)))
                    k = q.op("dve", [k], lambda e: e.tensor_copy(V_(3), rpi[:, t, :]))
                    c1, c2 = 6.28125, float(np.float32(np.round((2 * np.pi - 6.28125) * 2 ** 20) / 2 ** 20))
                    c3 = float(2 * np.pi - 6.28125 - c2)
                    yield
                    for n, cc in enumerate((c1, c2, c3)):
                        k = q.op("dve", [k], lambda e, n=n, cc=cc: e.scalar_tensor_tensor(
                            out=V_(1), in0=V_(3), scalar=-cc, in1=V_(1), op0=ALU.mult, op1=ALU.add))
                    yield
                    k = q.op("dve", [k], lambda e: e.tensor_scalar(V_(4), V_(1), PI, -PI, ALU.min, ALU.max))
                    k = q.op("dve", [k], lambda e: e.tensor_scalar(V_(5), V_(4), PI / 2, -2 * PI, ALU.is_gt, ALU.mult))
                    k = q.op("dve", [k], lambda e: e.scalar_tensor_tensor(
                        out=V_(6), in0=V_(4), scalar=PI / 2, in1=V_(5), op0=ALU.add, op1=ALU.add))
                    k = q.op("dve", [k], lambda e: e.tensor_scalar(V_(7), V_(6), PI, -PI, ALU.min, ALU.max))
                    yield
                    yield
                    a = q.op("act", [k], lambda e: e.activation(V_(8), V_(7), ACT.Sin))
                    rope_tok.append(q.op("act", [k], lambda e: e.activation(V_(9), V_(4), ACT.Sin)))
                    yield
                tok["rope"] = rope_tok

            for _ in transposed([X[:, 0, :], X[:, 1, :]], lambda t, j: [x_in[t, j // 2]], 8, XH, XL, xt_tok, [], C["ffn1"]):
                if state["spl"] < 3:
                    advance()
            assert not any(u[3] for u in stream[:5])
            tasks.extend([first_stats(), late_loads(), mem_norm(), tables()])

            def nothing(t, m):
                pass

            up_done, last = ffn("f1", "half", XH, XL, xt_tok, True, nothing)
            xt_free[0] = up_done

            after = [last, ("s_dve", q.count["s_dve"]), ("s_act", q.count["s_act"])]

            s_in = [q.dma("s_sg", after, gates[:, 0, 0:512], A["sg_ln_g"][0:1, :].to_broadcast([P, 512])),
                    q.dma("s_sg", after, gates[:, 0, 512:1024], A["sg_ln_b"][0:1, :].to_broadcast([P, 512])),
                    q.dma("s_sg", after, sgw[:, :, :], A["sg_wT"])][-1]
            sgw_tok = q.op("pool", after + [s_in], lambda e: e.affine_select(
                out=sgw[:, :, :], in_=sgw[:, :, :], compare_op=ALU.is_ge, fill=0.0, base=0,
                pattern=[[0, 8], [1, P]], channel_multiplier=-1))
            mk = q.op("pool", after, lambda e: e.memset(mask[:, :], 0.0))
            for o in (0, 256):
                mk = q.op("pool", [mk], lambda e, o=o: e.affine_select(
                    out=mask[:, o:o + P], in_=mask[:, o:o + P], compare_op=ALU.is_ge, fill=NEG, base=0,
                    pattern=[[-1, P]], channel_multiplier=1))
            mask_tok = mk

            def head_stats(src, n, hd, waits, junk):
                s3 = src.rearrange("p (h d) -> p h d", h=n)
                j3 = junk.rearrange("p (h d) -> p h d", h=n)
                ss = col(n)
                k = q.op("dve", waits, lambda e: e.tensor_tensor(j3, s3, s3, ALU.mult))
                k = q.op("dve", [k], lambda e: e.tensor_reduce(ss, j3, AX.X, ALU.add))
                return rstd(ss, hd, [k])

            def plain_evac(dst, banks, k0, w, key, func=None, accum=None):
                for t in (0, 1):
                    b = banks[t]
                    a = {} if accum is None else {"accum_out": accum[t]}
                    k = q.op("act", [k0[t]] + after, lambda e, t=t, b=b, a=a: e.activation(
                        dst[:, t, 0:w], ps[:, b, 0:w], func or ACT.Copy, **a))
                    give(b, [k])
                    tok[key, t] = k

            def mem_k(banks, k0):
                plain_evac(MK, banks, k0, 512, "mkr")
                yield
                for t in (0, 1):
                    k = tok["mkr", t]
                    r, k2 = head_stats(MK[:, t, :], 4, 128, [k] + sS_free[0], sS[:, :])
                    sS_free[0] = [k2]
                    m3 = MK[:, t, :].rearrange("p (h d) -> p h d", h=4)
                    tok["mk", t] = q.op("pool", [k2], lambda e, m3=m3, r=r: e.tensor_tensor(
                        m3, m3, r.unsqueeze(2).to_broadcast([P, 4, P]), ALU.mult))
                    yield
                tok["mk"] = [tok["mk", 0], tok["mk", 1]]

            sS_free, pS_free, pT_free, qkT_free = [after], [after], [after], [after]
            norm_task = normed(C["mix"], None, XH, XL, xt_tok, xt_free[0], 2)
            next(norm_task)
            tasks.append(norm_task)
            banks, k = group("mkv0", 8, 512, YH, YL, lambda kc: yt_tok[kc])
            begin(mem_k(banks, k))
            banks, k = group("mkv1", 8, 512, YH, YL, lambda kc: yt_tok[kc])
            yt_free[0] = [k[1]]
            plain_evac(MV, banks, k, 512, "mv")
            finish(norm_task)

            xr = lambda kc: xt_tok[kc]

            def latent(Z, w, n, key, first, gain):
                ks = []
                for t in (0, 1):
                    ss = col()
                    k = q.op("act", [tok[key, t]] + sS_free[0], lambda e, t=t, ss=ss: e.activation(
                        sS[:, 0:w], Z[:, t, 0:w], ACT.Square, accum_out=ss))
                    sS_free[0] = [k]
                    r, k = rstd(ss, w, [k])
                    ks.append([q.op("dve", [k], lambda e, t=t, r=r: e.tensor_scalar(
                        Z[:, t, 0:w], Z[:, t, 0:w], r, None, ALU.mult))])
                yield
                for j in range(0, n, 2):
                    bank = take("aux")
                    m = min(2, n - j)
                    for i in range(m):
                        for t in (0, 1):
                            o = ps[:, bank, i * 256 + t * P:i * 256 + t * P + P]
                            k = q.op("pe", ks[t] + (bank_free[bank] if i == 0 and t == 0 else []),
                                     lambda e, o=o, t=t, i=i: e.transpose(
                                         o, Z[:, t, (j + i) * P:(j + i) * P + P], ident[:, :]))
                    s = nt[0] % 2
                    nt[0] += 1
                    for i in range(m):
                        a = q.op("act", [k] + tmp_free[s], lambda e, i=i: e.activation(
                            tmpT[:, s, i * 256:i * 256 + 256], ps[:, bank, i * 256:i * 256 + 256], ACT.Copy,
                            scale=gain[:, j + i:j + i + 1]))
                    give(bank, [a])
                    f = first + j
                    src = tmpT[:, s, 0:m * 256].rearrange("p (c n) -> p c n", c=m)
                    ab = split_from(src, CH[:, f:f + m, :], CL[:, f:f + m, :], [a], after, on="dve")
                    tmp_free[s] = ab
                    for i in range(m):
                        tok["c", f + i] = ab
                    yield


            banks, k = group("cq", 8, 384, XH, XL, xr)
            plain_evac(ZQ, banks, k, 384, "zq")
            latents = [latent(ZQ, 384, 3, "zq", 0, C["cqn"]), latent(ZK, 256, 2, "zk", 3, C["ckvn"])]
            tasks.append(latents[0])
            banks, k = group("ckv", 8, 288, XH, XL, xr)
            plain_evac(ZK, banks, k, 288, "zk")
            tasks.append(latents[1])
            banks, k = group("qm", 8, 512, XH, XL, xr)
            plain_evac(QM, banks, k, 512, "qmr")

            def turned(src, srctok, hi, lo, key):
                where = 0 if key in ("ya", "yb") else 4
                d = {}
                yield from transposed([src[:, 0, :], src[:, 1, :]], lambda t, j: srctok[t], 4, hi, lo, d, yfree[where],
                                      first=where)
                for kc, v in d.items():
                    tok[key, kc - where] = v

            yfree = {0: yt_free[0], 4: yt_free[0]}

            def pipeline(n, turn_in, scores, turn_p, values):
                for step in range(2 * n + 3):
                    m = step // 2
                    if step % 2 == 0:
                        if m >= 2:
                            values(m - 2)
                        if m < n:
                            turn_in(m)
                    else:
                        if m >= 1:
                            turn_p(m - 1)
                        if m < n:
                            scores(m)
                    yield

            def mem_attention():
                mqk, mpT = hn[:, 0, 0:512], hn[:, 1, 0:512]
                mp = (hn[:, 0, 512:1024], hn[:, 1, 512:1024])
                free = {k: hn_free[0] + hn_free[1] for k in ("qk", "p0", "p1", "pt")}
                for t in (0, 1):
                    k = tok["qmr", t]
                    r, k2 = head_stats(QM[:, t, :], 4, 128, [k] + free["p0"], mp[0])
                    free["p0"] = [k2]
                    m3 = QM[:, t, :].rearrange("p (h d) -> p h d", h=4)
                    tok["qm", t] = q.op("pool", [k2], lambda e: e.tensor_tensor(
                        m3, m3, r.unsqueeze(2).to_broadcast([P, 4, P]), ALU.mult))
                    yield
                for _ in range(2):
                    yield
                SC = 128.0 ** -0.5
                at = {}

                def turn_in(h):
                    hs = slice(h * P, h * P + P)
                    b = take("aux")
                    for i, (src, key) in enumerate(((QM, "qm"), (MK, "mk"))):
                        for t in (0, 1):
                            k = q.op("pe", [tok[key, t]] + (bank_free[b] if i + t == 0 else []), lambda e: e.transpose(
                                ps[:, b, i * 256 + t * P:i * 256 + t * P + P], src[:, t, hs], ident[:, :]))
                    for i, g in enumerate(("mqn", "mkn")):
                        a = q.op("act", [k] + free["qk"], lambda e: e.activation(
                            mqk[:, i * 256:i * 256 + 256], ps[:, b, i * 256:i * 256 + 256], ACT.Copy, scale=C[g]))
                    give(b, [a])
                    at["qk", h] = a

                def scores(h):
                    b = take("aux")
                    for t in (0, 1):
                        k = q.op("pe", [at["qk", h]] + (bank_free[b] if t == 0 else []), lambda e: e.matmul(
                            ps[:, b, t * 256:t * 256 + 256], mqk[:, t * P:t * P + P], mqk[:, 256:512],
                            start=True, stop=True))
                    free["qk"] = [k]
                    mx, nm, rs, ri = col(2), col(2), col(2), col(2)
                    d = q.op("dve", [k], lambda e: e.tensor_reduce(
                        mx, ps[:, b, :].rearrange("p (t k) -> p t k", t=2), AX.X, ALU.max))
                    d = q.op("dve", [d], lambda e: e.tensor_scalar(nm, mx, -SC, None, ALU.mult))
                    pf = "p0" if h % 2 == 0 else "p1"
                    for t in (0, 1):
                        a = q.op("act", [d] + free[pf], lambda e: e.activation(
                            mp[h % 2][:, t * 256:t * 256 + 256], ps[:, b, t * 256:t * 256 + 256], ACT.Exp,
                            bias=nm[:, t:t + 1], scale=SC, accum_out=rs[:, t:t + 1]))
                    give(b, [a])
                    at["p", h] = a, rs, ri

                def turn_p(h):
                    a, rs, ri = at["p", h]
                    at["ri", h] = q.op("dve", [a], lambda e: e.reciprocal(ri, rs))
                    b = take("aux")
                    for j in range(4):
                        k = q.op("pe", [a] + (bank_free[b] if j == 0 else []), lambda e: e.transpose(
                            ps[:, b, j * P:j * P + P], mp[h % 2][:, j * P:j * P + P], ident[:, :]))
                    free["p0" if h % 2 == 0 else "p1"] = [k]
                    at["pt", h] = a = q.op("act", [k] + free["pt"], lambda e: e.activation(
                        mpT, ps[:, b, :], ACT.Copy))
                    give(b, [a])

                def values(h):
                    hs = slice(h * P, h * P + P)
                    b = take("aux")
                    for t in (0, 1):
                        for kt in (0, 1):
                            k = q.op("pe", [at["pt", h], tok["mv", 0], tok["mv", 1]]
                                     + (bank_free[b] if t + kt == 0 else []), lambda e: e.matmul(
                                         ps[:, b, t * P:t * P + P], mpT[:, (2 * t + kt) * P:(2 * t + kt) * P + P],
                                         MV[:, kt, hs], start=kt == 0, stop=kt == 1))
                    free["pt"] = [k]
                    ri = at["p", h][2]
                    for t in (0, 1):
                        d = q.op("dve", [k, at["ri", h]], lambda e: e.tensor_scalar(
                            QM[:, t, hs], ps[:, b, t * P:t * P + P], ri[:, t:t + 1], None, ALU.mult))
                        tok["yc", "src", t] = d
                    give(b, [d])

                yield from pipeline(4, turn_in, scores, turn_p, values)
                hn_free[0] = hn_free[1] = [("s_pe", q.count["s_pe"])]
                yield from turned(QM, [[tok["yc", "src", 0]], [tok["yc", "src", 1]]], YH, YL, "yc")

            def spatial_v(banks, k0):
                sms = (col(), col())
                plain_evac(V, banks, k0, 512, "vr", ACT.Gelu, sms)
                yield
                ks = {}
                for t in (0, 1):
                    mu = col()
                    k = q.op("dve", [tok["vr", t]], lambda e: e.tensor_scalar(mu, sms[t], 1.0 / 512, None, ALU.mult))
                    ks[t] = q.op("dve", [k], lambda e: e.tensor_scalar(V[:, t, :], V[:, t, :], mu, None, ALU.subtract))
                yield
                for t in (0, 1):
                    ss = col()
                    a = q.op("act", [ks[t]] + sS_free[0], lambda e: e.activation(
                        sS[:, :], V[:, t, :], ACT.Square, accum_out=ss))
                    sS_free[0] = [a]
                    ks[t] = rstd(ss, 512, [a])
                yield
                for t in (0, 1):
                    r, k = ks[t]
                    k = q.op("dve", [k, s_in], lambda e: e.scalar_tensor_tensor(
                        out=V[:, t, :], in0=V[:, t, :], scalar=r, in1=gates[:, 0, 0:512],
                        op0=ALU.mult, op1=ALU.mult))
                    tok["v", t] = q.op("pool", [k, s_in], lambda e: e.tensor_tensor(
                        V[:, t, :], V[:, t, :], gates[:, 0, 512:1024], ALU.add))
                yield

            def spatial_u(banks, k0):
                plain_evac(U, banks, k0, 512, "u", ACT.Gelu)
                yield
                for t in (0, 1):
                    b = take("aux")
                    for g in range(8):
                        k = q.op("pe", [sgw_tok, tok["v", t]] + (bank_free[b] if g == 0 else []),
                                 lambda e, t=t, g=g: e.matmul(ps[:, b, g * 64:g * 64 + 64], sgw[:, g, :],
                                                              V[:, t, g * 64:g * 64 + 64], start=True, stop=True))
                    v3 = V[:, t, :].rearrange("p (g d) -> p g d", g=8)
                    p3 = ps[:, b, :].rearrange("p (g d) -> p g d", g=8)
                    d = q.op("dve", [k], lambda e, v3=v3, p3=p3: e.tensor_tensor(
                        v3, p3, C["sgb"].unsqueeze(2).to_broadcast([P, 8, 64]), ALU.add))
                    give(b, [d])
                    tok["ya", "src", t] = q.op("pool", [d, tok["u", t]], lambda e, t=t: e.tensor_tensor(
                        U[:, t, :], U[:, t, :], V[:, t, :], ALU.mult))
                    yield
                yield from turned(U, [[tok["ya", "src", 0]], [tok["ya", "src", 1]]], YH, YL, "ya")
                tok["u_free"] = [("s_pe", q.count["s_pe"])]

            while "mk" not in tok:
                step_tasks()
            mem_task = mem_attention()
            tasks.append(mem_task)
            for task in latents:
                finish(task)
            cready = lambda kc: tok["c", kc]

            def rotated(T, t, gain, waits, key):
                junk = acc2[:, t, 0:768]
                r, k = head_stats(T[:, t, :], 8, 96, waits + ada["free"][t], junk)
                yield
                t3 = T[:, t, :].rearrange("p (h d) -> p h d", h=8)
                k = q.op("dve", [k], lambda e: e.tensor_tensor(
                    t3, t3, r.unsqueeze(2).to_broadcast([P, 8, 96]), ALU.mult))
                k = q.op("pool", [k, late["bc"]], lambda e: e.tensor_tensor(
                    t3, t3, gqk[:, gain, :].unsqueeze(1).to_broadcast([P, 8, 96]), ALU.mult))
                yield
                x1, x2 = t3[:, :, 64:80], t3[:, :, 80:96]
                h4 = acc2[:, t, 0:512].rearrange("p (a h d) -> p a h d", a=4, h=8)
                cs = rp[:, t, 8, :].unsqueeze(1).to_broadcast([P, 8, 16])
                sn = rp[:, t, 9, :].unsqueeze(1).to_broadcast([P, 8, 16])
                m = [q.op("pool", [k, *tok["rope"]], lambda e: e.tensor_tensor(h4[:, i], a, b, ALU.mult))
                     for i, (a, b) in enumerate(((x1, cs), (x2, sn), (x2, cs), (x1, sn)))]
                q.op("pool", m, lambda e: e.tensor_tensor(x1, h4[:, 0], h4[:, 1], ALU.subtract))
                k = q.op("pool", m, lambda e: e.tensor_tensor(x2, h4[:, 2], h4[:, 3], ALU.add))
                ada["free"][t] = [k]
                tok[key, t] = k
                yield

            def read_q(j, banks, toks):
                for t in (0, 1):
                    k = q.op("act", [toks[t]] + after, lambda e: e.activation(
                        QT[:, t, j * 384:j * 384 + 384], ps[:, banks[t], 0:384], ACT.Copy))
                    give(banks[t], [k])
                    tok["qr", t] = [k]

            def read_kv(j, banks, toks):
                for t in (0, 1):
                    k3 = KT[:, t, :].rearrange("p (h d) -> p h d", h=8)
                    p3 = ps[:, banks[t], :].rearrange("p (h d) -> p h d", h=4)
                    v3 = VT[:, t, j * 256:j * 256 + 256].rearrange("p (h d) -> p h d", h=4)
                    q.op("act", [toks[t]] + after, lambda e: e.activation(
                        k3[:, 4 * j:4 * j + 4, 0:64], p3[:, :, 0:64], ACT.Copy))
                    k = q.op("act", [toks[t]], lambda e: e.activation(v3, p3[:, :, 64:128], ACT.Copy))
                    give(banks[t], [k])
                    tok["vt", t] = k
                    if j == 1:
                        k2 = q.op("pool", [tok["zk", t]] + after, lambda e: e.tensor_copy(
                            k3[:, :, 64:96], ZK[:, t, 256:288].unsqueeze(1).to_broadcast([P, 8, 32])))
                        tok["kr", t] = [k, k2]

            def mla_rows():
                for t in (0, 1):
                    yield from rotated(QT, t, 0, tok["qr", t], "q")
                for t in (0, 1):
                    yield from rotated(KT, t, 1, tok["kr", t], "k")

            for j in (0, 1):
                banks, k = group(f"uq{j}", 3, 384, CH, CL, cready)
                read_q(j, banks, k)
            for j in (0, 1):
                banks, k = group(f"ukv{j}", 2, 512, CH[:, 3:5, :], CL[:, 3:5, :], lambda kc: cready(kc + 3))
                read_kv(j, banks, k)
            rows_task = mla_rows()
            tasks.append(rows_task)
            banks, k = group("v", 8, 512, XH, XL, xr)
            v_task = spatial_v(banks, k)
            begin(v_task, True)
            banks, k = group("u", 8, 512, XH, XL, xr)
            finish(v_task)
            u_task = spatial_u(banks, k)
            begin(u_task, True)

            def attention():
                SC = 96.0 ** -0.5
                while rows_task in tasks or u_task in tasks:
                    yield
                yield
                at = {}
                free = {"qk": after, "s": sS_free[0], "p0": after, "p1": after, "pt": after}

                def turn_in(h):
                    hs = slice(h * 96, h * 96 + 96)
                    b = take("aux")
                    for i, (src, key) in enumerate(((QT, "q"), (KT, "k"))):
                        for t in (0, 1):
                            k = q.op("pe", [tok[key, t]] + (bank_free[b] if i + t == 0 else []), lambda e: e.transpose(
                                ps[0:96, b, i * 256 + t * P:i * 256 + t * P + P], src[:, t, hs], ident[:, :]))
                    at["qk", h] = a = q.op("act", [k] + free["qk"], lambda e: e.activation(
                        qkT[0:96, :], ps[0:96, b, :], ACT.Copy))
                    give(b, [a])

                def scores(h):
                    b = take("aux")
                    for t in (0, 1):
                        n = P * (t + 1)
                        k = q.op("pe", [at["qk", h]] + (bank_free[b] if t == 0 else []), lambda e: e.matmul(
                            ps[:, b, t * P:t * P + n], qkT[0:96, t * P:t * P + P], qkT[0:96, 256:256 + n],
                            start=True, stop=True))
                    free["qk"] = [k]
                    mx, nm, rs, ri = col(2), col(2), col(2), col(2)
                    s = q.op("dve", [k, mask_tok] + free["s"], lambda e: e.scalar_tensor_tensor(
                        out=sS[:, 0:384], in0=ps[:, b, 0:384], scalar=SC, in1=mask[:, :], op0=ALU.mult, op1=ALU.add))
                    give(b, [s])
                    q.op("dve", [s], lambda e: e.tensor_reduce(mx[:, 0:1], sS[:, 0:P], AX.X, ALU.max))
                    d = q.op("dve", [s], lambda e: e.tensor_reduce(mx[:, 1:2], sS[:, P:384], AX.X, ALU.max))
                    d = q.op("dve", [d], lambda e: e.tensor_scalar(nm, mx, -1.0, None, ALU.mult))
                    pf = "p0" if h % 2 == 0 else "p1"
                    for t in (0, 1):
                        sl = slice(t * P, t * P + P * (t + 1))
                        a = q.op("act", [d] + free[pf], lambda e: e.activation(
                            pS[:, h % 2, sl], sS[:, sl], ACT.Exp, bias=nm[:, t:t + 1], accum_out=rs[:, t:t + 1]))
                    free["s"] = [a]
                    at["p", h] = a, rs, ri

                def turn_p(h):
                    a, rs, ri = at["p", h]
                    at["ri", h] = q.op("dve", [a], lambda e: e.reciprocal(ri, rs))
                    b = take("aux")
                    for j in range(3):
                        k = q.op("pe", [a] + (bank_free[b] if j == 0 else []), lambda e: e.transpose(
                            ps[:, b, j * P:j * P + P], pS[:, h % 2, j * P:j * P + P], ident[:, :]))
                    free["p0" if h % 2 == 0 else "p1"] = [k]
                    at["pt", h] = a = q.op("act", [k] + free["pt"], lambda e: e.activation(
                        pT[:, :], ps[:, b, 0:384], ACT.Copy))
                    give(b, [a])

                def values(h):
                    b = take("aux")
                    vs = slice(h * 64, h * 64 + 64)
                    for n, (t, kt, j) in enumerate(((0, 0, 0), (1, 0, 1), (1, 1, 2))):
                        k = q.op("pe", [at["pt", h], tok["vt", 0], tok["vt", 1]] + (bank_free[b] if n == 0 else []),
                                 lambda e: e.matmul(ps[:, b, t * 64:t * 64 + 64], pT[:, j * P:j * P + P],
                                                    VT[:, kt, vs], start=kt == 0, stop=kt == t))
                    free["pt"] = [k]
                    ri = at["p", h][2]
                    for t in (0, 1):
                        d = q.op("dve", [k, at["ri", h]] + tok["u_free"], lambda e: e.tensor_scalar(
                            U[:, t, vs], ps[:, b, t * 64:t * 64 + 64], ri[:, t:t + 1], None, ALU.mult))
                        tok["yb", "src", t] = d
                    give(b, [d])

                yield from pipeline(8, turn_in, scores, turn_p, values)
                yield
                yield from turned(U, [[tok["yb", "src", 0]], [tok["yb", "src", 1]]], YH, YL, "yb")

            at_task = attention()
            tasks.append(at_task)

            merged_tok = {}
            gates_free = [[tok["v", 0], tok["v", 1]]]
            bg_free = [after]
            merged_t = {}

            def merge(n, j, banks, k, tiles=(0, 1)):
                h = slice(j * 512, j * 512 + 512)
                for t in tiles:
                    b, g, m = banks[t], gates[:, t, h], hn[:, t, h]
                    if n == 0:
                        d = q.op("dve", [k[t], tok["gate", t, j]] + hn_free[0] + hn_free[1],
                                 lambda e: e.tensor_tensor(m, ps[:, b, :], g, ALU.mult))
                        give(b, [d])
                        merged_tok[t, j] = d
                    else:
                        d = q.op("dve", [k[t], tok["gate", t, j]], lambda e: e.tensor_tensor(
                            g, ps[:, b, :], g, ALU.mult))
                        give(b, [d])
                        merged_tok[t, j] = q.op("dve", [d, merged_tok[t, j]], lambda e: e.tensor_tensor(
                            m, m, g, ALU.add))
                    gates_free[0] = gates_free[0] + [merged_tok[t, j]]

            def merged_turn(t, j):
                tile_turned(hn[:, t, :], t, j, [merged_tok[t, j]], XH, XL, merged_t, xt_free[0], None, None)
                if j == 1:
                    hn_free[t] = [("s_pe", q.count["s_pe"])]

            def merged_hook(banks):
                def hook(t, m, toks):
                    if (t, m) == (0, 1):
                        merged_turn(0, 0)
                    elif (t, m) == (1, 0):
                        merge(2, 1, banks, toks, (0,))
                        merged_turn(1, 0)
                return hook

            def merged_last():
                merged_turn(0, 1)
                yield
                merged_turn(1, 1)

            for n, br in enumerate("acb"):
                bg = q.dma("s_bg", bg_free[0], bgate[:, :], A["b_gate"]["acb".index(br):"acb".index(br) + 1, :]
                           .to_broadcast([P, D]))
                free, gates_free[0] = gates_free[0], []
                for j in (0, 1):
                    banks, k = group(f"g{br}{j}", 8, 512, XH, XL, xr)
                    for t in (0, 1):
                        b = banks[t]
                        g = gates[:, t, j * 512:j * 512 + 512]
                        d = q.op("dve", [k[t], bg] + free, lambda e: e.tensor_tensor(
                            g, ps[:, b, :], bgate[:, j * 512:j * 512 + 512], ALU.add))
                        give(b, [d])
                        tok["gate", t, j] = q.op("act", [d], lambda e: e.activation(g, g, ACT.Sigmoid))
                bg_free[0] = [d]
                if br == "b":
                    xt_free[0] = [k[1]]
                where = 4 if br == "c" else 0

                def yready(kc):
                    while ("y" + br, kc) not in tok:
                        step_tasks()
                    return tok["y" + br, kc]

                if n == 0:
                    while mem_task in tasks:
                        step_tasks()
                for j in (0, 1):
                    end = j and n == 2
                    banks, k = group(f"br{br}{j}", 4, 512, YH[:, where:where + 4, :], YL[:, where:where + 4, :],
                                     yready, head=2 if end else 1, last_hook=merged_hook if end else None)
                    merge(n, j, banks, k, (1,) if end else (0, 1))
                    if n == 2 and j == 0:
                        drain()
                yfree[where] = [k[1]]
            tasks.append(merged_last())
            next(tasks[-1])

            def mready(kc):
                while kc not in merged_t:
                    assert tasks
                    step_tasks()
                return merged_t[kc]

            f2_gained = []

            def start_f2():
                drain()
                f2_gained.append(gained(C["ffn2"], YH, YL, yt_tok, yfree[0] + yfree[4]))

            def x_turn(t):
                tile_turned(X[:, t, :], t, 1, [x_tok[t, 1]], YH, YL, yt_tok, yfree[0] + yfree[4], C["ffn2"], None)

            def x_last():
                yield
                x_turn(1)

            def wo_tail(t, m):
                if (t, m) in ((1, 0), (1, 1)):
                    next(f2_gained[0])
                elif m == 2 and t:
                    x_turn(0)
                elif m == 3:
                    begin(x_last(), True)

            yt_tok.clear()
            late_product("wo", XH, XL, mready, "plain", start_f2, wo_tail)
            xt_free[0] = [("s_pe", q.count["s_pe"])]
            ffn_free[0] = [("s_" + e, q.count["s_" + e]) for e in ("pe", "act", "dve", "pool")]

            norm = Norm(mod["a1"], mod["b1"], XH, XL, xt_tok, xt_free[0], ready=("a1", "b1"))
            up_done, last = ffn("f2", "half", YH, YL, yt_tok, True, norm.tail)
            yfree[0] = yfree[4] = up_done

            after = [("s_" + e, q.count["s_" + e]) for e in ("pe", "act", "dve", "pool")]
            xr = lambda kc: xt_tok[kc]
            ct_free = {0: after, 1: after}
            gc_free, uu_free, gb_free = [after], [after], [after]
            tk = {}

            def turn_pair(src, toks, j):
                b = take("aux")
                for t in (0, 1):
                    for c2 in (0, 1):
                        k = q.op("pe", toks[t] + (bank_free[b] if c2 + t == 0 else []), lambda e: e.transpose(
                            ps[:, b, c2 * 256 + t * P:c2 * 256 + t * P + P],
                            src[:, t, (2 * j + c2) * P:(2 * j + c2) * P + P], ident[:, :]))
                return b, k

            def convolve(i, ut):
                yield
                for j in (0, 1):
                    b1, k = turn_pair(UU, ut, j)
                    ta = q.op("act", [k] + ct_free[j], lambda e: e.activation(uT[:, j, :], ps[:, b1, :], ACT.Copy))
                    give(b1, [ta])
                    yield
                    ds = []
                    for c2 in (0, 1):
                        ch = 4 * i + 2 * j + c2
                        u3 = uT[:, j, c2 * 256:c2 * 256 + 256].rearrange("p (r n) -> p r n", r=4)
                        c3 = cT[:, j, c2 * 256:c2 * 256 + 256].rearrange("p (r n) -> p r n", r=4)
                        w = [C["cw"][:, n * 8 + ch:n * 8 + ch + 1] for n in range(3)]
                        d = q.op("dve", [ta] + ct_free[j], lambda e: e.tensor_scalar(c3, u3, w[1], None, ALU.mult))
                        d = q.op("dve", [d], lambda e: e.scalar_tensor_tensor(
                            out=c3[:, :, 1:64], in0=u3[:, :, 0:63], scalar=w[0], in1=c3[:, :, 1:64],
                            op0=ALU.mult, op1=ALU.add))
                        d = q.op("dve", [d], lambda e: e.scalar_tensor_tensor(
                            out=c3[:, :, 0:63], in0=u3[:, :, 1:64], scalar=w[2], in1=c3[:, :, 0:63],
                            op0=ALU.mult, op1=ALU.add))
                        ds.append(d)
                    tk["conv", i, j] = ds
                    yield
                uu_free[0] = [("s_pe", q.count["s_pe"])]

            def gate(i, gt):
                for j in (0, 1):
                    b2, k = turn_pair(GB, gt, j)
                    d = q.op("dve", [k] + tk["conv", i, j], lambda e: e.tensor_tensor(
                        cT[:, j, :], ps[:, b2, :], cT[:, j, :], ALU.mult))
                    give(b2, [d])
                    ch = 4 * i + 2 * j
                    ab = split_from(cT[:, j, :].rearrange("p (c n) -> p c n", c=2), YH[:, ch:ch + 2, :],
                                    YL[:, ch:ch + 2, :], [d], yfree[0] + yfree[4])
                    ct_free[j] = ab
                    tk["y", ch] = tk["y", ch + 1] = ab
                    yield
                gb_free[0] = [("s_pe", q.count["s_pe"])]

            for i in (0, 1):
                banks, k = group(f"conv_cc{i}", 8, 512, XH, XL, xr, head=1 if i else 4,
                                 head_hook=None if i else norm.head)
                gcs = []
                for t in (0, 1):
                    b = banks[t]
                    a = q.op("act", [k[t]] + gc_free[0], lambda e: e.activation(GC[:, t, :], ps[:, b, :], ACT.Copy))
                    give(b, [a])
                    gcs.append(a)
                banks, k = group(f"conv_hv{i}", 8, 512, XH, XL, xr)
                drain()
                ut, gt = [], []
                for t in (0, 1):
                    b = banks[t]
                    d = q.op("dve", [k[t], gcs[t]] + uu_free[0], lambda e: e.tensor_tensor(
                        UU[:, t, :], GC[:, t, :], ps[:, b, :], ALU.mult))
                    give(b, [d])
                    ut.append([d])
                gc_free[0] = ut[0] + ut[1]
                c_task = convolve(i, ut)
                tasks.append(c_task)
                banks, k = group(f"conv_gb{i}", 8, 512, XH, XL, xr)
                for t in (0, 1):
                    b = banks[t]
                    a = q.op("act", [k[t]] + gb_free[0], lambda e: e.activation(GB[:, t, :], ps[:, b, :], ACT.Copy))
                    give(b, [a])
                    gt.append([a])
                finish(c_task)
                g_task = gate(i, gt)
                tasks.append(g_task)
            xt_free[0] = [k[1]]

            def vready(kc):
                while ("y", kc) not in tk:
                    step_tasks()
                return tk["y", kc]

            norm = Norm(mod["a2"], mod["b2"], XH, XL, xt_tok, xt_free[0], ready=("a2", "b2"))
            late_product("co", YH, YL, vready, 0, drain, norm.tail)
            ffn_free[0] = [("s_" + e, q.count["s_" + e]) for e in ("pe", "act", "dve", "pool")]

            f_in = q.dma("s_fin", ffn_free[0], FG[:, :], A["final_g"][0:1, :].to_broadcast([P, D]))
            done = []

            g_tok = {}

            def with_gain(t, j):
                h = slice(j * 512, j * 512 + 512)
                g_tok[t, j] = q.op("dve", [x_tok[t, j], f_in] + ada["free"][t], lambda e: e.tensor_tensor(
                    acc2[:, t, h], X[:, t, h], FG[:, h], ALU.mult))

            def final(t):
                h0, h1 = slice(0, 512), slice(512, 1024)
                k = q.op("dve", [R_tok[t], g_tok[t, 0]], lambda e: e.tensor_scalar(
                    acc2[:, t, h0], acc2[:, t, h0], R[t], None, ALU.mult))
                done.append(q.dma("s_out", [k], out[t][:, h0], acc2[:, t, h0]))
                k = q.op("act", [R_tok[t], g_tok[t, 1]], lambda e: e.activation(
                    acc2[:, t, h1], acc2[:, t, h1], ACT.Copy, scale=R[t]))
                done.append(q.dma("s_out", [k], out[t][:, h1], acc2[:, t, h1]))

            def f3_tail(t, m):
                if (t, m) == (1, 0):
                    for j in (0, 1):
                        with_gain(0, j)
                    final(0)
                    with_gain(1, 0)
                elif (t, m) == (1, 3):
                    with_gain(1, 1)
                elif (t, m) == (1, 4):
                    final(1)

            ffn("f3", 1, XH, XL, xt_tok, False, f3_tail, norm.head)
            q.wait("sp", done[-1:])

        block = ctx.enter_context(nc.Block())

        @block.sync
        def _(eng):
            schedule(Queues(sems, "sp", eng))

        @block.scalar
        def _(eng):
            schedule(Queues(sems, "act", eng))

        @block.vector
        def _(eng):
            schedule(Queues(sems, "dve", eng))

        @block.gpsimd
        def _(eng):
            schedule(Queues(sems, "pool", eng))

        @block.tensor
        def _(eng):
            schedule(Queues(sems, "pe", eng))


COLS = (("c", 8), ("ffn1", 8), ("mix", 8), ("ffn2", 8), ("mem_norm", 8), ("norm1", 8), ("norm2", 8),
        ("cqn", 3), ("ckvn", 2), ("mqn", 1), ("mkn", 1), ("sgb", 8), ("cw", 24),
        ("ab_sh1", 8), ("ab_sc1", 8), ("ab_sh2", 8), ("ab_sc2", 8))


def layout(i):
    f = lambda a: np.asarray(a)

    a = {}

    def add(name, w):
        k = f(w).reshape(-1, P, w.shape[-1])
        n, c = k.shape[0], w.shape[-1]
        if n % 2:
            k = np.concatenate([k, np.zeros((1, P, c), k.dtype)], 0)
        a[name] = k.reshape(-1, 2, P, c).transpose(0, 2, 1, 3).reshape(-1, P, 2 * c)

    def halves(name, w):
        c = w.shape[1] // 2
        for j in (0, 1):
            add(f"{name}{j}", w[:, c * j:c * j + c])

    def cc(v):
        return f(v).reshape(-1, P).T

    def ffn(tag, w, down):
        g, u = w[:, :FF].reshape(D, 11, 256), w[:, FF:].reshape(D, 11, 256)
        for j in range(11):
            add(f"{tag}_up{j}", np.concatenate([g[:, j], u[:, j]], 1))
        halves(f"{tag}_dn", down)

    a["x"] = f(i["x"])[0].reshape(2, P, D)
    a["mem"] = f(i["mem"])[0].reshape(2, P, D)
    ffn("f1", f(i["ffn1_w_gu"])[0], f(i["ffn1_w_down"])[0])
    ffn("f2", f(i["ffn2_w_gu"])[0], f(i["ffn2_w_down"])[0])
    ffn("f3", f(i["ffn_w_in_2"])[0], f(i["ffn_w_out_2"])[0])
    halves("mkv", f(i["mem_w_kv"])[0])
    w = f(i["w_in"])[0]
    for nm, lo, hi in (("u", 0, 512), ("v", 512, 1024), ("cq", 1024, 1408), ("ckv", 1408, 1696), ("qm", 1696, 2208)):
        add(nm, w[:, lo:hi])
    for n, nm in enumerate("abc"):
        o = 2208 + n * D
        halves("g" + nm, w[:, o:o + D])
        halves("br" + nm, f(i["w_branch_" + nm])[0])
    halves("uq", f(i["mla_w_uq"])[0])
    halves("ukv", f(i["mla_w_ukv"])[0])
    halves("wo", f(i["w_out"])[0])
    ci = f(i["conv_w_in_2"])[0]
    for nm, o in (("gb", 0), ("cc", D), ("hv", 2 * D)):
        halves("conv_" + nm, ci[:, o:o + D])
    halves("co", f(i["conv_w_out_2"])[0])
    aw = f(i["ada_w_2"])[0]
    a["ada"] = np.ascontiguousarray(aw.reshape(8, P, 6, D).transpose(2, 0, 1, 3).reshape(48, P, D))
    ab = f(i["ada_b_2"])[0].reshape(6, D)
    parts = {
        "c": cc(i["c_2"]), "ffn1": cc(i["ffn1_norm"]), "mix": cc(i["mix_norm"]), "ffn2": cc(i["ffn2_norm"]),
        "mem_norm": cc(i["mem_norm"]), "norm1": cc(i["norm1_g_2"]), "norm2": cc(i["norm2_g_2"]),
        "cqn": cc(i["mla_cq_norm"]), "ckvn": cc(i["mla_ckv_norm"]), "mqn": cc(i["mem_q_norm"]),
        "mkn": cc(i["mem_k_norm"]), "sgb": f(i["sg_b"])[0].T,
        "cw": np.concatenate([cc(f(i["conv_w_2"])[0, n]) for n in range(3)], 1),
        "ab_sh1": cc(ab[0]), "ab_sc1": cc(ab[1]), "ab_sh2": cc(ab[3]), "ab_sc2": cc(ab[4]),
    }
    a["cols"] = np.concatenate([parts[k] for k, _ in COLS], 1)
    a["adab_g"] = ab[[2, 5]]
    a["mla_q_norm"], a["mla_k_norm"] = f(i["mla_q_norm"]), f(i["mla_k_norm"])
    a["positions"] = f(i["positions"])[0].reshape(2, P).T
    a["inv"] = (10000.0 ** (-np.arange(16, dtype=np.float64) / 16)).astype(np.float32)[None]
    a["sg_ln_g"], a["sg_ln_b"] = f(i["sg_ln_g"]), f(i["sg_ln_b"])
    a["sg_wT"] = f(i["sg_w"])[0].transpose(2, 0, 1)
    a["b_gate"] = f(i["b_gate"])[0].reshape(3, D)[[0, 2, 1]]
    a["final_g"] = f(i["final_g_2"])[None]
    return {k: np.ascontiguousarray(v) for k, v in a.items()}


def kernel(**inputs):
    import concourse.bacc as _bacc
    from concourse.bass_utils import run_bass_kernel_spmd as _run

    nc = _bacc.Bacc("TRN2", target_bir_lowering=False, num_devices=1)
    arrays, args = {}, {}
    for name, a in layout(inputs).items():
        arrays[f"in_{name}"] = a
        args[name] = nc.dram_tensor(f"in_{name}", a.shape, mybir.dt.from_np(a.dtype), kind="ExternalInput").ap()
    out = nc.dram_tensor("out_0", (2, P, D), F32, kind="ExternalOutput").ap()
    build(nc, args, out)
    r = _run(nc, [arrays], core_ids=[0])
    return r.results[0]["out_0"].reshape(1, 2 * P, D)
```
